# Optimizing a Trainium2 kernel written in Bass

```python
import jax, jax.numpy as jnp
from jax import lax
import numpy as np
import jax
import jax.numpy as jnp

D_MODEL = 1024
BATCH = 1
SEQ = 256
DEPTH = 2

MIX_WIDTH = D_MODEL
N_MIXERS = 4
GROUP_WIDTH = MIX_WIDTH // N_MIXERS
N_GROUP_HEADS = 4
HEAD_DIM = GROUP_WIDTH // N_GROUP_HEADS
SHORT_CONV_WIDTH = 3
CHUNK = 128
IDX_HEADS = 4
IDX_DIM = 64
TOPK_MAX = 256
CONF_CONV_WIDTH = 31
Q_BLOCK = 128
ROPE_THETA = 10000.0
FFN_HIDDEN = -(-8 * D_MODEL // (3 * 256)) * 256
NORM_EPS = 1e-6
LN_EPS = 1e-5
NEG = -1e30
SPLIT_SIZES = (GROUP_WIDTH, GROUP_WIDTH, GROUP_WIDTH,
               GROUP_WIDTH, GROUP_WIDTH,
               GROUP_WIDTH, GROUP_WIDTH, GROUP_WIDTH,
               IDX_HEADS * IDX_DIM, IDX_DIM, IDX_HEADS,
               GROUP_WIDTH, GROUP_WIDTH)
IN_COLS = sum(SPLIT_SIZES)


def rmsnorm(x, g):
    xf = x.astype(jnp.float32)
    y = xf * lax.rsqrt(jnp.mean(xf * xf, axis=-1, keepdims=True) + NORM_EPS)
    return (y * g.astype(jnp.float32)).astype(x.dtype)

def layernorm(x, g, b):
    xf = x.astype(jnp.float32)
    mu = jnp.mean(xf, axis=-1, keepdims=True)
    var = jnp.mean(jnp.square(xf - mu), axis=-1, keepdims=True)
    y = (xf - mu) * lax.rsqrt(var + LN_EPS)
    return (y * g.astype(jnp.float32) + b.astype(jnp.float32)).astype(x.dtype)

def causal_dwconv(x, w):
    width, chans = w.shape
    return lax.conv_general_dilated(
        x, w[:, None, :].astype(x.dtype), window_strides=(1,),
        padding=[(width - 1, 0)], dimension_numbers=('NWC', 'WIO', 'NWC'),
        feature_group_count=chans)

def rope_tables(seq, dim):
    inv_freq = ROPE_THETA ** (-jnp.arange(0, dim, 2, dtype=jnp.float32) / dim)
    ang = jnp.arange(seq, dtype=jnp.float32)[:, None] * inv_freq[None, :]
    return jnp.cos(ang), jnp.sin(ang)

def apply_rope(x, cos, sin):
    half = x.shape[-1] // 2
    c = cos[None, :, None, :].astype(x.dtype)
    s = sin[None, :, None, :].astype(x.dtype)
    x1, x2 = x[..., :half], x[..., half:]
    return jnp.concatenate([x1 * c - x2 * s, x2 * c + x1 * s], axis=-1)

def short_conv_mixer(b, c, h, w_conv):
    return b * causal_dwconv(c * h, w_conv)

def gmlp_mixer(u, v, ln_g, ln_b, w_s, b_s):
    bsz, seq, _ = v.shape
    vn = layernorm(v, ln_g, ln_b)
    vc = vn.reshape(bsz, seq // CHUNK, CHUNK, N_GROUP_HEADS, HEAD_DIM)
    mask = jnp.tril(jnp.ones((CHUNK, CHUNK), dtype=bool))
    ws = jnp.where(mask[None], w_s, 0).astype(v.dtype)
    mixed = jnp.einsum('hts,bnshd->bnthd', ws, vc)
    mixed = mixed + b_s.T[None, None, :, :, None].astype(v.dtype)
    return u * mixed.reshape(bsz, seq, GROUP_WIDTH)

def dsa_mixer(q, k, v, q_idx, k_idx, w_idx):
    bsz, seq, _ = q.shape
    topk = min(TOPK_MAX, seq // 4)
    cos_a, sin_a = rope_tables(seq, HEAD_DIM)
    cos_i, sin_i = rope_tables(seq, IDX_DIM)
    q = apply_rope(q.reshape(bsz, seq, N_GROUP_HEADS, HEAD_DIM), cos_a, sin_a)
    k = apply_rope(k.reshape(bsz, seq, N_GROUP_HEADS, HEAD_DIM), cos_a, sin_a)
    v = v.reshape(bsz, seq, N_GROUP_HEADS, HEAD_DIM)
    qi = apply_rope(q_idx.reshape(bsz, seq, IDX_HEADS, IDX_DIM), cos_i, sin_i).astype(jnp.float32)
    ki = apply_rope(k_idx[:, :, None, :], cos_i, sin_i)[:, :, 0, :].astype(jnp.float32)
    wi = w_idx.astype(jnp.float32) * (IDX_HEADS ** -0.5) * (IDX_DIM ** -0.5)
    scale = HEAD_DIM ** -0.5
    nblk = seq // Q_BLOCK

    def to_blocks(t):
        return jnp.swapaxes(t.reshape((bsz, nblk, Q_BLOCK) + t.shape[2:]), 0, 1)

    kpos = jnp.arange(seq)
    tpos = kpos.reshape(nblk, Q_BLOCK)

    def block(args):
        qb, qib, wib, tb = args
        rel = jax.nn.relu(jnp.einsum('bqjd,bsd->bqjs', qib, ki))
        score = jnp.einsum('bqjs,bqj->bqs', rel, wib)
        admissible = kpos[None, :] <= tb[:, None]
        score = jnp.where(admissible[None], score, NEG)
        _, idx = lax.top_k(score, topk)
        valid = idx <= tb[None, :, None]
        kg = jax.vmap(lambda kk, ii: kk[ii])(k, idx)
        vg = jax.vmap(lambda vv, ii: vv[ii])(v, idx)
        logits = jnp.einsum('bqhd,bqkhd->bqhk', qb, kg).astype(jnp.float32) * scale
        logits = jnp.where(valid[:, :, None, :], logits, NEG)
        p = jax.nn.softmax(logits, axis=-1).astype(v.dtype)
        return jnp.einsum('bqhk,bqkhd->bqhd', p, vg)

    out = lax.map(block, (to_blocks(q), to_blocks(qi), to_blocks(wi), tpos))
    return jnp.swapaxes(out, 0, 1).reshape(bsz, seq, GROUP_WIDTH)

def conformer_conv_mixer(a, gate, w_dw, b_dw, ln_g, ln_b):
    y = a * jax.nn.sigmoid(gate)
    y = causal_dwconv(y, w_dw) + b_dw.astype(y.dtype)
    y = layernorm(y, ln_g, ln_b)
    return jax.nn.silu(y)

def hybrid_layer(x, g_mix, w_in, w_conv_a, gmlp_ln_g, gmlp_ln_b, w_s, b_s,
                 w_conf, b_conf, conf_ln_g, conf_ln_b, w_out,
                 g_ffn, w_gate, w_up, w_down):
    h = rmsnorm(x, g_mix)
    z = h @ w_in
    cuts, acc = [], 0
    for sz in SPLIT_SIZES[:-1]:
        acc += sz
        cuts.append(acc)
    (a_b, a_c, a_h, g_u, g_v, q, k, v, q_idx, k_idx, w_idx, d_a, d_g) = jnp.split(z, cuts, axis=-1)
    y_a = short_conv_mixer(a_b, a_c, a_h, w_conv_a)
    y_b = gmlp_mixer(g_u, g_v, gmlp_ln_g, gmlp_ln_b, w_s, b_s)
    y_c = dsa_mixer(q, k, v, q_idx, k_idx, w_idx)
    y_d = conformer_conv_mixer(d_a, d_g, w_conf, b_conf, conf_ln_g, conf_ln_b)
    x = x + jnp.concatenate([y_a, y_b, y_c, y_d], axis=-1) @ w_out
    hf = rmsnorm(x, g_ffn)
    return x + (jax.nn.silu(hf @ w_gate) * (hf @ w_up)) @ w_down

def first_inputs(seed: int = 0) -> dict:
    key = jax.random.key(seed)
    ks = jax.random.split(key, 20)
    f32 = jnp.float32
    G, H = GROUP_WIDTH, N_GROUP_HEADS

    def nrm(k, shape, scale):
        return jax.random.normal(k, shape, f32) * scale

    def gain(k, shape):
        return 1.0 + 0.05 * jax.random.normal(k, shape, f32)

    return {
        "x": jax.random.normal(ks[0], (BATCH, SEQ, D_MODEL), f32),
        "g_mix": gain(ks[1], (DEPTH, D_MODEL)),
        "w_in": nrm(ks[2], (DEPTH, D_MODEL, IN_COLS), D_MODEL ** -0.5),
        "w_conv_a": nrm(ks[3], (DEPTH, SHORT_CONV_WIDTH, G), SHORT_CONV_WIDTH ** -0.5),
        "gmlp_ln_g": gain(ks[4], (DEPTH, G)),
        "gmlp_ln_b": nrm(ks[5], (DEPTH, G), 0.02),
        "w_s": nrm(ks[6], (DEPTH, H, CHUNK, CHUNK), 0.5 * CHUNK ** -0.5),
        "b_s": 1.0 + nrm(ks[7], (DEPTH, H, CHUNK), 0.1),
        "w_conf": nrm(ks[8], (DEPTH, CONF_CONV_WIDTH, G), CONF_CONV_WIDTH ** -0.5),
        "b_conf": nrm(ks[9], (DEPTH, G), 0.02),
        "conf_ln_g": gain(ks[10], (DEPTH, G)),
        "conf_ln_b": nrm(ks[11], (DEPTH, G), 0.02),
        "w_out": nrm(ks[12], (DEPTH, MIX_WIDTH, D_MODEL), 0.5 * MIX_WIDTH ** -0.5),
        "g_ffn": gain(ks[13], (DEPTH, D_MODEL)),
        "w_gate": nrm(ks[14], (DEPTH, D_MODEL, FFN_HIDDEN), D_MODEL ** -0.5),
        "w_up": nrm(ks[15], (DEPTH, D_MODEL, FFN_HIDDEN), D_MODEL ** -0.5),
        "w_down": nrm(ks[16], (DEPTH, FFN_HIDDEN, D_MODEL), 0.5 * FFN_HIDDEN ** -0.5),
        "g_final": gain(ks[17], (D_MODEL,)),
    }

def first_block(x, g_mix, w_in, w_conv_a, gmlp_ln_g, gmlp_ln_b, w_s, b_s,
              w_conf, b_conf, conf_ln_g, conf_ln_b, w_out,
              g_ffn, w_gate, w_up, w_down, g_final):
    for l in range(DEPTH):
        x = hybrid_layer(x, g_mix[l], w_in[l], w_conv_a[l], gmlp_ln_g[l], gmlp_ln_b[l],
                         w_s[l], b_s[l], w_conf[l], b_conf[l], conf_ln_g[l], conf_ln_b[l],
                         w_out[l], g_ffn[l], w_gate[l], w_up[l], w_down[l])
    return rmsnorm(x, g_final)


DEPTH_2 = 1

GRID_W = 64
CTX_LEN = 256
D_MIX = D_MODEL
D_MLSTM = D_MIX // 2
MLSTM_HEADS = 4
MLSTM_DH = D_MLSTM // MLSTM_HEADS
QKV_BLOCK = 4
N_QKV_BLOCKS = D_MLSTM // QKV_BLOCK
CONV_K = 3
D_FOURIER = D_MIX - D_MLSTM
FOURIER_GROUPS = 4
FOURIER_CG = D_FOURIER // FOURIER_GROUPS
D_IN_PROJ = 2 * D_MLSTM + D_FOURIER
N_EXPERT_GROUPS = 4
EXPERTS_PER_GROUP = 4
N_EXPERTS = N_EXPERT_GROUPS * EXPERTS_PER_GROUP
TOP_K = 2
D_EXPERT = D_MODEL // 2
N_MOD = 6
EPS = 1e-6
POS_BASE = 10000.0
F32 = jnp.float32


def rmsnorm_2(x, g):
    x32 = x.astype(F32)
    y = x32 * lax.rsqrt(jnp.mean(x32 * x32, axis=-1, keepdims=True) + EPS)
    return (y * g.astype(F32)).astype(x.dtype)

def modulate(h, shift, scale):
    return h * (1 + scale) + shift

def sincos_2d(rows, cols):
    quarter = D_MODEL // 4
    freq = 1.0 / (POS_BASE ** (jnp.arange(quarter, dtype=F32) / quarter))
    r = jnp.arange(rows, dtype=F32)[:, None] * freq
    cl = jnp.arange(cols, dtype=F32)[:, None] * freq
    er = jnp.concatenate([jnp.sin(r), jnp.cos(r)], axis=-1)
    ec = jnp.concatenate([jnp.sin(cl), jnp.cos(cl)], axis=-1)
    half = D_MODEL // 2
    emb = jnp.concatenate([jnp.broadcast_to(er[:, None, :], (rows, cols, half)),
                           jnp.broadcast_to(ec[None, :, :], (rows, cols, half))], axis=-1)
    return emb.reshape(rows * cols, D_MODEL)

def short_conv(x, w, b):
    y = lax.conv_general_dilated(x, w[:, None, :], window_strides=(1,), padding='SAME',
                                 dimension_numbers=('NWC', 'WIO', 'NWC'),
                                 feature_group_count=x.shape[-1])
    return y + b

def headwise(x, w):
    y = jnp.einsum('btni,nio->btno', x.reshape(x.shape[:-1] + (N_QKV_BLOCKS, QKV_BLOCK)), w)
    return y.reshape(x.shape)

def to_heads(t):
    B, T, _ = t.shape
    return t.astype(F32).reshape(B, T, MLSTM_HEADS, MLSTM_DH).transpose(0, 2, 1, 3)

def flip_seq(t):
    return jnp.flip(t, axis=2)

def mixer_features(h, lp):
    proj = h @ lp['w_in']
    x_m = proj[..., :D_MLSTM]
    z = proj[..., D_MLSTM:2 * D_MLSTM]
    u = proj[..., 2 * D_MLSTM:]
    act = jax.nn.silu(short_conv(x_m, lp['conv_w'], lp['conv_b']))
    q = headwise(act, lp['w_q'])
    k = headwise(act, lp['w_k'])
    v = headwise(x_m, lp['w_v'])
    qkv = jnp.concatenate([q, k, v], axis=-1)

    def gates(w, b):
        g = (qkv @ w + b).astype(F32).transpose(0, 2, 1)
        return g[:, :MLSTM_HEADS], jax.nn.log_sigmoid(g[:, MLSTM_HEADS:])

    heads = (to_heads(q) * (MLSTM_DH ** -0.5), to_heads(k), to_heads(v))
    return heads, gates(lp['w_if_fwd'], lp['b_if_fwd']), gates(lp['w_if_bwd'], lp['b_if_bwd']), act, z, u

def mlstm_scan(k, v, ig, lf, state):
    B, H, T, DH = k.shape
    nc = T // CHUNK
    kc = k.reshape(B, H, nc, CHUNK, DH)
    vc = v.reshape(B, H, nc, CHUNK, DH)
    b = jnp.cumsum(lf.reshape(B, H, nc, CHUNK), axis=-1)
    btot = b[..., -1]
    a = btot[..., None] - b + ig.reshape(B, H, nc, CHUNK)
    amax = jnp.max(a, axis=-1)

    def step(carry, xs):
        C, n, m = carry
        k_, v_, a_, amax_, bt_ = xs
        m_new = jnp.maximum(bt_ + m, amax_)
        decay = jnp.exp(bt_ + m - m_new)
        kw = k_ * jnp.exp(a_ - m_new[..., None])[..., None]
        C_new = decay[..., None, None] * C + jnp.einsum('bhlk,bhlv->bhkv', kw, v_)
        n_new = decay[..., None] * n + jnp.sum(kw, axis=2)
        return (C_new, n_new, m_new), (C, n, m)

    xs = tuple(jnp.moveaxis(t, 2, 0) for t in (kc, vc, a, amax, btot))
    final, starts = lax.scan(step, state, xs)
    starts = tuple(jnp.moveaxis(s, 0, 2) for s in starts)
    return starts, final

def mlstm_out(q, k, v, ig, lf, starts):
    C0, n0, m0 = starts
    B, H, T, DH = q.shape
    nc = T // CHUNK
    qc = q.reshape(B, H, nc, CHUNK, DH)
    kc = k.reshape(B, H, nc, CHUNK, DH)
    vc = v.reshape(B, H, nc, CHUNK, DH)
    igc = ig.reshape(B, H, nc, CHUNK)
    b = jnp.cumsum(lf.reshape(B, H, nc, CHUNK), axis=-1)
    tri = jnp.tril(jnp.ones((CHUNK, CHUNK), dtype=bool))
    logd = jnp.where(tri, b[..., :, None] - b[..., None, :] + igc[..., None, :], -jnp.inf)
    m_inter = b + m0[..., None]
    m_t = jnp.maximum(m_inter, jnp.max(logd, axis=-1))
    w_inter = jnp.exp(m_inter - m_t)
    s = jnp.einsum('bhctd,bhcsd->bhcts', qc, kc) * jnp.exp(logd - m_t[..., None])
    num = jnp.einsum('bhcts,bhcsd->bhctd', s, vc) + w_inter[..., None] * jnp.einsum('bhctk,bhckv->bhctv', qc, C0)
    nq = jnp.sum(s, axis=-1) + w_inter * jnp.einsum('bhctk,bhck->bhct', qc, n0)
    h = num / jnp.maximum(jnp.abs(nq), jnp.exp(-m_t))[..., None]
    return h.reshape(B, H, T, DH)

def mlstm_direction(ctx_in, lat_in, with_ctx):
    qc, kc, vc, igc, lfc = ctx_in
    ql, kl, vl, igl, lfl = lat_in
    B = kl.shape[0]
    zero = (jnp.zeros((B, MLSTM_HEADS, MLSTM_DH, MLSTM_DH), F32),
            jnp.zeros((B, MLSTM_HEADS, MLSTM_DH), F32),
            jnp.zeros((B, MLSTM_HEADS), F32))
    ctx_starts, ctx_final = mlstm_scan(kc, vc, igc, lfc, zero)
    lat_starts, _ = mlstm_scan(kl, vl, igl, lfl, ctx_final)
    h_lat = mlstm_out(ql, kl, vl, igl, lfl, lat_starts)
    h_ctx = mlstm_out(qc, kc, vc, igc, lfc, ctx_starts) if with_ctx else None
    return h_lat, h_ctx

def mlstm_readout(hf, hb, act, z, norm_w, skip):
    h = hf + hb
    mu = jnp.mean(h, axis=-1, keepdims=True)
    var = jnp.mean(jnp.square(h - mu), axis=-1, keepdims=True)
    hn = (h - mu) * lax.rsqrt(var + EPS)
    B, H, T, DH = hn.shape
    hn = hn.transpose(0, 2, 1, 3).reshape(B, T, D_MLSTM) * norm_w.astype(F32)
    out = (hn + skip.astype(F32) * act.astype(F32)) * jax.nn.silu(z.astype(F32))
    return out.astype(z.dtype)

def fourier_mix(u, w_fourier):
    B, T, _ = u.shape
    ug = u.astype(F32).reshape(B, T, FOURIER_GROUPS, FOURIER_CG)
    f = jnp.fft.fft2(ug, axes=(1, 3), norm='ortho').real
    y = jnp.einsum('btgc,gcd->btgd', f, w_fourier.astype(F32))
    return y.reshape(B, T, D_FOURIER).astype(u.dtype)

def token_mix(h, hc, lp, with_ctx):
    qkv_l, gf_l, gb_l, act_l, z_l, u_l = mixer_features(h, lp)
    qkv_c, gf_c, gb_c, act_c, z_c, u_c = mixer_features(hc, lp)
    hf_l, hf_c = mlstm_direction(qkv_c + gf_c, qkv_l + gf_l, with_ctx)
    hb_l, hb_c = mlstm_direction(tuple(flip_seq(t) for t in qkv_c + gb_c),
                                 tuple(flip_seq(t) for t in qkv_l + gb_l), with_ctx)

    def merge(hf, hb, act, z, u):
        m = mlstm_readout(hf, flip_seq(hb), act, z, lp['mlstm_norm_w'], lp['mlstm_skip'])
        f = fourier_mix(u, lp['w_fourier'])
        return jnp.concatenate([m, f], axis=-1) @ lp['w_out']

    y_l = merge(hf_l, hb_l, act_l, z_l, u_l)
    y_c = merge(hf_c, hb_c, act_c, z_c, u_c) if with_ctx else None
    return y_l, y_c

def hier_moe(h, lp):
    B, T, _ = h.shape
    g_logits = (h @ lp['w_router_group'] + lp['b_router_group']).astype(F32)
    p_group = jax.nn.softmax(g_logits, axis=-1)
    g_sel = jnp.argmax(g_logits, axis=-1)
    p_sel = jnp.take_along_axis(p_group, g_sel[..., None], axis=-1)
    e_logits = (h @ lp['w_router_expert'] + lp['b_router_expert']).astype(F32)
    e_logits = e_logits.reshape(B, T, N_EXPERT_GROUPS, EXPERTS_PER_GROUP)
    e_sel = jnp.take_along_axis(e_logits, g_sel[..., None, None], axis=2)[..., 0, :]
    top_v, top_i = lax.top_k(e_sel, TOP_K)
    w_top = jax.nn.softmax(top_v, axis=-1) * p_sel
    expert_id = g_sel[..., None] * EXPERTS_PER_GROUP + top_i
    combine = jnp.sum(jax.nn.one_hot(expert_id, N_EXPERTS, dtype=F32) * w_top[..., None], axis=-2)
    combine = combine.astype(h.dtype)
    y = jnp.zeros_like(h)
    for e in range(N_EXPERTS):
        a = jax.nn.silu(h @ lp['w_gate'][e]) * (h @ lp['w_up'][e])
        y = y + combine[..., e, None] * (a @ lp['w_down'][e])
    return y

def second_inputs(seed: int = 0) -> dict:
    key = jax.random.key(seed)
    ks = jax.random.split(key, 40)
    L = DEPTH_2
    H = MLSTM_HEADS

    def nrm(k, shape, s):
        return jax.random.normal(k, shape, F32) * s

    def b_if(k1, k2):
        return jnp.concatenate([nrm(k1, (L, H), 0.1),
                                jnp.linspace(3.0, 6.0, H, dtype=F32)[None, :] + nrm(k2, (L, H), 0.1)], axis=-1)

    return {
        'x': nrm(ks[0], (BATCH, SEQ, D_MODEL), 1.0),
        'c': nrm(ks[1], (BATCH, D_MODEL), 1.0),
        'ctx': nrm(ks[2], (BATCH, CTX_LEN, D_MODEL), 1.0),
        'c_ctx': nrm(ks[3], (D_MODEL,), 1.0),
        'w_ada': nrm(ks[4], (L, D_MODEL, N_MOD * D_MODEL), 0.5 * D_MODEL ** -0.5),
        'b_ada': nrm(ks[5], (L, N_MOD * D_MODEL), 0.01),
        'g_pre_mix': 1.0 + nrm(ks[6], (L, D_MODEL), 0.05),
        'g_post_mix': 1.0 + nrm(ks[7], (L, D_MODEL), 0.05),
        'g_pre_ffn': 1.0 + nrm(ks[8], (L, D_MODEL), 0.05),
        'g_post_ffn': 1.0 + nrm(ks[9], (L, D_MODEL), 0.05),
        'w_in': nrm(ks[10], (L, D_MODEL, D_IN_PROJ), D_MODEL ** -0.5),
        'conv_w': nrm(ks[11], (L, CONV_K, D_MLSTM), CONV_K ** -0.5),
        'conv_b': nrm(ks[12], (L, D_MLSTM), 0.01),
        'w_q': nrm(ks[13], (L, N_QKV_BLOCKS, QKV_BLOCK, QKV_BLOCK), QKV_BLOCK ** -0.5),
        'w_k': nrm(ks[14], (L, N_QKV_BLOCKS, QKV_BLOCK, QKV_BLOCK), QKV_BLOCK ** -0.5),
        'w_v': nrm(ks[15], (L, N_QKV_BLOCKS, QKV_BLOCK, QKV_BLOCK), QKV_BLOCK ** -0.5),
        'w_if_fwd': nrm(ks[16], (L, 3 * D_MLSTM, 2 * H), 0.02),
        'b_if_fwd': b_if(ks[17], ks[18]),
        'w_if_bwd': nrm(ks[19], (L, 3 * D_MLSTM, 2 * H), 0.02),
        'b_if_bwd': b_if(ks[20], ks[21]),
        'mlstm_norm_w': 1.0 + nrm(ks[22], (L, D_MLSTM), 0.05),
        'mlstm_skip': 1.0 + nrm(ks[23], (L, D_MLSTM), 0.05),
        'w_fourier': nrm(ks[24], (L, FOURIER_GROUPS, FOURIER_CG, FOURIER_CG), FOURIER_CG ** -0.5),
        'w_out': nrm(ks[25], (L, D_MIX, D_MODEL), D_MIX ** -0.5),
        'w_router_group': nrm(ks[26], (L, D_MODEL, N_EXPERT_GROUPS), D_MODEL ** -0.5),
        'b_router_group': nrm(ks[27], (L, N_EXPERT_GROUPS), 0.01),
        'w_router_expert': nrm(ks[28], (L, D_MODEL, N_EXPERTS), D_MODEL ** -0.5),
        'b_router_expert': nrm(ks[29], (L, N_EXPERTS), 0.01),
        'w_gate': nrm(ks[30], (L, N_EXPERTS, D_MODEL, D_EXPERT), D_MODEL ** -0.5),
        'w_up': nrm(ks[31], (L, N_EXPERTS, D_MODEL, D_EXPERT), D_MODEL ** -0.5),
        'w_down': nrm(ks[32], (L, N_EXPERTS, D_EXPERT, D_MODEL), D_EXPERT ** -0.5),
    }

def second_block(x, c, ctx, c_ctx, w_ada, b_ada, g_pre_mix, g_post_mix, g_pre_ffn, g_post_ffn,
              w_in, conv_w, conv_b, w_q, w_k, w_v, w_if_fwd, b_if_fwd, w_if_bwd, b_if_bwd,
              mlstm_norm_w, mlstm_skip, w_fourier, w_out, w_router_group, b_router_group,
              w_router_expert, b_router_expert, w_gate, w_up, w_down):
    T = x.shape[1]
    rows = T // GRID_W
    x = x + sincos_2d(rows, GRID_W).astype(x.dtype)[None]
    xc = ctx
    for l in range(DEPTH_2):
        with_ctx = l + 1 < DEPTH_2
        lp = {
            'w_in': w_in[l], 'conv_w': conv_w[l], 'conv_b': conv_b[l],
            'w_q': w_q[l], 'w_k': w_k[l], 'w_v': w_v[l],
            'w_if_fwd': w_if_fwd[l], 'b_if_fwd': b_if_fwd[l],
            'w_if_bwd': w_if_bwd[l], 'b_if_bwd': b_if_bwd[l],
            'mlstm_norm_w': mlstm_norm_w[l], 'mlstm_skip': mlstm_skip[l],
            'w_fourier': w_fourier[l], 'w_out': w_out[l],
            'w_router_group': w_router_group[l], 'b_router_group': b_router_group[l],
            'w_router_expert': w_router_expert[l], 'b_router_expert': b_router_expert[l],
            'w_gate': w_gate[l], 'w_up': w_up[l], 'w_down': w_down[l],
        }
        mod = [m[:, None, :] for m in jnp.split(jax.nn.silu(c) @ w_ada[l] + b_ada[l], N_MOD, axis=-1)]
        mod_c = [m[None, :] for m in jnp.split(jax.nn.silu(c_ctx) @ w_ada[l] + b_ada[l], N_MOD, axis=-1)]
        shift1, scale1, gate1, shift2, scale2, gate2 = mod
        h = modulate(rmsnorm_2(x, g_pre_mix[l]), shift1, scale1)
        hc = modulate(rmsnorm_2(xc, g_pre_mix[l]), mod_c[0], mod_c[1])
        y, yc = token_mix(h, hc, lp, with_ctx)
        x = x + gate1 * rmsnorm_2(y, g_post_mix[l])
        h2 = modulate(rmsnorm_2(x, g_pre_ffn[l]), shift2, scale2)
        x = x + gate2 * rmsnorm_2(hier_moe(h2, lp), g_post_ffn[l])
        if with_ctx:
            xc = xc + mod_c[2] * rmsnorm_2(yc, g_post_mix[l])
            hc2 = modulate(rmsnorm_2(xc, g_pre_ffn[l]), mod_c[3], mod_c[4])
            xc = xc + mod_c[5] * rmsnorm_2(hier_moe(hc2, lp), g_post_ffn[l])
    return x


def setup_inputs(seed=0):
    out = dict(first_inputs(seed))
    for name, value in second_inputs(seed + 1).items():
        if name != "x":
            out[name + "_2"] = value
    return out


def reference(
    x, g_mix, w_in, w_conv_a, gmlp_ln_g, gmlp_ln_b, w_s, b_s, w_conf, b_conf, conf_ln_g,
    conf_ln_b, w_out, g_ffn, w_gate, w_up, w_down, g_final, c_2, ctx_2, c_ctx_2, w_ada_2,
    b_ada_2, g_pre_mix_2, g_post_mix_2, g_pre_ffn_2, g_post_ffn_2, w_in_2, conv_w_2, conv_b_2,
    w_q_2, w_k_2, w_v_2, w_if_fwd_2, b_if_fwd_2, w_if_bwd_2, b_if_bwd_2, mlstm_norm_w_2,
    mlstm_skip_2, w_fourier_2, w_out_2, w_router_group_2, b_router_group_2, w_router_expert_2,
    b_router_expert_2, w_gate_2, w_up_2, w_down_2,
):
    x = first_block(
        x, g_mix, w_in, w_conv_a, gmlp_ln_g, gmlp_ln_b, w_s, b_s, w_conf, b_conf, conf_ln_g,
        conf_ln_b, w_out, g_ffn, w_gate, w_up, w_down, g_final,
    )
    return second_block(
        x, c_2, ctx_2, c_ctx_2, w_ada_2, b_ada_2, g_pre_mix_2, g_post_mix_2, g_pre_ffn_2,
        g_post_ffn_2, w_in_2, conv_w_2, conv_b_2, w_q_2, w_k_2, w_v_2, w_if_fwd_2, b_if_fwd_2,
        w_if_bwd_2, b_if_bwd_2, mlstm_norm_w_2, mlstm_skip_2, w_fourier_2, w_out_2,
        w_router_group_2, b_router_group_2, w_router_expert_2, b_router_expert_2, w_gate_2,
        w_up_2, w_down_2,
    )


_drawn_inputs = setup_inputs


def setup_inputs(seed=0):
    import zlib

    import numpy as np

    out = dict(_drawn_inputs(seed))
    spreads = {}
    factors = {'gmlp_ln_b': 3.81,
     'b_conf': 3.083,
     'g_post_ffn_2': 4.79,
     'mlstm_norm_w_2': 2.848,
     'b_router_group_2': 2.685,
     'b_router_expert_2': 5.661}
    for name, (base, spread) in spreads.items():
        noise = np.random.default_rng([zlib.crc32(name.encode()), seed]).standard_normal(out[name].shape)
        drawn = base * np.exp(spread * noise) if base else spread * noise
        out[name] = jnp.asarray(drawn.astype(out[name].dtype))
    for name, factor in factors.items():
        out[name] = (out[name] * factor).astype(out[name].dtype)
    return out
```

```python
from contextlib import ExitStack

import numpy as np

import concourse.bass as bass
from concourse import mybir

F32 = mybir.dt.float32
ALU = mybir.AluOpType
ACT = mybir.ActivationFunctionType
AX = mybir.AxisListType

P = 128
T = 256
NT = T // P
D = 1024
KD = D // P
DEPTH = 2
G = 256
H = 4
HD = G // H
TOPK = 64
SHORT, LONG = 3, 31
FFN = 2816
FB = 256
NFB = FFN // FB
NEG = -1e30
TAKEN = -3e38
EPS, LN_EPS = 1e-6, 1e-5

CTX = 256
S2 = CTX + T
MW = 512
MH = 4
DH = MW // MH
NMOD = 6
NE, EPG, NG = 16, 4, 4
DE = 512
GRID_W, POS_BASE, ROPE_THETA = 64, 10000.0, 10000.0

C_GMIX, C_GFFN, C_SHORT = 0, KD, 2 * KD
C_LONG = C_SHORT + 2 * SHORT
C_BCONF = C_LONG + 2 * LONG
C_LNG, C_LNB, C_BS = C_BCONF + 2, C_BCONF + 4, C_BCONF + 6
N_PRM = C_BS + H
C2_PREMIX, C2_PREFFN, C2_CONV = 0, KD, 2 * KD
C2_CONVB = C2_CONV + 3 * MH
C2_NORM, C2_SKIP, C2_C = C2_CONVB + MH, C2_CONVB + 2 * MH, C2_CONVB + 3 * MH
C2_IG, C2_FG = C2_C + 2 * KD, C2_C + 2 * KD + 1
N_PRM2 = C2_FG + 1
ROWS = 32 + MH
K_ID, K_COS, K_SIN = 0, P, P + 2 * HD
K_CC = K_SIN + 2 * HD
K_SC = K_CC + P
K_DFT = K_SC + P
K_RANK = K_DFT + NT * 2 * T
N_CONST = K_RANK + NE

IN_COLS = {"vqi": 512, "kwi": 68, "dadg": 512, "qk": 512, "guv": 512, "abac": 512, "ah": 256}
IN_AT = dict(zip(IN_COLS, np.cumsum([0] + [KD * w for w in IN_COLS.values()])[:-1].tolist()))
N_IN = KD * sum(IN_COLS.values())
BLOCK = 3 * KD * FB
EXPERT = 3 * 4096

DVE_STEPS, POOL_STEPS = 122, 11
N_SCRATCH = 13400


class Banks:

    def __init__(self):
        self.count, self.at = [0] * 8, {}

    def add(self, bank, *names, times=1):
        for name in names:
            self.at[name] = (bank, self.count[bank])
            self.count[bank] += times


def layer_banks():
    b = Banks()
    for bank, name in [
        (0, "tx1_00"), (1, "tx1_01"), (2, "tx1_10"), (3, "tx1_11"), (4, "vqi0"), (5, "vqi1"), (6, "kwi0"),
        (7, "kwi1"), (0, "da"), (1, "dg"), (2, "riT0"), (3, "riT1"), (4, "qk0"), (5, "qk1"), (2, "sc0a"),
        (0, "sc0b"), (3, "sc1a"), (6, "sc1b"), (7, "guv0"), (6, "guv1"), (0, "cvT"), (1, "ab"), (4, "ac"), (5, "ah"),
        (2, "rqT0"), (3, "rqT1"), (6, "mix0"), (7, "mix1"), (4, "lg0a"), (2, "lg0b"), (5, "lg1a"), (6, "lg1b"), (0, "ybT"),
        (7, "cnT"), (0, "wo0"), (1, "wo1"), (2, "wo2"), (3, "wo3"), (7, "pT0"), (4, "pT1a"), (5, "pT1b"),
        (6, "av0"), (7, "av1"), (4, "ycT"), (4, "tx2_00"), (5, "tx2_01"), (6, "tx2_10"), (7, "tx2_11"),
    ]:
        b.add(bank, name)
    b.add(4, "gu0", times=NFB)
    b.add(5, "gu1", times=NFB)
    for n in range(4):
        b.add(n, f"y{n}")
    return b


def second_banks():
    b = Banks()
    for s in range(4):
        b.add(s, f"ada{s}", times=3)
    b.add(4, "modT")
    for s in range(4):
        b.add(s, f"gate{s}")
    for n in range(4):
        b.add(4 + n, f"tc{n}")
    for n in range(4):
        b.add(n, f"tl{n}")
    for j in range(4):
        b.add(4 + j, f"xm{j}")
    b.add(0, "z0")
    b.add(1, "z1")
    b.add(2, "u0")
    b.add(3, "u1")
    for n in range(4):
        b.add(n, f"vt{n}")
    for n in range(12):
        b.add(4 + n % 4, f"qkv{n}")
    b.add(4, "gates")
    for g in range(4):
        b.add(g, f"fp{g}")
    b.add(6, "ff0")
    b.add(7, "ff1")
    b.add(6, "fy0")
    b.add(7, "fy1")
    b.add(5, "rT")
    for h in range(MH):
        b.add(6 + h % 2, f"rb{h}")
        b.add(2 * (h % 2), f"qk{h}a")
        b.add(2 * (h % 2) + 1, f"qk{h}b")
        b.add(4, f"o{h}0")
        b.add(5, f"o{h}1")
    b.add(6, "hT0")
    b.add(7, "hT1")
    for n in range(4):
        b.add(n, f"wo{n}")
    for n in range(4):
        b.add(4 + n, f"t2{n}")
    b.add(0, "rt0")
    b.add(1, "rt1")
    b.add(2, "cT")
    for n in range(8):
        b.add(3 + n % 2, f"cb{n}")
    b.add(4, "eg0", times=2 * NE)
    b.add(5, "eg1", times=2 * NE)
    for n in range(4):
        b.add(n, f"ye{n}")
    return b



LAY, SEC = layer_banks(), second_banks()


class Results:

    def __init__(self, filled, drained, plan, base):
        self.filled, self.drained, self.plan, self.base = filled, drained, plan, base

    def index(self, name, i):
        bank, n = self.plan.at[name]
        return bank, self.base[bank] + n + i

    def room(self, eng, name, i=0):
        bank, n = self.index(name, i)
        eng.wait_ge(self.drained[bank], n + 1)

    def done(self, ins, name):
        ins.then_inc(self.filled[self.plan.at[name][0]], 1)

    def ready(self, eng, name, i=0):
        bank, n = self.index(name, i)
        eng.wait_ge(self.filled[bank], n + 1)

    def moved(self, ins, name):
        ins.then_inc(self.drained[self.plan.at[name][0]], 1)

    def arrived(self, eng, name, i=0):
        bank, n = self.index(name, i)
        eng.wait_ge(self.drained[bank], n + 2)


def settle(eng, passed):
    eng.sem_inc(passed, 1)


class Steps:

    def __init__(self, eng, sem, base):
        self.eng, self.sem, self.base, self.n = eng, sem, base, 0

    def did(self, ins):
        self.n += 1
        ins.then_inc(self.sem, 1)
        return self.n

    def need(self, n):
        self.eng.wait_ge(self.sem, self.base + n)

    def then(self, ins):
        self.need(self.did(ins))



def build(nc, a, out):
    ctx = ExitStack()
    with ctx:
        def sb(name, shape):
            return ctx.enter_context(nc.sbuf_tensor(name, shape, F32))

        def sem(name):
            return ctx.enter_context(nc.semaphore(name))

        bank = [ctx.enter_context(nc.psum_tensor(f"bank{n}", [P, 512], F32)) for n in range(8)]

        blocks_w = sb("blocks_w", [P, 2, BLOCK])
        m = sb("m", [P, 4, 4096])
        kwi_w = sb("kwi_w", [P, KD, 68])
        const = sb("const", [P, N_CONST])
        prm = sb("prm", [P, N_PRM])
        prm2 = sb("prm2", [P, N_PRM2])
        x = sb("x", [P, NT, D])
        hT = sb("hT", [P, KD, T])
        hC = sb("hC", [P, KD, T])
        yT = sb("yT", [P, KD, T])
        ss = sb("ss", [P, 4])
        ms = sb("ms", [P, 8])
        rstd = sb("rstd", [P, 8])
        half = sb("half", [P, 8])
        scratch = sb("scratch", [P, N_SCRATCH])

        class Region:

            def __init__(self, mem, size, at=0):
                self.mem, self.size, self.at = mem, size, at

            def take(self, *shape):
                n = int(np.prod(shape))
                v = self.mem[:, self.at:self.at + n]
                self.at += n
                assert self.at <= self.size, (self.at, self.size)
                names = "abcd"[:len(shape)]
                if len(shape) == 1:
                    return v
                return v.rearrange(f"p ({' '.join(names)}) -> p {' '.join(names)}",
                                   **{k: s for k, s in zip(names[1:], shape[1:])})

        ident = const[:, K_ID:K_ID + P]
        cos2 = const[:, K_COS:K_COS + 2 * HD].rearrange("p (t d) -> p t d", t=NT)
        sin2 = const[:, K_SIN:K_SIN + 2 * HD].rearrange("p (t d) -> p t d", t=NT)
        ccos = const[:, K_CC:K_CC + P]
        nsin = const[:, K_SC:K_SC + P]
        dft = const[:, K_DFT:K_RANK].rearrange("p (t c) -> p t c", t=NT)

        lay = Region(scratch, N_SCRATCH)
        xn = lay.take(NT, D)
        lnrow = lay.take(2, G)
        wsT = lay.take(H, P)
        zi_at = lay.at
        zi = lay.take(NT, 320)
        wi = lay.take(NT, H)
        va = lay.take(NT, G)
        ra, rb = lay.take(5, HD), lay.take(5, HD)
        ga, gc = lay.take(8, HD), lay.take(8, HD)
        ri = lay.take(NT, 6, HD)
        riT = lay.take(3, T)
        rqT = lay.take(4, T)
        rel_at = lay.at
        rel = [lay.take(H, P), lay.take(H, T)]
        score = [lay.take(P), lay.take(T)]
        work = [lay.take(P), lay.take(T)]
        sel = [lay.take(P), lay.take(T)]
        mx = lay.take(NT, 8)
        cpad = lay.take(2, LONG - 1 + T)
        conv = lay.take(2, T)
        ycat = lay.take(NT, 2, G)
        nmx, nms, rsum, rinv = (lay.take(NT, H) for _ in range(4))
        bnst, bnag = lay.take(4, 6), lay.take(4, 2)
        again = Region(scratch, N_SCRATCH, rel_at)
        lg = [again.take(H, P), again.take(H, T)]
        chp = Region(scratch, N_SCRATCH, zi_at).take(2, SHORT - 1 + T)
        conv_n = conv
        rq = xn[:, :, 0:512].rearrange("p t (h d) -> p t h d", h=8)
        acs, sig = xn[:, :, 512:768], xn[:, :, 768:1024]
        chy = sig
        zz = hC[:, :, :].rearrange("p k t -> p (k t)")
        zq = zz[:, 0:1024].rearrange("p (t c) -> p t c", t=NT)
        zg = zz[:, 1024:2048].rearrange("p (t c) -> p t c", t=NT)
        pT0 = zz[:, 0:512].rearrange("p (h q) -> p h q", h=H)
        pT1 = zz[:, 1024:2048].rearrange("p (s h q) -> p s h q", s=2, h=H)
        ffn = Region(scratch, N_SCRATCH)
        sga, aT = ffn.take(2, T), ffn.take(2, T)

        again = Region(scratch, N_SCRATCH)
        gb = again.take(2, D)
        modc = again.take(4, KD, 2)
        cb_at = again.at
        xmp = again.take(MH, 2, CTX + 2)
        actT = again.take(MH, S2)
        ctx_at = again.at
        h_rows = again.take(NT, MW)
        pre_at = again.at
        pre = again.take(2, 2, CTX)
        xn2_at = again.at
        xn2 = again.take(NT, D)
        fT = again.take(4, T)
        w_rt = again.take(KD, NG + NE)
        b_rt = again.take(NG + NE)
        bst, bag = again.take(8, 6), again.take(8, 2)
        emn, rcol = again.take(NT, ROWS), again.take(4, ROWS)
        nq, rq2 = again.take(NT), again.take(NT)
        logit, expert_l, rank_v, pick1, pick2 = (again.take(NT, NG + NE) for _ in range(5))
        gd, ge, gsel = (again.take(NT, NG) for _ in range(3))
        t1, t2, t3, t4 = (again.take(NT) for _ in range(4))
        comb, combT = again.take(NT, NE), again.take(T)
        cs = again.take(KD, 2)
        cb = Region(scratch, N_SCRATCH, cb_at).take(NE, T)
        ctx_x = Region(scratch, N_SCRATCH, ctx_at).take(NT, D)
        tmp = Region(scratch, N_SCRATCH, ctx_at).take(4, 512)
        hm = Region(scratch, N_SCRATCH, pre_at).take(MH, T)
        pair = Region(scratch, N_SCRATCH, pre_at)
        sgE, aE = pair.take(2, T), pair.take(2, T)
        gfin = fT.rearrange("p a b -> p (a b)")
        fP = Region(scratch, N_SCRATCH, xn2_at).take(4, 512)
        pos = yT[:, :, :].rearrange("p k t -> p (k t)").rearrange("p (t d) -> p t d", t=NT)
        szT = hC[:, 0:4, :]
        u_rows = hC[:, 4:8, :].rearrange("p k t -> p (k t)").rearrange("p (t c) -> p t c", t=NT)
        w3 = Region(m[:, 3, :], 4096)
        bd = w3.take(3, MH, P)
        w_if = w3.take(3 * MH, P)
        w_f = w3.take(4, P)
        E = Region(m[:, 2, :], 4096).take(2, 2, 4, T)
        flat = blocks_w[:, :, :].rearrange("p s n -> p (s n)")
        modrow = flat[0:2, 0:NMOD * D]
        gpost = flat[0:2, NMOD * D:(NMOD + 2) * D]
        wide = Region(flat, 2 * BLOCK)
        qkvT = wide.take(3, MH, S2)
        vtok = wide.take(4, MH, DH + 1)
        gi, gf, gx, cum, rr, rmax = (wide.take(S2) for _ in range(6))

        filled = [sem(f"filled{n}") for n in range(8)]
        drained = [sem(f"drained{n}") for n in range(8)]
        dve_step, pool_step, passed = sem("dve_step"), sem("pool_step"), sem("passed")
        const_in, x_in, prm2_in = sem("const_in"), sem("x_in"), sem("prm2_in")
        prm_in, kwi_in, ab_in = sem("prm_in"), sem("kwi_in"), sem("ab_in")
        m_in = [sem(f"m{n}_in") for n in range(4)]
        block_in = [sem(f"block{n}_in") for n in range(2)]
        block_used = [sem(f"block{n}_used") for n in range(2)]
        half_ready, pads_ready = sem("half_ready"), sem("pads_ready")
        ss_ready, rstd_ready, xn_ready = sem("ss_ready"), sem("rstd_ready"), sem("xn_ready")
        ri_ready, rq_ready, ws_ready = sem("ri_ready"), sem("rq_ready"), sem("ws_ready")
        score_ready, score_masked = sem("score_ready"), sem("score_masked")
        sel_ready, sel_masked = sem("sel_ready"), sem("sel_masked")
        conv_ready, var_ready, norm_rstd = sem("conv_ready"), sem("var_ready"), sem("norm_rstd")
        v_norm, v_ready = sem("v_norm"), sem("v_ready")
        yb_ready, lg_ready, exp_ready, silu_ready = sem("yb_ready"), sem("lg_ready"), sem("exp_ready"), sem("silu_ready")
        weighed = sem("weighed")
        rows_in, pos_in, ctx_in, heads_in, router_in = (sem("rows_in"), sem("pos_in"), sem("ctx_in"), sem("heads_in"),
                                                     sem("router_in"))
        silu_c, mod_ready, mod_rows, gate_rows = sem("silu_c"), sem("mod_ready"), sem("mod_rows"), sem("gate_rows")
        x_ready, zeros_ready, pre_ready, act_ready = sem("x_ready"), sem("zeros_ready"), sem("pre_ready"), sem("act_ready")
        f_abs, f_log, scan_ready, e_masked, s_ready = (sem("f_abs"), sem("f_log"), sem("scan_ready"), sem("e_masked"),
                                                       sem("s_ready"))
        h_var, h_rstd, hn_ready, y_ready = sem("h_var"), sem("h_rstd"), sem("hn_ready"), sem("y_ready")
        g_diff, g_exp, e_diff, e_exp, comb_ready = (sem("g_diff"), sem("g_exp"), sem("e_diff"), sem("e_exp"),
                                                    sem("comb_ready"))
        expert_in = [sem(f"expert{n}_in") for n in range(2)]
        expert_used = [sem(f"expert{n}_used") for n in range(2)]
        out_ready, out_stored = sem("out_ready"), sem("out_stored")
        block = ctx.enter_context(nc.Block())

        def layer_results(l):
            return Results(filled, drained, LAY, [l * n for n in LAY.count])

        sec = Results(filled, drained, SEC, [DEPTH * n for n in LAY.count])
        B1, B0 = NFB // 2, (NFB + 1) // 2

        @block.sync
        def _(sp):
            for t in range(NT):
                sp.dma_start(x[:, t, :], a["x"][t * P:(t + 1) * P, :]).then_inc(x_in, 16)
            sp.dma_start(const[:, :], a["const"]).then_inc(const_in, 16)
            with sp.Fori(0, DEPTH) as l:
                res = layer_results(l)

                def w_in(name):
                    return a["w_in"][bass.ds(l, 1), :, IN_AT[name]:IN_AT[name] + KD * IN_COLS[name]]\
                        .rearrange("a p n -> p (a n)")

                def ffn_block(b):
                    return a["ffn"][bass.ds(l, 1), bass.ds(b, 1)].rearrange("a b p n -> p (a b n)")

                sp.dma_start(prm[:, :], a["prm"][bass.ds(l, 1)].rearrange("a p n -> p (a n)")).then_inc(prm_in, 16)
                sp.dma_start(lnrow.rearrange("p r n -> p (r n)"), a["gmlp_ln"][bass.ds(l, 1)]
                             .rearrange("a n -> (a n)").partition_broadcast(P)).then_inc(prm_in, 16)
                sp.dma_start(wsT.rearrange("p h n -> p (h n)"), a["w_s"][bass.ds(l, 1)]
                             .rearrange("a p n -> p (a n)")).then_inc(prm_in, 16)
                sp.dma_start(m[:, 0, :], w_in("vqi")).then_inc(m_in[0], 16)
                sp.dma_start(kwi_w[:, :, :].rearrange("p k n -> p (k n)"), w_in("kwi")).then_inc(kwi_in, 16)
                sp.dma_start(m[:, 2, :], w_in("dadg")).then_inc(m_in[2], 16)
                sp.dma_start(m[:, 1, :], w_in("qk")).then_inc(m_in[1], 16)
                sp.dma_start(m[:, 3, :], w_in("guv")).then_inc(m_in[3], 16)
                src = w_in("abac")
                sp.wait_ge(drained[3], l * LAY.count[3] + 1)
                sp.dma_start(blocks_w[:, 0, 0:4096], src).then_inc(ab_in, 16)
                sp.dma_start(blocks_w[:, 0, 4096:6144], w_in("ah")).then_inc(ab_in, 16)
                src = ffn_block(1)
                sp.wait_ge(block_used[1], B1 * l + 1)
                sp.dma_start(blocks_w[:, 1, :], src).then_inc(block_in[1], 16)
                for s, job in ((0, "vqi1"), (1, "qk1")):
                    src = a["w_out"][bass.ds(l, 1), :, s * 4096:(s + 1) * 4096].rearrange("a p n -> p (a n)")
                    res.ready(sp, job)
                    sp.dma_start(m[:, s, :], src).then_inc(m_in[s], 16)
                src = ffn_block(0)
                res.ready(sp, "ah")
                settle(sp, passed)
                sp.dma_start(blocks_w[:, 0, :], src).then_inc(block_in[0], 16)
                with sp.Fori(0, B1 - 1) as r:
                    src = ffn_block(2 * r + 2)
                    sp.wait_ge(block_used[0], B1 * l + r + 1)
                    sp.dma_start(blocks_w[:, 0, :], src).then_inc(block_in[0], 16)
                    src = ffn_block(2 * r + 3)
                    sp.wait_ge(block_used[1], B1 * l + r + 2)
                    sp.dma_start(blocks_w[:, 1, :], src).then_inc(block_in[1], 16)
                src = ffn_block(NFB - 1)
                sp.wait_ge(block_used[0], B1 * l + B1)
                sp.dma_start(blocks_w[:, 0, :], src).then_inc(block_in[0], 16)

            sp.dma_start(prm2[:, :], a["prm2"]).then_inc(prm2_in, 16)
            for s in range(4):
                sp.dma_start(m[:, s, :], a["w_ada"][0, s]).then_inc(m_in[s], 16)
            sp.wait_ge(block_used[1], B1 * DEPTH + 1)
            sp.dma_start(gpost, a["g_post"].partition_broadcast(2)).then_inc(rows_in, 16)
            sp.wait_ge(filled[3], DEPTH * LAY.count[3])
            sp.dma_start(modrow, a["b_ada"].partition_broadcast(2)).then_inc(rows_in, 16)
            sp.dma_start(yT[:, :, :].rearrange("p k t -> p (k t)"), a["pos"]).then_inc(pos_in, 16)
            sp.wait_ge(drained[3], DEPTH * LAY.count[3] + 1)
            sp.dma_start(gfin, a["g_final"].partition_broadcast(P)).then_inc(pos_in, 16)
            for t in range(NT):
                sp.dma_start(ctx_x[:, t, :], a["ctx"][t * P:(t + 1) * P, :]).then_inc(ctx_in, 16)
            sp.dma_start(w_rt.rearrange("p k n -> p (k n)"), a["w_router"]).then_inc(router_in, 16)
            sp.dma_start(b_rt, a["b_router"].partition_broadcast(P)).then_inc(router_in, 16)
            with sp.Fori(1, 3) as i:
                for s in range(4):
                    src = a["w_ada"][bass.ds(i, 1), s].rearrange("a p n -> p (a n)")
                    sp.wait_ge(filled[s], sec.index(f"ada{s}", 0)[1] + i)
                    sp.dma_start(m[:, s, :], src).then_inc(m_in[s], 16)
            for s in range(3):
                sec.ready(sp, f"ada{s}", 2)
                sp.dma_start(m[:, s, :], a["w_in_2"][s]).then_inc(m_in[s], 16)
            sec.ready(sp, "ada3", 2)
            sp.dma_start(m[:, 3, 0:3584], a["heads_2"]).then_inc(heads_in, 16)
            for s, job in ((0, "xm3"), (1, "z1")):
                sec.ready(sp, job)
                sp.dma_start(m[:, s, :], a["w_out_2"][:, s * 4096:(s + 1) * 4096]).then_inc(m_in[s], 16)
            even = m[:, 0:3, :].rearrange("p s n -> p (s n)")
            sec.ready(sp, "wo3")
            sp.dma_start(even, a["experts"][0]).then_inc(expert_in[0], 16)
            sp.dma_start(flat, a["experts"][1]).then_inc(expert_in[1], 16)
            with sp.Fori(0, NE // 2 - 1) as r:
                for n, to in enumerate((even, flat)):
                    src = a["experts"][bass.ds(2 * r + 2 + n, 1)].rearrange("a p n -> p (a n)")
                    sp.wait_ge(expert_used[n], r + 1)
                    sp.dma_start(to, src).then_inc(expert_in[n], 16)
            for t in range(NT):
                sp.wait_ge(out_ready, 2 * t + 2)
                sp.dma_start(out[t * P:(t + 1) * P, :], x[:, t, :]).then_inc(out_stored, 16)
            sp.wait_ge(out_stored, 16 * NT)

        @block.tensor
        def _(pe):
            def chain(out_, pairs, first=True, last=True):
                for n, (lhsT, rhs) in enumerate(pairs):
                    ins = pe.matmul(out_, lhsT, rhs, start=first and n == 0, stop=last and n == len(pairs) - 1,
                                    skip_group_check=not (first and last))
                return ins

            pe.wait_ge(const_in, 16)
            with pe.Fori(0, DEPTH) as l:
                res = layer_results(l)

                def to(job):
                    return bank[LAY.at[job][0]]

                def transposes(name, ready):
                    for t in range(NT):
                        pe.wait_ge(xn_ready, ready + t)
                        for b in range(2):
                            job = f"{name}_{t}{b}"
                            res.room(pe, job)
                            for k in range(4):
                                c = (4 * b + k) * P
                                ins = pe.transpose(to(job)[:, k * P:(k + 1) * P], xn[:, t, c:c + P], ident)
                            res.done(ins, job)

                def token_job(name, w, t):
                    job, cols = f"{name}{t}", w.shape[2]
                    res.room(pe, job)
                    res.done(chain(to(job)[:, 0:cols], [(hT[:, k, t * P:(t + 1) * P], w[:, k, :]) for k in range(KD)]), job)

                def feature_job(job, w, c0):
                    res.room(pe, job)
                    for g in range(2):
                        ins = chain(to(job)[:, g * T:(g + 1) * T],
                                    [(w[:, k, c0 + g * P:c0 + (g + 1) * P], hT[:, k, :]) for k in range(KD)])
                    res.done(ins, job)

                def w_view(s):
                    return m[:, s, :].rearrange("p (k n) -> p k n", k=KD)

                transposes("tx1", 4 * l + 1)
                pe.wait_ge(m_in[0], 32 * l + 16)
                for t in range(NT):
                    for b in range(2):
                        res.arrived(pe, f"tx1_{t}{b}")
                    token_job("vqi", w_view(0), t)
                pe.wait_ge(kwi_in, 16 * l + 16)
                for t in range(NT):
                    token_job("kwi", kwi_w[:, :, :], t)
                pe.wait_ge(m_in[2], 16 * l + 16)
                feature_job("da", w_view(2), 0)
                feature_job("dg", w_view(2), 256)

                for t in range(NT):
                    job = f"riT{t}"
                    pe.wait_ge(ri_ready, 2 * l + t + 1)
                    res.room(pe, job)
                    for c in range(3):
                        ins = pe.transpose(to(job)[:, c * P:(c + 1) * P],
                                           ri[:, t, 2 * c:2 * c + 2, :].rearrange("p h d -> p (h d)"), ident)
                    res.done(ins, job)
                pe.wait_ge(m_in[1], 32 * l + 16)
                for t in range(NT):
                    token_job("qk", w_view(1), t)
                for job, t, heads in (("sc0a", 0, (0, 2)), ("sc0b", 0, (1, 3)), ("sc1a", 1, (0, 2)), ("sc1b", 1, (1, 3))):
                    nk = (t + 1) * P
                    for u in range(t + 1):
                        res.arrived(pe, f"riT{u}")
                    res.room(pe, job)
                    for n, j in enumerate(heads):
                        o = HD * (j % 2)
                        ins = pe.matmul(to(job)[:, n * nk:(n + 1) * nk], riT[o:o + HD, j // 2, t * P:(t + 1) * P],
                                        riT[o:o + HD, 2, 0:nk], start=True, stop=True)
                    res.done(ins, job)
                pe.wait_ge(m_in[3], 16 * l + 16)
                for t in range(NT):
                    token_job("guv", w_view(3), t)
                pe.wait_ge(ab_in, 32 * l + 32)
                ab_w = blocks_w[:, 0, 0:4096].rearrange("p (k n) -> p k n", k=KD)
                feature_job("ab", ab_w, 0)
                feature_job("ac", ab_w, 256)
                feature_job("ah", blocks_w[:, 0, 4096:6144].rearrange("p (k n) -> p k n", k=KD), 0)
                for t in range(NT):
                    job = f"rqT{t}"
                    pe.wait_ge(rq_ready, 2 * l + t + 1)
                    res.room(pe, job)
                    for c in range(4):
                        ins = pe.transpose(to(job)[:, c * P:(c + 1) * P],
                                           rq[:, t, 2 * c:2 * c + 2, :].rearrange("p h d -> p (h d)"), ident)
                    res.done(ins, job)
                pe.wait_ge(conv_ready, l + 1)
                res.room(pe, "cvT")
                for t in range(NT):
                    for g in range(2):
                        ins = pe.transpose(to("cvT")[:, t * T + g * P:t * T + (g + 1) * P],
                                           conv[:, g, t * P:(t + 1) * P], ident)
                res.done(ins, "cvT")
                pe.wait_ge(ws_ready, l + 1)
                for t in range(NT):
                    job = f"mix{t}"
                    pe.wait_ge(v_ready, 2 * l + t + 1)
                    res.room(pe, job)
                    for h in range(H):
                        ins = pe.matmul(to(job)[:, h * HD:(h + 1) * HD], wsT[:, h, :],
                                        zg[:, t, G + h * HD:G + (h + 1) * HD], start=True, stop=True)
                    res.done(ins, job)
                for job, t, heads in (("lg0a", 0, (0, 2)), ("lg0b", 0, (1, 3)), ("lg1a", 1, (0, 2)), ("lg1b", 1, (1, 3))):
                    nk = (t + 1) * P
                    for u in range(t + 1):
                        res.arrived(pe, f"rqT{u}")
                    res.room(pe, job)
                    for n, h in enumerate(heads):
                        o = HD * (h % 2)
                        ins = pe.matmul(to(job)[:, n * nk:(n + 1) * nk], rqT[o:o + HD, h // 2, t * P:(t + 1) * P],
                                        rqT[o:o + HD, 2 + h // 2, 0:nk], start=True, stop=True)
                    res.done(ins, job)

                def mixed_rows(job, part, t):
                    for k in range(2):
                        ins = pe.transpose(to(job)[:, k * T + t * P:k * T + (t + 1) * P],
                                           ycat[:, t, part, k * P:(k + 1) * P], ident)
                    return ins

                res.room(pe, "ybT")
                for t in range(NT):
                    pe.wait_ge(yb_ready, 2 * l + t + 1)
                    ins = mixed_rows("ybT", 0, t)
                res.done(ins, "ybT")
                res.arrived(pe, "cvT")
                res.room(pe, "cnT")
                for g in range(2):
                    for t in range(NT):
                        ins = pe.transpose(to("cnT")[:, g * T + t * P:g * T + (t + 1) * P],
                                           conv_n[:, t, g * P:(g + 1) * P], ident)
                res.done(ins, "cnT")

                def out_proj(ks, first, last):
                    for n in range(4):
                        t, c = n // 2, n % 2
                        if first:
                            res.room(pe, f"wo{n}")
                        ins = chain(bank[n][:, :],
                                    [(yT[:, k, t * P:(t + 1) * P],
                                      m[:, k // 4, (k % 4) * D + c * 512:(k % 4) * D + (c + 1) * 512]) for k in ks],
                                    first, last)
                        if last:
                            res.done(ins, f"wo{n}")

                pe.wait_ge(m_in[0], 32 * l + 32)
                pe.wait_ge(m_in[1], 32 * l + 32)
                res.arrived(pe, "ybT")
                res.arrived(pe, "ab")
                out_proj((2, 3, 0, 1), True, False)
                res.arrived(pe, "cnT")
                out_proj((6, 7), False, False)
                for job, t, u in (("pT0", 0, 0), ("pT1a", 1, 0), ("pT1b", 1, 1)):
                    pe.wait_ge(exp_ready, 8 * l + 4 * t + 4)
                    res.room(pe, job)
                    for h in range(H):
                        ins = pe.transpose(to(job)[:, h * P:(h + 1) * P], lg[t][:, h, u * P:(u + 1) * P], ident)
                    res.done(ins, job)
                for t in range(NT):
                    job = f"av{t}"
                    for p_job in (("pT0",), ("pT1a", "pT1b"))[t]:
                        res.arrived(pe, p_job)
                    res.room(pe, job)
                    for h in range(H):
                        ins = chain(to(job)[:, h * HD:(h + 1) * HD],
                                    [(pT0[:, h, :] if t == 0 else pT1[:, u, h, :], va[:, u, h * HD:(h + 1) * HD])
                                     for u in range(t + 1)])
                    res.done(ins, job)
                res.room(pe, "ycT")
                for t in range(NT):
                    res.arrived(pe, f"av{t}")
                    ins = mixed_rows("ycT", 1, t)
                res.done(ins, "ycT")
                res.arrived(pe, "ycT")
                out_proj((4, 5), False, True)

                transposes("tx2", 4 * l + 3)
                for t in range(NT):
                    for b in range(2):
                        res.arrived(pe, f"tx2_{t}{b}")

                def gate_up(slot, j, i):
                    job = f"gu{j}"
                    res.room(pe, job, i)
                    w = blocks_w[:, slot, 0:4096].rearrange("p (q k n) -> p q k n", q=2, k=KD)
                    for q in range(2):
                        ins = chain(to(job)[:, q * T:(q + 1) * T],
                                    [(w[:, q, k, j * P:(j + 1) * P], hT[:, k, :]) for k in range(KD)])
                    res.done(ins, job)

                def down(slot, j, i, first=False, last=False):
                    res.arrived(pe, f"gu{j}", i)
                    for n in range(4):
                        t, c = n // 2, n % 2
                        if first:
                            res.room(pe, f"y{n}")
                        o = 4096 + j * D + c * 512
                        ins = chain(bank[n][:, :], [(aT[:, j, t * P:(t + 1) * P], blocks_w[:, slot, o:o + 512])], first, last)
                        if last:
                            res.done(ins, f"y{n}")
                    return ins

                pe.wait_ge(block_in[0], 16 * B0 * l + 16)
                gate_up(0, 0, 0)
                gate_up(0, 1, 0)
                down(0, 0, 0, first=True)
                with pe.Fori(0, B1) as r:
                    pe.wait_ge(block_in[1], 16 * B1 * l + 16 * r + 16)
                    gate_up(1, 0, 2 * r + 1)
                    down(0, 1, 2 * r).then_inc(block_used[0], 1)
                    gate_up(1, 1, 2 * r + 1)
                    down(1, 0, 2 * r + 1)
                    pe.wait_ge(block_in[0], 16 * B0 * l + 16 * r + 32)
                    gate_up(0, 0, 2 * r + 2)
                    down(1, 1, 2 * r + 1).then_inc(block_used[1], 1)
                    gate_up(0, 1, 2 * r + 2)
                    down(0, 0, 2 * r + 2)
                down(0, 1, NFB - 1, last=True)

            def to(job):
                return bank[SEC.at[job][0]]

            pe.wait_ge(silu_c, 1)
            with pe.Fori(0, 3) as i:
                for s in range(4):
                    pe.wait_ge(m_in[s], 16 * DEPTH * (2 if s < 2 else 1) + 16 * i + 16)
                    sec.room(pe, f"ada{s}", i)
                    w = m[:, s, :].rearrange("p (k n) -> p k n", k=KD)
                    sec.done(chain(bank[s][0:2, :], [(cs[:, k, :], w[:, k, :]) for k in range(KD)]), f"ada{s}")
            for s in range(4):
                sec.arrived(pe, f"ada{s}", 2)
            sec.room(pe, "modT")
            for n, row in enumerate((0, 1, 3, 4)):
                for k in range(KD):
                    ins = pe.transpose(to("modT")[:, 2 * (KD * n + k):2 * (KD * n + k) + 2],
                                       modrow[:, row * D + k * P:row * D + (k + 1) * P], ident[0:2, 0:2])
            sec.done(ins, "modT")
            pe.wait_ge(gate_rows, 2)
            for n in range(4):
                o = (2 + 3 * (n // 2)) * D + (n % 2) * 512
                sec.room(pe, f"gate{n}")
                sec.done(pe.matmul(bank[n][:, :], ident[0:2, 0:1].to_broadcast([2, P]), modrow[:, o:o + 512],
                                   start=True, stop=True), f"gate{n}")

            def transposes2(name, ready):
                for t in range(NT):
                    pe.wait_ge(xn_ready, ready + t)
                for n in range(4):
                    sec.room(pe, f"{name}{n}")
                    for k in range(2):
                        for t in range(NT):
                            c = (2 * n + k) * P
                            ins = pe.transpose(to(f"{name}{n}")[:, k * T + t * P:k * T + (t + 1) * P],
                                               xn2[:, t, c:c + P], ident)
                    sec.done(ins, f"{name}{n}")

            XN = 4 * DEPTH
            transposes2("tc", XN + 1)
            transposes2("tl", XN + 3)
            for n in range(4):
                sec.arrived(pe, f"tc{n}")
                sec.arrived(pe, f"tl{n}")
            M01, M23 = 32 * DEPTH + 48, 16 * DEPTH + 48
            w = [m[:, s, :].rearrange("p (k n) -> p k n", k=KD) for s in range(3)]
            pe.wait_ge(m_in[0], M01 + 16)
            for j in range(MH):
                sec.room(pe, f"xm{j}")
                for q, src in enumerate((hC, hT)):
                    ins = chain(to(f"xm{j}")[:, q * T:(q + 1) * T],
                                [(w[0][:, k, j * P:(j + 1) * P], src[:, k, :]) for k in range(KD)])
                sec.done(ins, f"xm{j}")
            pe.wait_ge(m_in[1], M01 + 16)
            for q in range(2):
                sec.room(pe, f"z{q}")
                for g in range(2):
                    j = 2 * q + g
                    ins = chain(to(f"z{q}")[:, g * T:(g + 1) * T],
                                [(w[1][:, k, j * P:(j + 1) * P], hT[:, k, :]) for k in range(KD)])
                sec.done(ins, f"z{q}")
            pe.wait_ge(m_in[2], M23 + 16)
            for t in range(NT):
                sec.room(pe, f"u{t}")
                sec.done(chain(to(f"u{t}")[:, :], [(hT[:, k, t * P:(t + 1) * P], w[2][:, k, :]) for k in range(KD)]), f"u{t}")
            pe.wait_ge(heads_in, 16)
            for j in range(MH):
                sec.arrived(pe, f"xm{j}")
            for c in range(4):
                sec.room(pe, f"vt{c}")
                for j in range(MH):
                    ins = pe.matmul(to(f"vt{c}")[:, j * DH:(j + 1) * DH],
                                    xmp[:, j, c // 2, 1 + (c % 2) * P:1 + (c % 2 + 1) * P], bd[:, 2, j, :], start=True, stop=True)
                sec.done(ins, f"vt{c}")
            for n in range(12):
                j, q = n // 3, n % 3
                if q == 0:
                    pe.wait_ge(act_ready, j + 1)
                sec.room(pe, f"qkv{n}")
                src = actT[:, j, :].rearrange("p (s t) -> p s t", s=2) if q < 2 else xmp[:, j, :, 1:1 + CTX]
                sec.done(pe.matmul(to(f"qkv{n}")[:, :].rearrange("p (s t) -> p s t", s=2), bd[:, q, j, :], src,
                                   start=True, stop=True), f"qkv{n}")
            for g in range(4):
                sec.room(pe, f"fp{g}")
                for t in range(NT):
                    sec.arrived(pe, f"u{t}")
                sec.done(chain(to(f"fp{g}")[:, :], [(u_rows[:, t, g * P:(g + 1) * P], dft[:, t, :]) for t in range(NT)]), f"fp{g}")
            for n in range(12):
                sec.arrived(pe, f"qkv{n}")
            sec.room(pe, "gates")
            sec.done(chain(to("gates")[:, :], [(w_if[:, 4 * q + j, :], qkvT[:, q, j, :]) for j in range(MH) for q in range(3)]),
                     "gates")
            for p in range(2):
                sec.room(pe, f"ff{p}")
                for g in (2 * p, 2 * p + 1):
                    sec.arrived(pe, f"fp{g}")
                    ins = chain(to(f"ff{p}")[:, (g % 2) * T:(g % 2 + 1) * T],
                                [(ccos, fP[:, g, 0:T]), (nsin, fP[:, g, T:2 * T])])
                sec.done(ins, f"ff{p}")
            for p in range(2):
                sec.arrived(pe, f"ff{p}")
                sec.room(pe, f"fy{p}")
                for g in (2 * p, 2 * p + 1):
                    ins = pe.matmul(to(f"fy{p}")[:, (g % 2) * T:(g % 2 + 1) * T], w_f[:, g, :], fT[:, g, :],
                                    start=True, stop=True)
                sec.done(ins, f"fy{p}")
            pe.wait_ge(scan_ready, 1)
            sec.room(pe, "rT")
            for c in range(4):
                pe.transpose(to("rT")[:, c * ROWS:(c + 1) * ROWS], rr[0:ROWS, c * P:(c + 1) * P], ident[0:ROWS, 0:ROWS])
            for t in range(NT):
                ins = pe.transpose(to("rT")[:, (4 + t) * ROWS:(5 + t) * ROWS], cum[0:ROWS, CTX + t * P:CTX + (t + 1) * P],
                                   ident[0:ROWS, 0:ROWS])
            sec.done(ins, "rT")

            def head_scores(h):
                sec.room(pe, f"rb{h}")
                for d in range(2):
                    r = 32 * d + h
                    ins = pe.matmul(to(f"rb{h}")[:, d * T:(d + 1) * T], ident[0:ROWS, r:r + 1].to_broadcast([ROWS, P]),
                                    rmax[0:ROWS, CTX:S2], start=True, stop=True)
                sec.done(ins, f"rb{h}")
                for job, cc in ((f"qk{h}a", 0), (f"qk{h}b", 2)):
                    sec.room(pe, job)
                    for c in (cc, cc + 1):
                        ins = pe.matmul(to(job)[:, (c - cc) * T:(c - cc + 1) * T], qkvT[:, 1, h, c * P:(c + 1) * P],
                                        qkvT[:, 0, h, CTX:S2], start=True, stop=True)
                    sec.done(ins, job)

            def head_values(h):
                for d in range(2):
                    if d == 0:
                        pe.wait_ge(s_ready, h + 1)
                    else:
                        sec.arrived(pe, f"qk{h}b")
                    job = f"o{h}{d}"
                    sec.room(pe, job)
                    for t in range(NT):
                        seen = ((0, 1, 2), (0, 1, 2, 3))[t] if d == 0 else ((0, 1, 2, 3), (0, 1, 3))[t]
                        ins = chain(to(job)[:, t * (DH + 1):(t + 1) * (DH + 1)],
                                    [(E[:, h % 2, d, c, t * P:(t + 1) * P], vtok[:, c, h, :]) for c in seen])
                    sec.done(ins, job)

            head_scores(0)
            for h in range(MH):
                if h + 1 < MH:
                    head_scores(h + 1)
                head_values(h)
            for p in range(2):
                pe.wait_ge(hn_ready, 1)
                sec.room(pe, f"hT{p}")
                for g in range(2):
                    for t in range(NT):
                        h = 2 * p + g
                        ins = pe.transpose(to(f"hT{p}")[:, g * T + t * P:g * T + (t + 1) * P],
                                           h_rows[:, t, h * DH:(h + 1) * DH], ident)
                sec.done(ins, f"hT{p}")
            pe.wait_ge(m_in[0], M01 + 32)
            pe.wait_ge(m_in[1], M01 + 32)

            def out_proj2(ks, first, last):
                for n in range(4):
                    t, c = n // 2, n % 2
                    if first:
                        sec.room(pe, f"wo{n}")
                    ins = chain(bank[n][:, :],
                                [(yT[:, k, t * P:(t + 1) * P],
                                  m[:, k // 4, (k % 4) * D + c * 512:(k % 4) * D + (c + 1) * 512]) for k in ks], first, last)
                    if last:
                        sec.done(ins, f"wo{n}")

            for p in range(2):
                sec.arrived(pe, f"fy{p}")
            out_proj2((4, 5, 6, 7), True, False)
            pe.wait_ge(y_ready, MH)
            out_proj2((0, 1, 2, 3), False, True)
            transposes2("t2", XN + 5)
            for n in range(4):
                sec.arrived(pe, f"t2{n}")
            pe.wait_ge(router_in, 32)
            for t in range(NT):
                sec.room(pe, f"rt{t}")
                sec.done(chain(to(f"rt{t}")[:, 0:NG + NE], [(hT[:, k, t * P:(t + 1) * P], w_rt[:, k, :]) for k in range(KD)]),
                         f"rt{t}")
            pe.wait_ge(comb_ready, 1)
            sec.room(pe, "cT")
            for t in range(NT):
                ins = pe.transpose(to("cT")[0:NE, t * P:(t + 1) * P], comb[:, t, :], ident)
            sec.done(ins, "cT")
            sec.arrived(pe, "cT")
            for n in range(NE // 2):
                sec.room(pe, f"cb{n}")
                for q in range(2):
                    e = 2 * n + q
                    ins = pe.matmul(to(f"cb{n}")[:, q * T:(q + 1) * T], ident[0:NE, e:e + 1].to_broadcast([NE, P]),
                                    combT[0:NE, :], start=True, stop=True)
                sec.done(ins, f"cb{n}")

            expert_w = [m[:, 0:3, :].rearrange("p s n -> p (s n)"), flat]

            def expert_gate_up(slot, j, i):
                job = f"eg{j % 2}"
                sec.room(pe, job, i)
                w = expert_w[slot][:, 0:2 * 4096].rearrange("p (q k n) -> p q k n", q=2, k=KD)
                for q in range(2):
                    ins = chain(to(job)[:, q * T:(q + 1) * T],
                                [(w[:, q, k, j * P:(j + 1) * P], hT[:, k, :]) for k in range(KD)])
                sec.done(ins, job)

            def expert_down(slot, j, i, first=False, last=False):
                sec.arrived(pe, f"eg{j % 2}", i)
                for n in range(4):
                    t, c = n // 2, n % 2
                    if first:
                        sec.room(pe, f"ye{n}")
                    o = 2 * 4096 + j * D + c * 512
                    ins = chain(bank[n][:, :], [(aE[:, j % 2, t * P:(t + 1) * P], expert_w[slot][:, o:o + 512])], first, last)
                    if last:
                        sec.done(ins, f"ye{n}")
                return ins

            def expert_pair(r, first=False, last=False):
                for slot in range(2):
                    for j in range(4):
                        n = 4 * slot + j
                        if n == 3:
                            pe.wait_ge(expert_in[1], 16 * r + 16)
                        if n == 7 and not last:
                            pe.wait_ge(expert_in[0], 16 * r + 32)
                        if n < 7 or not last:
                            expert_gate_up((n + 1) // 4 % 2, (n + 1) % 4, 4 * r + (n + 1) // 2)
                        ins = expert_down(slot, j, 4 * r + n // 2, first and n == 0, last and n == 7)
                    if not (last and slot):
                        ins.then_inc(expert_used[slot], 1)

            pe.wait_ge(expert_in[0], 16)
            expert_gate_up(0, 0, 0)
            expert_pair(0, first=True)
            with pe.Fori(1, NE // 2 - 1) as r:
                expert_pair(r)
            expert_pair(NE // 2 - 1, last=True)

        @block.scalar
        def _(act):
            act.wait_ge(x_in, 16 * NT)
            with act.Fori(0, DEPTH) as l:
                res = layer_results(l)

                def to(job):
                    return bank[LAY.at[job][0]]

                def copy(job, dst, src, func=ACT.Copy, last=True):
                    ins = act.activation(dst, src, func)
                    if last:
                        res.moved(ins, job)

                def squares():
                    for t in range(NT):
                        act.activation(xn[:, t, :], x[:, t, :], ACT.Square, accum_out=ss[:, t:t + 1]).then_inc(ss_ready, 1)

                act.wait_ge(drained[3], l * LAY.count[3] + 1)
                squares()
                act.wait_ge(prm_in, 48 * l + 48)
                for t in range(NT):
                    res.ready(act, f"vqi{t}")
                    copy(None, zi[:, t, 0:256], to(f"vqi{t}")[:, 256:512], last=False)
                    copy(f"vqi{t}", va[:, t, :], to(f"vqi{t}")[:, 0:256])
                for t in range(NT):
                    res.ready(act, f"kwi{t}")
                    act.activation(wi[:, t, :], to(f"kwi{t}")[:, 64:68], ACT.Copy, scale=(H * HD) ** -0.5)
                    copy(f"kwi{t}", zi[:, t, 256:320], to(f"kwi{t}")[:, 0:64])
                res.ready(act, "dg")
                copy("dg", sig, to("dg")[:, :].rearrange("p (g t) -> p g t", g=2), ACT.Sigmoid)
                for t in range(NT):
                    res.ready(act, f"riT{t}")
                    copy(f"riT{t}", riT[:, :, t * P:(t + 1) * P], to(f"riT{t}")[:, 0:3 * P].rearrange("p (c q) -> p c q", c=3))
                for t in range(NT):
                    res.ready(act, f"qk{t}")
                    copy(f"qk{t}", zq[:, t, :], to(f"qk{t}")[:, :])
                for job, t, h0 in (("sc0a", 0, 0), ("sc0b", 0, 1), ("sc1a", 1, 0), ("sc1b", 1, 1)):
                    res.ready(act, job)
                    copy(job, rel[t][:, h0::2, :], to(job)[:, 0:2 * (t + 1) * P].rearrange("p (h s) -> p h s", h=2), ACT.Relu)
                for t in range(NT):
                    res.ready(act, f"guv{t}")
                    copy(f"guv{t}", zg[:, t, :], to(f"guv{t}")[:, :])
                res.ready(act, "ac")
                copy("ac", acs, to("ac")[:, :].rearrange("p (g t) -> p g t", g=2))
                for t in range(NT):
                    res.ready(act, f"rqT{t}")
                    copy(f"rqT{t}", rqT[:, :, t * P:(t + 1) * P], to(f"rqT{t}")[:, :].rearrange("p (c q) -> p c q", c=4))
                res.ready(act, "ybT")
                copy("ybT", yT[:, 2:4, :], to("ybT")[:, :].rearrange("p (k t) -> p k t", k=2))
                res.ready(act, "cnT")
                for g in range(2):
                    ins = act.activation(yT[:, 6 + g, :], to("cnT")[:, g * T:(g + 1) * T], ACT.Silu,
                                         scale=prm[:, C_LNG + g:C_LNG + g + 1], bias=prm[:, C_LNB + g:C_LNB + g + 1])
                res.moved(ins, "cnT")
                for t in range(NT):
                    act.wait_ge(lg_ready, 2 * l + t + 1)
                    for h in range(H):
                        act.activation(lg[t][:, h, :], lg[t][:, h, :], ACT.Exp, scale=HD ** -0.5, bias=nms[:, t, h:h + 1],
                                       accum_out=rsum[:, t, h:h + 1]).then_inc(exp_ready, 1)
                for job, dst in (("pT0", pT0), ("pT1a", pT1[:, 0]), ("pT1b", pT1[:, 1])):
                    res.ready(act, job)
                    copy(job, dst, to(job)[:, :].rearrange("p (h q) -> p h q", h=H))
                res.ready(act, "ycT")
                copy("ycT", yT[:, 4:6, :], to("ycT")[:, :].rearrange("p (k t) -> p k t", k=2))
                res.arrived(act, "wo3")
                squares()
                with act.Fori(0, NFB) as i:
                    for j in range(2):
                        res.ready(act, f"gu{j}", i)
                        act.activation(sga[:, j, :], to(f"gu{j}")[:, 0:T], ACT.Silu).then_inc(silu_ready, 1)

            def to(job):
                return bank[SEC.at[job][0]]

            def copy(job, dst, src):
                sec.ready(act, job)
                sec.moved(act.activation(dst, src, ACT.Copy), job)

            act.wait_ge(drained[3], DEPTH * LAY.count[3] + 1)
            act.wait_ge(prm2_in, 16)
            act.activation(cs.rearrange("p k r -> p r k"), prm2[:, C2_C:C2_C + 2 * KD].rearrange("p (r k) -> p r k", r=2),
                           ACT.Silu).then_inc(silu_c, 1)
            for t in range(NT):
                act.activation(xn2[:, t, :], x[:, t, :], ACT.Square, accum_out=ss[:, t:t + 1]).then_inc(ss_ready, 1)
            act.wait_ge(x_ready, 2)
            act.wait_ge(ctx_in, 32)
            for n, (src, o) in enumerate(((ctx_x, 2), (x, 0))):
                act.wait_ge(ss_ready, 4 * DEPTH + 2 + 2 * n)
                for t in range(NT):
                    act.activation(xn2[:, t, :], src[:, t, :], ACT.Square, accum_out=ss[:, o + t:o + t + 1])\
                       .then_inc(ss_ready, 1)
            for n in range(4):
                copy(f"gate{n}", gb[:, n // 2, (n % 2) * 512:(n % 2 + 1) * 512], to(f"gate{n}")[:, :])

            def modulated(name, dst, kind, row):
                for n in range(4):
                    sec.ready(act, f"{name}{n}")
                    for k in range(2):
                        f = 2 * n + k
                        ins = act.activation(dst[:, f, :], to(f"{name}{n}")[:, k * T:(k + 1) * T], ACT.Identity,
                                             scale=modc[:, kind + 1, f, row:row + 1], bias=modc[:, kind, f, row:row + 1])
                    sec.moved(ins, f"{name}{n}")

            act.wait_ge(mod_ready, 1)
            modulated("tc", hC, 0, 1)
            modulated("tl", hT, 0, 0)
            act.wait_ge(zeros_ready, 1)
            for j in range(MH):
                copy(f"xm{j}", xmp[:, j, :, 1:1 + CTX], to(f"xm{j}")[:, :].rearrange("p (s t) -> p s t", s=2))
            for q in range(2):
                sec.ready(act, f"z{q}")
                sec.moved(act.activation(szT[:, 2 * q:2 * q + 2, :], to(f"z{q}")[:, :].rearrange("p (g t) -> p g t", g=2),
                                         ACT.Silu), f"z{q}")
            for j in range(MH):
                act.wait_ge(pre_ready, j + 1)
                act.activation(actT[:, j, :].rearrange("p (s t) -> p s t", s=2), pre[:, j % 2], ACT.Silu,
                               bias=prm2[:, C2_CONVB + j:C2_CONVB + j + 1]).then_inc(act_ready, 1)
            for n in range(12):
                if n % 3 < 2:
                    copy(f"qkv{n}", qkvT[:, n % 3, n // 3, :], to(f"qkv{n}")[:, :])
            for g in range(4):
                copy(f"fp{g}", fP[:, g, :], to(f"fp{g}")[:, :])
            sec.ready(act, "gates")
            act.activation(gi[0:ROWS, :], to("gates")[0:ROWS, :], ACT.Identity, bias=prm2[0:ROWS, C2_IG:C2_IG + 1])
            sec.moved(act.activation(gf[0:ROWS, :], to("gates")[64:64 + ROWS, :], ACT.Copy), "gates")
            act.wait_ge(f_abs, 1)
            act.activation(gx[0:ROWS, :], gx[0:ROWS, :], ACT.Exp).then_inc(f_log, 1)
            act.wait_ge(f_log, 1)
            act.activation(gx[0:ROWS, :], gx[0:ROWS, :], ACT.Ln, bias=1.0).then_inc(f_log, 1)
            for p in range(2):
                copy(f"fy{p}", yT[:, 4 + 2 * p:6 + 2 * p, :], to(f"fy{p}")[:, :].rearrange("p (g t) -> p g t", g=2))
            sec.ready(act, "rT")
            act.activation(rcol, to("rT")[:, 0:4 * ROWS].rearrange("p (c r) -> p c r", c=4), ACT.Copy)
            sec.moved(act.activation(emn, to("rT")[:, 4 * ROWS:6 * ROWS].rearrange("p (t r) -> p t r", t=NT), ACT.Exp,
                                     scale=-1.0), "rT")
            sec.arrived(act, "rT")
            act.wait_ge(zeros_ready, 2)
            for h in range(MH):
                sec.ready(act, f"rb{h}")
                for d in range(2):
                    for c in range(4):
                        lo = P if (d, c) == (0, 3) else 0
                        hi = P if (d, c) == (1, 2) else T
                        ins = act.activation(E[:, h % 2, d, c, lo:hi], to(f"rb{h}")[:, d * T + lo:d * T + hi], ACT.Exp,
                                             scale=-1.0, bias=rcol[:, c, 32 * d + h:32 * d + h + 1])
                sec.moved(ins, f"rb{h}")
            for p in range(2):
                sec.ready(act, f"hT{p}")
                for g in range(2):
                    h = 2 * p + g
                    ins = act.activation(hm[:, h, :], to(f"hT{p}")[:, g * T:(g + 1) * T], ACT.Identity,
                                         scale=prm2[:, C2_NORM + h:C2_NORM + h + 1])
                sec.moved(ins, f"hT{p}")

            def result_squares(name):
                for n in range(4):
                    sec.ready(act, f"{name}{n}")
                    act.activation(xn2[:, n // 2, (n % 2) * 512:(n % 2 + 1) * 512], bank[n][:, :], ACT.Square,
                                   accum_out=ss[:, n:n + 1]).then_inc(ss_ready, 1)

            result_squares("wo")
            act.wait_ge(x_ready, 4)
            for t in range(NT):
                act.activation(xn2[:, t, :], x[:, t, :], ACT.Square, accum_out=ss[:, t:t + 1]).then_inc(ss_ready, 1)
            modulated("t2", hT, 2, 0)
            act.wait_ge(g_diff, 1)
            act.activation(ge, gd, ACT.Exp).then_inc(g_exp, 1)
            act.wait_ge(e_diff, 1)
            act.activation(t3, t3, ACT.Exp).then_inc(e_exp, 1)
            for n in range(NE // 2):
                copy(f"cb{n}", cb[:, 2 * n:2 * n + 2, :], to(f"cb{n}")[:, :].rearrange("p (e t) -> p e t", e=2))
            with act.Fori(0, NE) as e:
                for j in range(4):
                    sec.ready(act, f"eg{j % 2}", 2 * e + j // 2)
                    act.activation(sgE[:, j % 2, :], to(f"eg{j % 2}")[:, 0:T], ACT.Silu).then_inc(silu_ready, 1)
            result_squares("ye")

        @block.vector
        def _(dve):
            dve.memset(half[:, :], -0.5).then_inc(half_ready, 1)
            dve.memset(cpad[:, :, 0:LONG - 1], 0.0).then_inc(pads_ready, 1)
            dve.wait_ge(pads_ready, 1)
            dve.wait_ge(const_in, 16)
            with dve.Fori(0, DEPTH) as l:
                res = layer_results(l)
                S = Steps(dve, dve_step, l * DVE_STEPS)

                def to(job):
                    return bank[LAY.at[job][0]]

                def col(c):
                    return prm[:, c:c + 1]

                def norm(n):
                    dve.wait_ge(rstd_ready, 2 * l + n + 1)
                    for t in range(NT):
                        dve.tensor_scalar(xn[:, t, :], x[:, t, :], rstd[:, t:t + 1], None, ALU.mult).then_inc(xn_ready, 1)

                def gained(name, gain):
                    for t in range(NT):
                        for b in range(2):
                            job = f"{name}_{t}{b}"
                            res.ready(dve, job)
                            g = prm[:, gain + 4 * b:gain + 4 * b + 4].unsqueeze(2).to_broadcast([P, 4, P])
                            res.moved(dve.tensor_tensor(hT[:, 4 * b:4 * b + 4, t * P:(t + 1) * P],
                                                        to(job)[:, :].rearrange("p (k q) -> p k q", k=4), g, ALU.mult), job)

                norm(0)
                dve.wait_ge(prm_in, 48 * l + 48)
                gained("tx1", C_GMIX)
                for t in range(NT):
                    res.arrived(dve, f"kwi{t}")
                    z5 = zi[:, t, :].rearrange("p (h d) -> p h d", h=5)
                    hd = HD // 2
                    S.did(dve.tensor_tensor(ra, z5, cos2[:, t, :].unsqueeze(1).to_broadcast([P, 5, HD]), ALU.mult))
                    S.did(dve.tensor_tensor(rb[:, :, 0:hd], z5[:, :, hd:HD],
                                            sin2[:, t, 0:hd].unsqueeze(1).to_broadcast([P, 5, hd]), ALU.mult))
                    S.then(dve.tensor_tensor(rb[:, :, hd:HD], z5[:, :, 0:hd],
                                             sin2[:, t, hd:HD].unsqueeze(1).to_broadcast([P, 5, hd]), ALU.mult))
                    S.then(dve.tensor_tensor(ri[:, t, 0:5, :], ra, rb, ALU.add))
                    dve.tensor_copy(ri[:, t, 5, :], ri[:, t, 4, :]).then_inc(ri_ready, 1)
                res.ready(dve, "da")
                res.arrived(dve, "dg")
                res.moved(dve.tensor_tensor(cpad[:, :, LONG - 1:], to("da")[:, :].rearrange("p (g t) -> p g t", g=2), sig,
                                            ALU.mult), "da")
                res.arrived(dve, "da")
                tap_done = [0, 0]

                def taps(ws):
                    for w in ws:
                        for g in range(2):
                            c, shifted = col(C_LONG + 2 * w + g), cpad[:, g, w:w + T]
                            if w == 0:
                                ins = dve.tensor_scalar(conv[:, g, :], shifted, c, col(C_BCONF + g), ALU.mult, ALU.add)
                            else:
                                S.need(tap_done[g])
                                ins = dve.scalar_tensor_tensor(conv[:, g, :], shifted, c, conv[:, g, :], ALU.mult, ALU.add)
                            if (w, g) == (LONG - 1, 1):
                                ins.then_inc(conv_ready, 1)
                            else:
                                tap_done[g] = S.did(ins)

                taps(range(0, 13))
                for t in range(NT):
                    for job in (f"sc{t}a", f"sc{t}b"):
                        res.arrived(dve, job)
                    for j in range(H):
                        w = wi[:, t, j:j + 1]
                        if j == 0:
                            ins = dve.tensor_scalar(score[t], rel[t][:, 0, :], w, None, ALU.mult)
                        else:
                            ins = dve.scalar_tensor_tensor(score[t], rel[t][:, j, :], w, score[t], ALU.mult, ALU.add)
                        if j < H - 1:
                            S.then(ins)
                    ins.then_inc(score_ready, 1)
                taps((13, 14))
                for t in range(NT):
                    dve.wait_ge(score_masked, 2 * l + t + 1)
                settle(dve, passed)
                for r in range(TOPK // 8):
                    src = score if r == 0 else work
                    for t in range(NT):
                        n = S.did(dve.max(mx[:, t, :], src[t]))
                    taps((15 + 2 * r,))
                    S.need(n)
                    settle(dve, passed)
                    for t in range(NT):
                        n = S.did(dve.match_replace(work[t], mx[:, t, :], src[t], TAKEN))
                    taps((16 + 2 * r,))
                    S.need(n)
                    settle(dve, passed)
                for t in range(NT):
                    dve.tensor_scalar(sel[t], work[t], TAKEN, 1.0, ALU.is_equal, ALU.subtract).then_inc(sel_ready, 1)
                for t in range(NT):
                    res.arrived(dve, f"guv{t}")
                    S.did(dve.bn_stats(bnst[:, t, :], zg[:, t, G:2 * G]))
                res.ready(dve, "cvT")
                for t in range(NT):
                    n = S.did(dve.bn_stats(bnst[:, 2 + t, :], to("cvT")[:, t * T:(t + 1) * T]))
                S.need(n)
                settle(dve, passed)
                for t in range(4):
                    ins = dve.bn_aggr(bnag[:, t, :], bnst[:, t, :])
                ins.then_inc(var_ready, 1)
                dve.wait_ge(norm_rstd, l + 1)
                for t in range(NT):
                    dve.tensor_scalar(zg[:, t, G:2 * G], zg[:, t, G:2 * G], bnag[:, t, 0:1], rstd[:, 2 + t:3 + t],
                                      ALU.subtract, ALU.mult).then_inc(v_norm, 1)
                for t in range(NT):
                    ins = dve.tensor_scalar(conv_n[:, t, :], to("cvT")[:, t * T:(t + 1) * T], bnag[:, 2 + t, 0:1],
                                            rstd[:, 4 + t:5 + t], ALU.subtract, ALU.mult)
                res.moved(ins, "cvT")
                S.then(dve.memset(chp[:, :, 0:SHORT - 1], 0.0))
                res.ready(dve, "ah")
                res.arrived(dve, "ac")
                res.moved(dve.tensor_tensor(chp[:, :, SHORT - 1:], to("ah")[:, :].rearrange("p (g t) -> p g t", g=2), acs,
                                            ALU.mult), "ah")
                res.arrived(dve, "ah")
                for w in range(SHORT):
                    for g in range(2):
                        c, shifted = col(C_SHORT + 2 * w + g), chp[:, g, w:w + T]
                        if w == 0:
                            n = S.did(dve.tensor_scalar(chy[:, g, :], shifted, c, None, ALU.mult))
                        else:
                            S.need(n - 1)
                            n = S.did(dve.scalar_tensor_tensor(chy[:, g, :], shifted, c, chy[:, g, :], ALU.mult, ALU.add))
                S.need(n)
                res.ready(dve, "ab")
                res.moved(dve.tensor_tensor(yT[:, 0:2, :], to("ab")[:, :].rearrange("p (g t) -> p g t", g=2), chy, ALU.mult), "ab")
                for t in range(NT):
                    res.ready(dve, f"mix{t}")
                    yb = ycat[:, t, 0, :]
                    res.moved(dve.tensor_tensor(yb.rearrange("p (h d) -> p h d", h=H),
                                                to(f"mix{t}")[:, 0:G].rearrange("p (h d) -> p h d", h=H),
                                                prm[:, C_BS:C_BS + H].unsqueeze(2).to_broadcast([P, H, HD]), ALU.add), f"mix{t}")
                    res.arrived(dve, f"mix{t}")
                    dve.tensor_tensor(yb, yb, zg[:, t, 0:G], ALU.mult).then_inc(yb_ready, 1)
                for t in range(NT):
                    dve.wait_ge(sel_masked, 2 * l + t + 1)
                    nk = (t + 1) * P
                    for job, h0 in ((f"lg{t}a", 0), (f"lg{t}b", 1)):
                        res.ready(dve, job)
                        res.moved(dve.scalar_tensor_tensor(lg[t][:, h0::2, :], sel[t].unsqueeze(1).to_broadcast([P, 2, nk]),
                                                           -NEG, to(job)[:, 0:2 * nk].rearrange("p (h s) -> p h s", h=2),
                                                           ALU.mult, ALU.add), job)
                        res.arrived(dve, job)
                    S.then(dve.tensor_reduce(nmx[:, t, :], lg[t], AX.X, ALU.max, negate=True))
                    dve.tensor_scalar(nms[:, t, :], nmx[:, t, :], HD ** -0.5, None, ALU.mult).then_inc(lg_ready, 1)
                for t in range(NT):
                    dve.wait_ge(exp_ready, 8 * l + 4 * t + 4)
                    S.then(dve.reciprocal(rinv[:, t, :], rsum[:, t, :]))
                    res.ready(dve, f"av{t}")
                    res.moved(dve.tensor_tensor(ycat[:, t, 1, :].rearrange("p (h d) -> p h d", h=H),
                                                to(f"av{t}")[:, 0:G].rearrange("p (h d) -> p h d", h=H),
                                                rinv[:, t, :].unsqueeze(2).to_broadcast([P, H, HD]), ALU.mult), f"av{t}")

                def add_to_x(name):
                    for n in range(4):
                        res.ready(dve, f"{name}{n}")
                        part = x[:, n // 2, (n % 2) * 512:(n % 2 + 1) * 512]
                        res.moved(dve.tensor_tensor(part, part, bank[n][:, :], ALU.add), f"{name}{n}")

                add_to_x("wo")
                norm(1)
                gained("tx2", C_GFFN)
                with dve.Fori(0, NFB) as i:
                    for j in range(2):
                        dve.wait_ge(silu_ready, 2 * NFB * l + 2 * i + j + 1)
                        res.moved(dve.tensor_tensor(aT[:, j, :], sga[:, j, :], to(f"gu{j}")[:, T:2 * T], ALU.mult), f"gu{j}")
                add_to_x("y")
                assert S.n == DVE_STEPS, S.n

            S = Steps(dve, dve_step, DEPTH * DVE_STEPS)

            def to(job):
                return bank[SEC.at[job][0]]

            def copy(job, dst, src):
                sec.ready(dve, job)
                sec.moved(dve.tensor_copy(dst, src), job)

            def normed(count, src, o):
                dve.wait_ge(rstd_ready, 2 * DEPTH + count)
                for t in range(NT):
                    dve.tensor_scalar(xn2[:, t, :], src[:, t, :], rstd[:, o + t:o + t + 1], None, ALU.mult).then_inc(xn_ready, 1)

            dve.wait_ge(drained[3], DEPTH * LAY.count[3] + 1)
            dve.wait_ge(pos_in, 32)
            dve.wait_ge(rstd_ready, 2 * DEPTH + 1)
            for t in range(NT):
                S.then(dve.scalar_tensor_tensor(x[:, t, :], x[:, t, :], rstd[:, t:t + 1], gfin, ALU.mult, ALU.mult))
                dve.tensor_tensor(x[:, t, :], x[:, t, :], pos[:, t, :], ALU.add).then_inc(x_ready, 1)
            dve.wait_ge(rows_in, 32)
            with dve.Fori(0, 3) as i:
                for s in range(4):
                    sec.ready(dve, f"ada{s}", i)
                    part = modrow[:, bass.ds(2048 * i + 512 * s, 512)]
                    sec.moved(dve.tensor_tensor(part, part, bank[s][0:2, :], ALU.add), f"ada{s}")
            for s in range(4):
                sec.arrived(dve, f"ada{s}", 2)
            for q in range(2):
                part = modrow[:, (2 + 3 * q) * D:(3 + 3 * q) * D]
                dve.tensor_tensor(part, part, gpost[:, q * D:(q + 1) * D], ALU.mult).then_inc(gate_rows, 1)
            copy("modT", modc.rearrange("p n k r -> p (n k r)"), to("modT")[:, 0:64])
            sec.arrived(dve, "modT")
            for kind, gain in ((1, C2_PREMIX), (3, C2_PREFFN)):
                S.then(dve.tensor_scalar(modc[:, kind], modc[:, kind], 1.0, None, ALU.add))
                ins = dve.tensor_tensor(modc[:, kind], modc[:, kind],
                                        prm2[:, gain:gain + KD].unsqueeze(2).to_broadcast([P, KD, 2]), ALU.mult)
                if kind == 1:
                    S.then(ins)
            ins.then_inc(mod_ready, 1)
            normed(3, ctx_x, 2)
            sec.ready(dve, "tc3")
            normed(3, x, 0)
            for j in range(MH):
                sec.arrived(dve, f"xm{j}")
                if j >= 2:
                    dve.wait_ge(act_ready, j - 1)
                for w in range(3):
                    c, shifted = prm2[:, C2_CONV + 4 * w + j:C2_CONV + 4 * w + j + 1], xmp[:, j, :, w:w + CTX]
                    if w == 0:
                        S.then(dve.tensor_scalar(pre[:, j % 2], shifted, c, None, ALU.mult))
                    else:
                        ins = dve.scalar_tensor_tensor(pre[:, j % 2], shifted, c, pre[:, j % 2], ALU.mult, ALU.add)
                        if w == 1:
                            S.then(ins)
                ins.then_inc(pre_ready, 1)
            for t in range(NT):
                copy(f"u{t}", u_rows[:, t, :], to(f"u{t}")[:, :])
            dve.wait_ge(zeros_ready, 3)
            for c in range(4):
                copy(f"vt{c}", vtok[:, c, :, 0:DH], to(f"vt{c}")[:, :].rearrange("p (h d) -> p h d", h=MH))
            for j in range(MH):
                n = 3 * j + 2
                copy(f"qkv{n}", qkvT[:, 2, j, :], to(f"qkv{n}")[:, :])
            sec.arrived(dve, "gates")
            S.then(dve.tensor_scalar(gf[0:ROWS, :], gf[0:ROWS, :], prm2[0:ROWS, C2_FG:C2_FG + 1], None, ALU.add))
            dve.scalar_tensor_tensor(gx[0:ROWS, :], gf[0:ROWS, :], -1.0, gf[0:ROWS, :], ALU.mult, ALU.min).then_inc(f_abs, 1)
            dve.wait_ge(f_log, 2)
            S.then(dve.scalar_tensor_tensor(gf[0:ROWS, :], gf[0:ROWS, :], 0.0, gx[0:ROWS, :], ALU.min, ALU.subtract))

            def scan(dst, src, op, start):
                S.did(dve.tensor_tensor_scan(dst[0:MH, :], src[0:MH, :], src[0:MH, :], start, op, ALU.bypass))
                b = slice(32, 32 + MH)
                S.then(dve.tensor_tensor_scan(dst[b, CTX - 1::-1], src[b, CTX - 1::-1], src[b, CTX - 1::-1], start, op, ALU.bypass))
                S.then(dve.tensor_tensor_scan(dst[b, S2 - 1:CTX - 1:-1], src[b, S2 - 1:CTX - 1:-1], src[b, S2 - 1:CTX - 1:-1],
                                              dst[b, 0:1], op, ALU.bypass))

            dve.wait_ge(zeros_ready, 4)
            scan(cum, gf, ALU.add, 0.0)
            S.then(dve.tensor_tensor(rr[0:ROWS, :], gi[0:ROWS, :], cum[0:ROWS, :], ALU.subtract))
            scan(rmax, rr, ALU.max, TAKEN)
            dve.tensor_tensor(cum[0:ROWS, CTX:S2], cum[0:ROWS, CTX:S2], rmax[0:ROWS, CTX:S2], ALU.add).then_inc(scan_ready, 1)
            for p in range(2):
                copy(f"ff{p}", fT[:, 2 * p:2 * p + 2, :], to(f"ff{p}")[:, :].rearrange("p (g t) -> p g t", g=2))

            def weigh(h):
                dve.wait_ge(e_masked, 4 * h + 4)
                for d in range(2):
                    for n, job in enumerate((f"qk{h}a", f"qk{h}b")):
                        if d == 0:
                            sec.ready(dve, job)
                        part = E[:, h % 2, d, 2 * n:2 * n + 2, :]
                        ins = dve.scalar_tensor_tensor(part.rearrange("p c t -> p (c t)"), to(job)[:, :], DH ** -0.5,
                                                       part.rearrange("p c t -> p (c t)"), ALU.mult, ALU.mult)
                        if d == 1:
                            sec.moved(ins, job)
                        elif n == 1:
                            ins.then_inc(s_ready, 1)

            def combine(h):
                for d in range(2):
                    job = f"o{h}{d}"
                    sec.ready(dve, job)
                    o = to(job)[:, 0:2 * (DH + 1)].rearrange("p (t c) -> p t c", t=NT)
                    S.then(dve.tensor_tensor(nq, o[:, :, DH], emn[:, :, 32 * d + h], ALU.max))
                    S.then(dve.scalar_tensor_tensor(nq, o[:, :, DH], -1.0, nq, ALU.mult, ALU.max))
                    S.then(dve.reciprocal(rq2, nq))
                    for t in range(NT):
                        dst = h_rows[:, t, h * DH:(h + 1) * DH]
                        if d == 0:
                            ins = dve.tensor_scalar(dst, o[:, t, 0:DH], rq2[:, t:t + 1], None, ALU.mult)
                        else:
                            ins = dve.scalar_tensor_tensor(dst, o[:, t, 0:DH], rq2[:, t:t + 1], dst, ALU.mult, ALU.add)
                    sec.moved(ins, job)
                    sec.arrived(dve, job)

            sec.arrived(dve, "rT")
            weigh(0)
            for h in range(MH):
                if h + 1 < MH:
                    weigh(h + 1)
                combine(h)
            for n in range(8):
                t, h = n // MH, n % MH
                S.then(dve.bn_stats(bst[:, n, :], h_rows[:, t, h * DH:(h + 1) * DH]))
                ins = dve.bn_aggr(bag[:, n, :], bst[:, n, :])
            ins.then_inc(h_var, 1)
            dve.wait_ge(h_rstd, 1)
            for n in range(8):
                t, h = n // MH, n % MH
                part = h_rows[:, t, h * DH:(h + 1) * DH]
                ins = dve.tensor_scalar(part, part, bag[:, n, 0:1], rstd[:, n:n + 1], ALU.subtract, ALU.mult)
            ins.then_inc(hn_ready, 1)
            for h in range(MH):
                sec.arrived(dve, f"hT{h // 2}")
                S.then(dve.scalar_tensor_tensor(hm[:, h, :], actT[:, h, CTX:S2], prm2[:, C2_SKIP + h:C2_SKIP + h + 1], hm[:, h, :],
                                                ALU.mult, ALU.add))
                dve.tensor_tensor(yT[:, h, :], hm[:, h, :], szT[:, h, :], ALU.mult).then_inc(y_ready, 1)

            def gated_add(name, count, q, done):
                dve.wait_ge(rstd_ready, 2 * DEPTH + count)
                for n in range(4):
                    t, c = n // 2, slice((n % 2) * 512, (n % 2 + 1) * 512)
                    sec.moved(dve.scalar_tensor_tensor(tmp[:, n, :], bank[n][:, :], rstd[:, t:t + 1], gb[:, q, c], ALU.mult, ALU.mult),
                              f"{name}{n}")
                for n in range(4):
                    t, c = n // 2, slice((n % 2) * 512, (n % 2 + 1) * 512)
                    sec.arrived(dve, f"{name}{n}")
                    ins = dve.tensor_tensor(x[:, t, c], x[:, t, c], tmp[:, n, :], ALU.add)
                    if done is out_ready or n % 2:
                        ins.then_inc(done, 1)

            gated_add("wo", 4, 0, x_ready)
            normed(5, x, 0)
            dve.wait_ge(router_in, 32)
            for t in range(NT):
                sec.ready(dve, f"rt{t}")
                ins = dve.tensor_tensor(logit[:, t, :], to(f"rt{t}")[:, 0:NG + NE], b_rt, ALU.add)
                sec.moved(ins, f"rt{t}")
            for t in range(NT):
                sec.arrived(dve, f"rt{t}")

            def over(v, n):
                return v.unsqueeze(2).to_broadcast([P, NT, n])

            def first_max(dst, best, src, n):
                rank = const[:, K_RANK + NE - n:K_RANK + NE].unsqueeze(1).to_broadcast([P, NT, n])
                S.then(dve.tensor_reduce(best, src, AX.X, ALU.max))
                S.then(dve.tensor_tensor(dst, src, over(best, n), ALU.is_equal))
                S.then(dve.tensor_tensor(dst, dst, rank, ALU.mult))
                S.then(dve.tensor_reduce(t4, dst, AX.X, ALU.max))
                S.then(dve.tensor_tensor(dst, dst, over(t4, n), ALU.is_equal))

            first_max(gsel, t1, logit[:, :, 0:NG], NG)
            dve.tensor_tensor(gd, logit[:, :, 0:NG], over(t1, NG), ALU.subtract).then_inc(g_diff, 1)
            el = expert_l[:, :, 0:NE]
            by_group = "p t (g e) -> p t g e"
            for t in range(NT):
                S.then(dve.tensor_tensor(el[:, t].rearrange("p (g e) -> p g e", g=NG),
                                         logit[:, t, NG:].rearrange("p (g e) -> p g e", g=NG),
                                         gsel[:, t].unsqueeze(2).to_broadcast([P, NG, EPG]), ALU.mult))
            S.then(dve.tensor_scalar(gsel, gsel, 1.0, -NEG, ALU.subtract, ALU.mult))
            for t in range(NT):
                S.then(dve.tensor_tensor(el[:, t].rearrange("p (g e) -> p g e", g=NG), el[:, t].rearrange("p (g e) -> p g e", g=NG),
                                         gsel[:, t].unsqueeze(2).to_broadcast([P, NG, EPG]), ALU.add))
            p1, p2 = pick1[:, :, 0:NE], pick2[:, :, 0:NE]
            first_max(p1, t1, el, NE)
            S.then(dve.scalar_tensor_tensor(el, p1, 2 * NEG, el, ALU.mult, ALU.add))
            first_max(p2, t2, el, NE)
            dve.tensor_tensor(t3, t2, t1, ALU.subtract).then_inc(e_diff, 1)
            dve.wait_ge(g_exp, 1)
            dve.wait_ge(e_diff, 1)
            S.then(dve.tensor_reduce(t1, ge, AX.X, ALU.add))
            S.then(dve.reciprocal(t1, t1))
            dve.wait_ge(e_exp, 1)
            S.then(dve.tensor_scalar(t2, t3, 1.0, None, ALU.add))
            S.then(dve.reciprocal(t2, t2))
            S.then(dve.tensor_tensor(t1, t1, t2, ALU.mult))
            S.then(dve.tensor_tensor(t2, t3, t1, ALU.mult))
            S.then(dve.tensor_tensor(p1, p1, over(t1, NE), ALU.mult))
            S.then(dve.tensor_tensor(p2, p2, over(t2, NE), ALU.mult))
            dve.tensor_tensor(comb, p1, p2, ALU.add).then_inc(comb_ready, 1)
            copy("cT", combT[0:NE, :], to("cT")[0:NE, 0:T])
            for n in range(NE // 2):
                sec.arrived(dve, f"cb{n}")
            with dve.Fori(0, NE) as e:
                for j in range(4):
                    dve.wait_ge(silu_ready, 2 * NFB * DEPTH + 4 * e + j + 1)
                    dve.tensor_tensor(sgE[:, j % 2, :], sgE[:, j % 2, :], cb[:, bass.ds(e, 1), :].rearrange("p a t -> p (a t)"),
                                      ALU.mult).then_inc(weighed, 1)
                    dve.wait_ge(weighed, 4 * e + j + 1)
                    sec.moved(dve.tensor_tensor(aE[:, j % 2, :], sgE[:, j % 2, :], to(f"eg{j % 2}")[:, T:2 * T], ALU.mult),
                              f"eg{j % 2}")
            gated_add("ye", 6, 1, out_ready)

        @block.gpsimd
        def _(pool):
            for n in range(8):
                pool.sem_inc(drained[n], 1)
            pool.sem_inc(block_used[1], 1)
            pool.wait_ge(half_ready, 1)
            pool.wait_ge(const_in, 16)

            def root(S, dst, src, n, scale, eps, ready):
                v = ms[:, dst:dst + n]
                settle(pool, passed)
                if scale is None:
                    S.then(pool.tensor_scalar(v, src, eps, None, ALU.add))
                else:
                    S.then(pool.tensor_scalar(v, src, scale, eps, ALU.mult, ALU.add))
                pool.tensor_tensor(rstd[:, dst:dst + n], v, half[:, 0:n], ALU.pow).then_inc(ready, 1)

            with pool.Fori(0, DEPTH) as l:
                res = layer_results(l)
                S = Steps(pool, pool_step, l * POOL_STEPS)
                pool.wait_ge(ss_ready, 4 * l + 2)
                root(S, 0, ss[:, 0:2], 2, 1.0 / D, EPS, rstd_ready)
                pool.wait_ge(prm_in, 48 * l + 48)
                settle(pool, passed)
                pool.affine_select(out=wsT, in_=wsT, pattern=[[0, H], [1, P]], compare_op=ALU.is_ge, fill=0.0, base=0,
                                   channel_multiplier=-1).then_inc(ws_ready, 1)
                for t in range(NT):
                    res.arrived(pool, f"qk{t}")
                    z8 = zq[:, t, :].rearrange("p (h d) -> p h d", h=8)
                    hd = HD // 2
                    S.did(pool.tensor_tensor(ga, z8, cos2[:, t, :].unsqueeze(1).to_broadcast([P, 8, HD]), ALU.mult))
                    S.did(pool.tensor_tensor(gc[:, :, 0:hd], z8[:, :, hd:HD],
                                             sin2[:, t, 0:hd].unsqueeze(1).to_broadcast([P, 8, hd]), ALU.mult))
                    S.then(pool.tensor_tensor(gc[:, :, hd:HD], z8[:, :, 0:hd],
                                              sin2[:, t, hd:HD].unsqueeze(1).to_broadcast([P, 8, hd]), ALU.mult))
                    pool.tensor_tensor(rq[:, t], ga, gc, ALU.add).then_inc(rq_ready, 1)
                    pool.wait_ge(rq_ready, 2 * l + t + 1)
                for t in range(NT):
                    pool.wait_ge(score_ready, 2 * l + t + 1)
                    settle(pool, passed)
                    part = score[t][:, t * P:(t + 1) * P]
                    pool.affine_select(out=part, in_=part, pattern=[[-1, P]], compare_op=ALU.is_ge, fill=NEG, base=0,
                                       channel_multiplier=1).then_inc(score_masked, 1)
                for t in range(NT):
                    pool.wait_ge(sel_ready, 2 * l + t + 1)
                    settle(pool, passed)
                    part = sel[t][:, t * P:(t + 1) * P]
                    pool.affine_select(out=part, in_=part, pattern=[[-1, P]], compare_op=ALU.is_ge, fill=-1.0, base=0,
                                       channel_multiplier=1).then_inc(sel_masked, 1)
                pool.wait_ge(var_ready, l + 1)
                root(S, 2, bnag[:, :, 1], 4, None, LN_EPS, norm_rstd)
                for t in range(NT):
                    pool.wait_ge(v_norm, 2 * l + t + 1)
                    v = zg[:, t, G:2 * G]
                    S.then(pool.tensor_tensor(v, v, lnrow[:, 0, :], ALU.mult))
                    pool.tensor_tensor(v, v, lnrow[:, 1, :], ALU.add).then_inc(v_ready, 1)
                pool.wait_ge(ss_ready, 4 * l + 4)
                root(S, 0, ss[:, 0:2], 2, 1.0 / D, EPS, rstd_ready)
                assert S.n == POOL_STEPS, S.n

            S = Steps(pool, pool_step, DEPTH * POOL_STEPS)
            N = 4 * DEPTH
            pool.wait_ge(ss_ready, N + 2)
            root(S, 0, ss[:, 0:2], 2, 1.0 / D, EPS, rstd_ready)
            pool.wait_ge(x_ready, 2)
            S.then(pool.memset(xmp[:, :, :, 0:1], 0.0))
            pool.memset(xmp[:, :, :, CTX + 1:CTX + 2], 0.0).then_inc(zeros_ready, 1)
            pool.wait_ge(ss_ready, N + 4)
            root(S, 2, ss[:, 2:4], 2, 1.0 / D, EPS, rstd_ready)
            pool.wait_ge(ss_ready, N + 6)
            root(S, 0, ss[:, 0:2], 2, 1.0 / D, EPS, rstd_ready)
            sec.arrived(pool, "gate3")
            S.then(pool.memset(cum[0:ROWS, :], 0.0))
            S.then(pool.memset(rmax[0:ROWS, :], 0.0))
            sec.ready(pool, "u1")
            S.then(pool.memset(E[:, :, 0, 3, 0:P], 0.0))
            pool.memset(E[:, :, 1, 2, P:T], 0.0).then_inc(zeros_ready, 1)
            pool.memset(vtok[:, :, :, DH:DH + 1], 1.0).then_inc(zeros_ready, 1)
            S.then(pool.memset(nq, 0.0))
            pool.memset(rq2, 0.0).then_inc(zeros_ready, 1)
            for h in range(MH):
                sec.arrived(pool, f"rb{h}")
                for d in range(2):
                    for c in (2, 3):
                        part = E[:, h % 2, d, c, (c - 2) * P:(c - 1) * P]
                        s = 1 if d == 0 else -1
                        pool.affine_select(out=part, in_=part, pattern=[[s, P]], compare_op=ALU.is_ge, fill=0.0, base=0,
                                           channel_multiplier=-s).then_inc(e_masked, 1)
            pool.wait_ge(h_var, 1)
            root(S, 0, bag[:, :, 1], 8, None, EPS, h_rstd)

            def result_root(count):
                pool.wait_ge(ss_ready, N + count)
                halves = ss[:, 0:4].rearrange("p (t c) -> p t c", t=NT)
                S.then(pool.tensor_tensor(ms[:, 6:8], halves[:, :, 0], halves[:, :, 1], ALU.add))
                root(S, 0, ms[:, 6:8], 2, 1.0 / D, EPS, rstd_ready)

            result_root(10)
            pool.wait_ge(ss_ready, N + 12)
            root(S, 0, ss[:, 0:2], 2, 1.0 / D, EPS, rstd_ready)
            result_root(16)


def constants():
    c = np.zeros((P, N_CONST), np.float64)
    c[:, K_ID:K_ID + P] = np.eye(P)
    angle = np.arange(T, dtype=np.float32)[:, None] * (np.float32(ROPE_THETA) ** (-np.arange(0, HD, 2, dtype=np.float32) / HD))
    angle = angle.astype(np.float32).astype(np.float64).reshape(NT, P, HD // 2).transpose(1, 0, 2)
    cos, sin = np.cos(angle), np.sin(angle)
    c[:, K_COS:K_COS + 2 * HD] = np.concatenate([cos, cos], -1).reshape(P, -1)
    c[:, K_SIN:K_SIN + 2 * HD] = np.concatenate([-sin, sin], -1).reshape(P, -1)
    w = 2 * np.pi * (np.outer(np.arange(P), np.arange(P)) % P) / P
    c[:, K_CC:K_CC + P] = np.cos(w) / P ** 0.5
    c[:, K_SC:K_SC + P] = -np.sin(w) / P ** 0.5
    w = 2 * np.pi * (np.outer(np.arange(T), np.arange(T)) % T) / T
    w = np.concatenate([np.cos(w), np.sin(w)], 1) / T ** 0.5
    c[:, K_DFT:K_RANK] = w.reshape(NT, P, 2 * T).transpose(1, 0, 2).reshape(P, -1)
    c[:, K_RANK:] = np.arange(NE, 0, -1)
    quarter = D // 4
    freq = (1.0 / (np.float32(POS_BASE) ** (np.arange(quarter, dtype=np.float32) / np.float32(quarter)))).astype(np.float32)

    def table(n):
        v = (np.arange(n, dtype=np.float32)[:, None] * freq).astype(np.float64)
        return np.concatenate([np.sin(v), np.cos(v)], -1)

    rows = T // GRID_W
    pos = np.concatenate([np.repeat(table(rows), GRID_W, 0), np.tile(table(GRID_W), (rows, 1))], -1)
    return c.astype(np.float32), by_partition(pos.astype(np.float32))


def by_partition(w):
    *lead, k, n = w.shape
    w = w.reshape(*lead, k // P, P, n)
    return np.ascontiguousarray(np.moveaxis(w, -3, -2)).reshape(*lead, P, k // P * n)


def columns(*vectors):
    return np.concatenate([np.swapaxes(v.reshape(-1, P), 0, 1) for v in vectors], 1)


def layouts(i):
    cuts = np.cumsum([256] * 9 + [64, 4, 256, 256])[:-1]
    ab, ac, ah, gu, gv, q, k, v, qi, ki, wi, da, dg = np.split(i["w_in"], cuts, axis=2)
    groups = {"vqi": (v, qi), "kwi": (ki, wi), "dadg": (da, dg), "qk": (q, k), "guv": (gu, gv), "abac": (ab, ac), "ah": (ah,)}
    a = {}
    a["x"] = i["x"][0]
    a["w_in"] = np.concatenate([by_partition(np.concatenate(groups[n], 2)) for n in IN_COLS], 2)
    a["prm"] = np.stack([np.concatenate([
        columns(i["g_mix"][l], i["g_ffn"][l], i["w_conv_a"][l], i["w_conf"][l], i["b_conf"][l], i["conf_ln_g"][l],
                i["conf_ln_b"][l]), i["b_s"][l].T], 1) for l in range(DEPTH)])
    a["gmlp_ln"] = np.concatenate([i["gmlp_ln_g"], i["gmlp_ln_b"]], 1)
    a["w_s"] = i["w_s"].transpose(0, 3, 1, 2).reshape(DEPTH, P, H * P)
    a["w_out"] = by_partition(i["w_out"])

    def in_blocks(w, n):
        *lead, k, c = w.shape
        return by_partition(np.moveaxis(w.reshape(*lead, k, c // n, n), -2, -3))

    a["ffn"] = np.concatenate([in_blocks(i["w_gate"], FB), in_blocks(i["w_up"], FB),
                               by_partition(i["w_down"].reshape(DEPTH, NFB, FB, D))], 3)
    a["g_final"] = i["g_final"]
    pad = np.zeros((P, 2), np.float32)
    for d, name in enumerate(("b_if_fwd_2", "b_if_bwd_2")):
        for q in range(2):
            pad[32 * d:32 * d + MH, q] = i[name][0, q * MH:(q + 1) * MH]
    a["prm2"] = np.concatenate([columns(i["g_pre_mix_2"], i["g_pre_ffn_2"], i["conv_w_2"], i["conv_b_2"], i["mlstm_norm_w_2"],
                                        i["mlstm_skip_2"], i["c_2"], i["c_ctx_2"]), pad], 1)
    a["w_ada"] = in_blocks(i["w_ada_2"][0], 512).reshape(3, 4, P, 4096)
    a["b_ada"] = i["b_ada_2"][0]
    a["g_post"] = np.concatenate([i["g_post_mix_2"][0], i["g_post_ffn_2"][0]])
    a["ctx"] = i["ctx_2"][0]
    a["w_in_2"] = in_blocks(i["w_in_2"][0], 512)
    n = P // 4
    bd = np.zeros((3, MH, n, 4, n, 4), np.float32)
    for q, name in enumerate(("w_q_2", "w_k_2", "w_v_2")):
        for b in range(n):
            bd[q, :, b, :, b, :] = i[name][0].reshape(MH, n, 4, 4)[:, b]
    w_if = np.zeros((12, P, P), np.float32)
    for d, name in enumerate(("w_if_fwd_2", "w_if_bwd_2")):
        for q in range(2):
            w_if[:, :, 64 * q + 32 * d:64 * q + 32 * d + MH] = i[name][0].reshape(12, P, 2, MH)[:, :, q]
    a["heads_2"] = np.concatenate([bd.reshape(12, P, P), w_if, i["w_fourier_2"][0]]).transpose(1, 0, 2).reshape(P, -1)
    a["w_out_2"] = by_partition(i["w_out_2"][0])
    a["w_router"] = by_partition(np.concatenate([i["w_router_group_2"][0], i["w_router_expert_2"][0]], 1))
    a["b_router"] = np.concatenate([i["b_router_group_2"][0], i["b_router_expert_2"][0]])
    a["experts"] = np.concatenate([by_partition(i["w_gate_2"][0]), by_partition(i["w_up_2"][0]), by_partition(i["w_down_2"][0])], 2)
    a["const"], a["pos"] = constants()
    return {f"in_{k}": np.ascontiguousarray(v) for k, v in a.items()}


def kernel(**inputs):
    import concourse.bacc as bacc
    from concourse.bass_utils import run_bass_kernel_spmd

    arrays = layouts({k: np.asarray(v) for k, v in inputs.items()})
    nc = bacc.Bacc("TRN2", target_bir_lowering=False, num_devices=1)
    args = {n[3:]: nc.dram_tensor(n, v.shape, F32, kind="ExternalInput").ap() for n, v in arrays.items()}
    out = nc.dram_tensor("out", (T, D), F32, kind="ExternalOutput").ap()
    build(nc, args, out)
    return run_bass_kernel_spmd(nc, [arrays], core_ids=[0]).results[0]["out"].reshape(1, T, D)
```

```python
from contextlib import ExitStack

import numpy as np

import concourse.bass as bass
from concourse import mybir

F32, F32R, I32 = mybir.dt.float32, mybir.dt.float32r, mybir.dt.int32
ALU = mybir.AluOpType
ACT = mybir.ActivationFunctionType
AX = mybir.AxisListType

P = 128
T = 256
NT = T // P
D = 1024
KD = D // P
DEPTH = 2
G = 256
H = 4
HD = G // H
TOPK = 64
SHORT, LONG = 3, 31
FFN = 2816
FB = 256
NFB = FFN // FB
NEG = -1e30
TAKEN = -3e38
EPS, LN_EPS = 1e-6, 1e-5

CTX = 256
S2 = CTX + T
MW = 512
MH = 4
DH = MW // MH
NMOD = 6
NE, EPG, NG = 16, 4, 4
DE = 512
QUAD = 4
OVER = QUAD
NPASS = NE + OVER
GRID_W, POS_BASE, ROPE_THETA = 64, 10000.0, 10000.0

C_GMIX, C_GFFN, C_SHORT = 0, KD, 2 * KD
C_LONG = C_SHORT + 2 * SHORT
C_BCONF = C_LONG + 2 * LONG
C_LNG, C_LNB, C_BS = C_BCONF + 2, C_BCONF + 4, C_BCONF + 6
N_PRM = C_BS + H
C2_PREMIX, C2_PREFFN, C2_CONV = 0, KD, 2 * KD
C2_CONVB = C2_CONV + 3 * MH
C2_NORM, C2_SKIP, C2_C = C2_CONVB + MH, C2_CONVB + 2 * MH, C2_CONVB + 3 * MH
C2_IG, C2_FG = C2_C + 2 * KD, C2_C + 2 * KD + 1
N_PRM2 = C2_FG + 1
ROWS = 32 + MH
K_ID, K_COS, K_SIN = 0, P, P + 2 * HD
K_CC = K_SIN + 2 * HD
K_SC = K_CC + P
K_DFT = K_SC + P
K_RANK = K_DFT + NT * 2 * T
K_SLOT = K_RANK + NE
K_BEFORE = K_SLOT + P
K_ONES = K_BEFORE + P
N_CONST = K_ONES + P

IN_COLS = {"vqi": 512, "kwi": 68, "dadg": 512, "qk": 512, "guv": 512, "abac": 512, "ah": 256}
IN_AT = dict(zip(IN_COLS, np.cumsum([0] + [KD * w for w in IN_COLS.values()])[:-1].tolist()))
N_IN = KD * sum(IN_COLS.values())
BLOCK = 3 * KD * FB
GU = 2 * KD * FB
SUBS, SUB = 6, BLOCK // 6
EXPERT = 3 * 4096

IN_SUBS = 18
DVE_STEPS, POOL_STEPS = 123, 14
N_SCRATCH = 13400


class Banks:

    def __init__(self):
        self.count, self.at = [0] * 8, {}

    def add(self, bank, *names, times=1):
        for name in names:
            self.at[name] = (bank, self.count[bank])
            self.count[bank] += times


def layer_banks():
    b = Banks()
    for bank, name in [
        (0, "tx1_00"), (1, "tx1_01"), (2, "tx1_10"), (3, "tx1_11"), (4, "vqi0"), (5, "vqi1"), (6, "kwi0"),
        (7, "kwi1"), (0, "da"), (1, "dg"), (2, "riT0"), (3, "riT1"), (4, "qk0"), (5, "qk1"), (2, "sc0a"),
        (0, "sc0b"), (3, "sc1a"), (6, "sc1b"), (7, "guv0"), (6, "guv1"), (0, "cvT"), (1, "ab"), (4, "ac"), (5, "ah"),
        (2, "rqT0"), (3, "rqT1"), (6, "mix0"), (7, "mix1"), (4, "lg0a"), (2, "lg0b"), (5, "lg1a"), (6, "lg1b"), (0, "ybT"),
        (7, "cnT"), (0, "wo0"), (1, "wo1"), (2, "wo2"), (3, "wo3"), (7, "pT0"), (4, "pT1a"), (5, "pT1b"),
        (6, "av0"), (7, "av1"), (4, "ycT"), (4, "tx2_00"), (5, "tx2_01"), (6, "tx2_10"), (7, "tx2_11"),
    ]:
        b.add(bank, name)
    b.add(4, "gu0", times=NFB)
    b.add(5, "gu1", times=NFB)
    for n in range(4):
        b.add(n, f"y{n}")
    return b


def second_banks():
    b = Banks()
    for s in range(4):
        b.add(s, f"ada{s}", times=3)
    b.add(4, "modT")
    for s in range(4):
        b.add(s, f"gate{s}")
    for n in range(4):
        b.add(4 + n, f"tc{n}")
    for n in range(4):
        b.add(n, f"tl{n}")
    for j in range(4):
        b.add(4 + j, f"xm{j}")
    b.add(0, "z0")
    b.add(1, "z1")
    for n in range(4):
        b.add(n, f"vt{n}")
    for n in range(12):
        b.add(4 + n % 4, f"qkv{n}")
    b.add(4, "gates")
    b.add(2, "u0")
    b.add(3, "u1")
    for g in range(4):
        b.add(g, f"fp{g}")
    b.add(6, "ff0")
    b.add(7, "ff1")
    b.add(6, "fy0")
    b.add(7, "fy1")
    b.add(5, "rT")
    for h in range(MH):
        b.add(6 + h % 2, f"rb{h}")
        b.add(2 * (h % 2), f"qk{h}a")
        b.add(2 * (h % 2) + 1, f"qk{h}b")
        b.add(4, f"o{h}0")
        b.add(5, f"o{h}1")
    for n in range(4):
        b.add(n, f"wo{n}")
    b.add(6, "hT0")
    b.add(7, "hT1")
    for n in range(4):
        b.add(4 + n, f"t2{n}")
    b.add(0, "rt0")
    b.add(1, "rt1")
    b.add(2, "rank")
    for n in range(4):
        b.add(4 + n, f"first{n}")
    b.add(6, "first_sT0")
    b.add(7, "first_sT1")
    b.add(4, "eG")
    b.add(4, "eD0", times=2 * NPASS - 1)
    b.add(5, "eU")
    b.add(5, "eD1", times=2 * NPASS - 1)
    b.add(6, "e6", times=6 * NPASS // QUAD)
    b.add(7, "e7", times=10 * NPASS // QUAD)
    for n in range(4):
        b.add(n, f"ye{n}")
    return b



LAY, SEC = layer_banks(), second_banks()


class Results:

    def __init__(self, filled, drained, plan, base):
        self.filled, self.drained, self.plan, self.base = filled, drained, plan, base

    def index(self, name, i):
        bank, n = self.plan.at[name]
        return bank, self.base[bank] + n + i

    def room(self, eng, name, i=0):
        bank, n = self.index(name, i)
        eng.wait_ge(self.drained[bank], n + 1)

    def done(self, ins, name):
        ins.then_inc(self.filled[self.plan.at[name][0]], 1)

    def ready(self, eng, name, i=0):
        bank, n = self.index(name, i)
        eng.wait_ge(self.filled[bank], n + 1)

    def moved(self, ins, name):
        ins.then_inc(self.drained[self.plan.at[name][0]], 1)

    def arrived(self, eng, name, i=0):
        bank, n = self.index(name, i)
        eng.wait_ge(self.drained[bank], n + 2)


HIDDEN_T, CHOSEN_T6 = (0, 1, 3, 4), {1: 2, 3: 5}
PIECES, CHOSEN_T7 = ((0, 1), (2, 3), (5, 6), (7, 8)), {1: 4, 3: 9}


def f32(ap):
    return ap.bitcast(F32)


def settle(eng, passed):
    eng.sem_inc(passed, 1)


class Steps:

    def __init__(self, eng, sem, base):
        self.eng, self.sem, self.base, self.n = eng, sem, base, 0

    def did(self, ins):
        self.n += 1
        ins.then_inc(self.sem, 1)
        return self.n

    def need(self, n):
        self.eng.wait_ge(self.sem, self.base + n)

    def then(self, ins):
        self.need(self.did(ins))



def build(nc, a, out):
    ctx = ExitStack()
    with ctx:
        placed = {}

        def sb(name, shape):
            placed[name] = -(-nc.sbuf_base // 32) * 32
            return ctx.enter_context(nc.sbuf_tensor(name, shape, F32))

        def rounded_place(name, of, at, *shape):
            return nc.alloc_sbuf_tensor_at(name, [P, *shape], F32R, offset=placed[of] + 4 * at)

        def sem(name):
            return ctx.enter_context(nc.semaphore(name))

        bank = [ctx.enter_context(nc.psum_tensor(f"bank{n}", [P, 512], F32)) for n in range(8)]

        blocks_w = sb("blocks_w", [P, 2, BLOCK])
        m = sb("m", [P, 4, 4096])
        kwi_w = sb("kwi_w", [P, KD, 68])
        const = sb("const", [P, N_CONST])
        prm = sb("prm", [P, N_PRM])
        prm2 = sb("prm2", [P, N_PRM2])
        x = sb("x", [P, NT, D])
        hT = sb("hT", [P, KD, T])
        hC = sb("hC", [P, KD, T])
        yT = sb("yT", [P, KD, T])
        ss = sb("ss", [P, 4])
        ms = sb("ms", [P, 8])
        rstd = sb("rstd", [P, 8])
        table_i = ctx.enter_context(nc.sbuf_tensor("table_i", [P, QUAD + 1], I32))
        half = sb("half", [P, 8])
        scratch = sb("scratch", [P, N_SCRATCH])

        class Region:

            def __init__(self, mem, size, at=0):
                self.mem, self.size, self.at = mem, size, at

            def take(self, *shape):
                n = int(np.prod(shape))
                v = self.mem[:, self.at:self.at + n]
                self.at += n
                assert self.at <= self.size, (self.at, self.size)
                names = "abcd"[:len(shape)]
                if len(shape) == 1:
                    return v
                return v.rearrange(f"p ({' '.join(names)}) -> p {' '.join(names)}",
                                   **{k: s for k, s in zip(names[1:], shape[1:])})

        ident = const[:, K_ID:K_ID + P]
        cos2 = const[:, K_COS:K_COS + 2 * HD].rearrange("p (t d) -> p t d", t=NT)
        sin2 = const[:, K_SIN:K_SIN + 2 * HD].rearrange("p (t d) -> p t d", t=NT)
        ccos = const[:, K_CC:K_CC + P]
        nsin = const[:, K_SC:K_SC + P]
        dft = const[:, K_DFT:K_RANK].rearrange("p (t c) -> p t c", t=NT)

        lay = Region(scratch, 2 * BLOCK)
        xn = lay.take(NT, D)
        keep = Region(scratch, N_SCRATCH, 2 * BLOCK)
        lnrow = keep.take(2, G)
        wsT = keep.take(H, P)
        zi_at = lay.at
        zi = lay.take(NT, 320)
        wi = lay.take(NT, H)
        va = lay.take(NT, G)
        ra, rb = lay.take(5, HD), lay.take(5, HD)
        ga, gc = lay.take(8, HD), lay.take(8, HD)
        ri = lay.take(NT, 6, HD)
        riT = lay.take(3, T)
        rqT = lay.take(4, T)
        rel_at = lay.at
        rel = [lay.take(H, P), lay.take(H, T)]
        score = [lay.take(P), lay.take(T)]
        work = [lay.take(P), lay.take(T)]
        sel = [lay.take(P), lay.take(T)]
        mx = lay.take(NT, 8)
        cpad = lay.take(2, LONG - 1 + T)
        conv = lay.take(2, T)
        ycat = lay.take(NT, 2, G)
        nmx, nms, rsum, rinv = (lay.take(NT, H) for _ in range(4))
        bnst, bnag = keep.take(4, 6), keep.take(4, 2)
        again = Region(scratch, N_SCRATCH, rel_at)
        lg = [again.take(H, P), again.take(H, T)]
        chp = Region(scratch, N_SCRATCH, zi_at).take(2, SHORT - 1 + T)
        conv_n = conv
        rq = xn[:, :, 0:512].rearrange("p t (h d) -> p t h d", h=8)
        acs, sig = xn[:, :, 512:768], xn[:, :, 768:1024]
        chy = sig
        zz = hC[:, :, :].rearrange("p k t -> p (k t)")
        zq = zz[:, 0:1024].rearrange("p (t c) -> p t c", t=NT)
        zg = zz[:, 1024:2048].rearrange("p (t c) -> p t c", t=NT)
        pT0 = zz[:, 0:512].rearrange("p (h q) -> p h q", h=H)
        pT1 = zz[:, 1024:2048].rearrange("p (s h q) -> p s h q", s=2, h=H)
        h1_h, h1_l = rounded_place("h1_h", "yT", 0, KD, T), rounded_place("h1_l", "hT", 0, KD, T)
        y_h, y_l = rounded_place("y_h", "hT", 0, KD, T), rounded_place("y_l", "yT", 0, KD, T)
        w_l = rounded_place("w_l", "m", 0, 4, 4096)
        fw_h = rounded_place("fw_h", "scratch", 0, 2, BLOCK)
        fw_l = rounded_place("fw_l", "blocks_w", 0, 2, BLOCK)
        h_h, h_l = rounded_place("h_h", "hT", 0, KD, T), rounded_place("h_l", "hC", 0, KD, T)
        h_full = hC
        sga = Region(yT[:, :, :].rearrange("p k t -> p (k t)"), D).take(2, T)
        a2 = rounded_place("a2", "yT", 2 * T, 2, 2, T)

        again = Region(scratch, keep.at)
        gb = again.take(2, D)
        modc = again.take(4, KD, 2)
        cb_at = again.at
        xmp = again.take(MH, 2, CTX + 2)
        actT = again.take(MH, S2)
        ctx_at = again.at
        h_rows = again.take(NT, MW)
        pre_at = again.at
        pre = again.take(2, 2, CTX)
        xn2_at = again.at
        xn2 = again.take(NT, D)
        ft_at = again.at
        fT = again.take(4, T)
        w_rt = again.take(KD, NG + NE)
        b_rt = again.take(NG + NE)
        bst, bag = again.take(8, 6), again.take(8, 2)
        emn, rcol = again.take(NT, ROWS), again.take(4, ROWS)
        nq, rq2 = again.take(NT), again.take(NT)
        logit, expert_l, pick1, pick2 = (again.take(NT, NG + NE) for _ in range(4))
        gd, ge, gsel = (again.take(NT, NG) for _ in range(3))
        t1, t2, t3, t4 = (again.take(NT) for _ in range(4))
        chosen, comb, place = again.take(NT, NE), again.take(NT, NPASS), again.take(NT, NPASS)
        comb_at = again.at = -(-again.at // 8) * 8
        again.take(NT, NPASS)
        comb_h, comb_l = rounded_place("comb_h", "scratch", comb_at, NT, NPASS), again.take(NT, NPASS)
        over_e, over_n, over_1 = again.take(NE), again.take(NE), again.take(NE)
        over_t = again.take(NT, NE)
        table = again.take(QUAD + 1)
        pick_at = again.at = -(-again.at // 8) * 8
        again.take(QUAD, P + 4)
        pick_w = rounded_place("pick_w", "scratch", pick_at, QUAD, P + 4)
        slot_w = again.take(QUAD)
        cs = keep.take(KD, 2)
        xg = rounded_place("xg", "scratch", cb_at, 2, 2, KD, 2 * P)
        xg_full = Region(scratch, N_SCRATCH, cb_at).take(2, 2, KD, 2 * P)
        w_h = rounded_place("w_h", "blocks_w", 0, 3, 4096)
        xn_h, xn_l = rounded_place("xn_h", "hC", 0, NT, D), rounded_place("xn_l", "hT", 0, NT, D)
        choice = rounded_place("choice", "scratch", 0, 2, NT, 2 * P)
        choice_t = rounded_place("choice_t", "scratch", ft_at, QUAD, T)
        hidden = const[:, K_COS:K_COS + DE]
        aT2 = rounded_place("aT2", "const", K_COS + DE, 2, 4, P)
        y2 = rounded_place("y2", "yT", 0, 2, D)
        ctx_x = Region(scratch, N_SCRATCH, ctx_at).take(NT, D)
        tmp = Region(scratch, N_SCRATCH, ctx_at).take(4, 512)
        hm = Region(scratch, N_SCRATCH, pre_at).take(MH, T)
        h_rt = Region(scratch, N_SCRATCH, ctx_at).take(KD, T)
        ada_h = [rounded_place("ada_h0", "blocks_w", (NMOD + 2) * D, 4096), rounded_place("ada_h1", "scratch", cb_at, 4096)]
        cs_at = keep.at = -(-keep.at // 8) * 8
        keep.take(2, KD, 2)
        cs2 = rounded_place("cs2", "scratch", cs_at, 2, KD, 2)
        gfin = fT.rearrange("p a b -> p (a b)")
        fP = Region(scratch, N_SCRATCH, xn2_at).take(4, 512)
        pos = yT[:, :, :].rearrange("p k t -> p (k t)").rearrange("p (t d) -> p t d", t=NT)
        szT = hC[:, 0:4, :]
        u_rows = hC[:, 4:8, :].rearrange("p k t -> p (k t)").rearrange("p (t c) -> p t c", t=NT)
        w3 = Region(m[:, 3, :], 4096)
        bd = w3.take(3, MH, P)
        w_if = w3.take(3 * MH, P)
        w_f = w3.take(4, P)
        E = Region(m[:, 2, :], 4096).take(2, 2, 4, T)
        flat = blocks_w[:, :, :].rearrange("p s n -> p (s n)")
        modrow = flat[0:2, 0:NMOD * D]
        gpost = flat[0:2, NMOD * D:(NMOD + 2) * D]
        wide = Region(flat, 2 * BLOCK)
        qkvT = wide.take(3, MH, S2)
        vtok = wide.take(4, MH, DH + 1)
        gi, gf, gx, cum, rr, rmax = (wide.take(S2) for _ in range(6))

        filled = [sem(f"filled{n}") for n in range(8)]
        drained = [sem(f"drained{n}") for n in range(8)]
        dve_step, pool_step, passed = sem("dve_step"), sem("pool_step"), sem("passed")
        const_in, x_in, prm2_in = sem("const_in"), sem("x_in"), sem("prm2_in")
        prm_in, kwi_in, ab_in = sem("prm_in"), sem("kwi_in"), sem("ab_in")
        m_in = [sem(f"m{n}_in") for n in range(4)]
        gu_in, down_in = ([sem(f"{w}{n}_in") for n in range(2)] for w in ("gu", "down"))
        in_hi, in_lo, h1_rounded, h1_ready = sem("in_hi"), sem("in_lo"), sem("h1_rounded"), sem("h1_ready")
        out_lo = sem("out_lo")
        mix_rounded, mix_ready = sem("mix_rounded"), sem("mix_ready")
        ffn_hi, ffn_lo, h_rounded, h_ready = sem("ffn_hi"), sem("ffn_lo"), sem("h_rounded"), sem("h_ready")
        block_used = [sem(f"block{n}_used") for n in range(2)]
        half_ready = sem("half_ready")
        ss_ready, rstd_ready, xn_ready = sem("ss_ready"), sem("rstd_ready"), sem("xn_ready")
        ri_ready, rq_ready, ws_ready = sem("ri_ready"), sem("rq_ready"), sem("ws_ready")
        score_ready, score_masked = sem("score_ready"), sem("score_masked")
        sel_ready, sel_masked = sem("sel_ready"), sem("sel_masked")
        conv_ready, var_ready, norm_rstd = sem("conv_ready"), sem("var_ready"), sem("norm_rstd")
        v_norm, v_ready = sem("v_norm"), sem("v_ready")
        yb_ready, lg_ready, exp_ready, silu_ready = sem("yb_ready"), sem("lg_ready"), sem("exp_ready"), sem("silu_ready")
        rows_in, pos_in, ctx_in, heads_in, router_in = (sem("rows_in"), sem("pos_in"), sem("ctx_in"), sem("heads_in"),
                                                     sem("router_in"))
        ada_hi, ada_lo, cs_ready = sem("ada_hi"), sem("ada_lo"), sem("cs_ready")
        a_step, silu_c, mod_ready, mod_rows, gate_rows = sem("a_step"), sem("silu_c"), sem("mod_ready"), sem("mod_rows"), sem("gate_rows")
        x_ready, zeros_ready, pre_ready, act_ready = sem("x_ready"), sem("zeros_ready"), sem("pre_ready"), sem("act_ready")
        f_abs, f_log, scan_ready, e_masked, s_ready = (sem("f_abs"), sem("f_log"), sem("scan_ready"), sem("e_masked"),
                                                       sem("s_ready"))
        h_var, h_rstd, hn_ready, y_ready = sem("h_var"), sem("h_rstd"), sem("hn_ready"), sem("y_ready")
        g_diff, g_exp, e_diff, e_exp, comb_ready = (sem("g_diff"), sem("g_exp"), sem("e_diff"), sem("e_exp"),
                                                    sem("comb_ready"))
        piece_in = [sem(f"piece{n}_in") for n in range(4)]
        chosen_ready, choice_ready, table_ready = sem("chosen_ready"), sem("choice_ready"), sem("table_ready")
        hi_ready, lo_ready, xg_ready = sem("hi_ready"), sem("lo_ready"), sem("xg_ready")
        xg_moved, xg_rounded, hidden_rounded = sem("xg_moved"), sem("xg_rounded"), sem("hidden_rounded")
        slot_ready, y_rounded, y_zero = sem("slot_ready"), sem("y_rounded"), sem("y_zero")
        out_ready, out_stored = sem("out_ready"), sem("out_stored")
        block = ctx.enter_context(nc.Block())

        def layer_results(l):
            return Results(filled, drained, LAY, [l * n for n in LAY.count])

        sec = Results(filled, drained, SEC, [DEPTH * n for n in LAY.count])
        B1, B0 = NFB // 2, (NFB + 1) // 2

        @block.sync
        def _(sp):
            for t in range(NT):
                sp.dma_start(x[:, t, :], a["x"][t * P:(t + 1) * P, :]).then_inc(x_in, 16)
            sp.dma_start(const[:, :], a["const"]).then_inc(const_in, 16)
            with sp.Fori(0, DEPTH) as l:
                res = layer_results(l)

                def w_in(name):
                    return a["w_in"][bass.ds(l, 1), :, IN_AT[name]:IN_AT[name] + KD * IN_COLS[name]]\
                        .rearrange("a p n -> p (a n)")

                def ffn_part(b, lo, hi):
                    return a["ffn"][bass.ds(l, 1), bass.ds(b, 1), :, lo:hi].rearrange("a b p n -> p (a b n)")


                sp.dma_start(prm[:, :], a["prm"][bass.ds(l, 1)].rearrange("a p n -> p (a n)")).then_inc(prm_in, 16)
                sp.dma_start(lnrow.rearrange("p r n -> p (r n)"), a["gmlp_ln"][bass.ds(l, 1)]
                             .rearrange("a n -> (a n)").partition_broadcast(P)).then_inc(prm_in, 16)
                sp.dma_start(wsT.rearrange("p h n -> p (h n)"), a["w_s"][bass.ds(l, 1)]
                             .rearrange("a p n -> p (a n)")).then_inc(prm_in, 16)
                sp.dma_start(m[:, 0, :], w_in("vqi")).then_inc(m_in[0], 16)
                sp.dma_start(kwi_w[:, :, :].rearrange("p k n -> p (k n)"), w_in("kwi")).then_inc(kwi_in, 16)
                sp.dma_start(m[:, 2, :], w_in("dadg")).then_inc(m_in[2], 16)
                sp.dma_start(m[:, 1, :], w_in("qk")).then_inc(m_in[1], 16)
                sp.dma_start(m[:, 3, :], w_in("guv")).then_inc(m_in[3], 16)
                src = w_in("abac")
                sp.wait_ge(drained[3], l * LAY.count[3] + 1)
                sp.dma_start(blocks_w[:, 0, 0:4096], src).then_inc(ab_in, 16)
                sp.dma_start(blocks_w[:, 0, 4096:6144], w_in("ah")).then_inc(ab_in, 16)
                for s, job in ((0, "vqi1"), (1, "qk1")):
                    src = a["w_out"][bass.ds(l, 1), :, s * 4096:(s + 1) * 4096].rearrange("a p n -> p (a n)")
                    res.ready(sp, job)
                    sp.dma_start(m[:, s, :], src).then_inc(m_in[s], 16)
                src = ffn_part(0, 0, GU)
                res.ready(sp, "ah")
                settle(sp, passed)
                sp.dma_start(blocks_w[:, 0, 0:GU], src).then_inc(gu_in[0], 16)
                sp.dma_start(blocks_w[:, 0, GU:], ffn_part(0, GU, BLOCK)).then_inc(down_in[0], 16)
                sp.dma_start(blocks_w[:, 1, 0:GU], ffn_part(1, 0, GU)).then_inc(gu_in[1], 16)
                sp.dma_start(blocks_w[:, 1, GU:], ffn_part(1, GU, BLOCK)).then_inc(down_in[1], 16)

                def next_block(b, slot, used):
                    src = ffn_part(b, 0, GU)
                    res.ready(sp, "gu1", b - 2)
                    sp.dma_start(blocks_w[:, slot, 0:GU], src).then_inc(gu_in[slot], 16)
                    src = ffn_part(b, GU, BLOCK)
                    sp.wait_ge(block_used[slot], used)
                    sp.dma_start(blocks_w[:, slot, GU:], src).then_inc(down_in[slot], 16)

                with sp.Fori(0, B1 - 1) as r:
                    next_block(2 * r + 2, 0, B1 * l + r + 1)
                    next_block(2 * r + 3, 1, B1 * l + r + 2)
                next_block(NFB - 1, 0, B1 * l + B1)

            sp.dma_start(prm2[:, :], a["prm2"]).then_inc(prm2_in, 16)
            for s in range(4):
                sp.dma_start(m[:, s, :], a["w_ada"][0, s]).then_inc(m_in[s], 16)
            sp.wait_ge(block_used[1], B1 * DEPTH + 1)
            sp.dma_start(gpost, a["g_post"].partition_broadcast(2)).then_inc(rows_in, 16)
            sp.wait_ge(filled[3], DEPTH * LAY.count[3])
            sp.dma_start(modrow, a["b_ada"].partition_broadcast(2)).then_inc(rows_in, 16)
            sp.dma_start(yT[:, :, :].rearrange("p k t -> p (k t)"), a["pos"]).then_inc(pos_in, 16)
            sp.wait_ge(drained[3], DEPTH * LAY.count[3] + 1)
            sp.dma_start(gfin, a["g_final"].partition_broadcast(P)).then_inc(pos_in, 16)
            for t in range(NT):
                sp.dma_start(ctx_x[:, t, :], a["ctx"][t * P:(t + 1) * P, :]).then_inc(ctx_in, 16)
            sp.dma_start(w_rt.rearrange("p k n -> p (k n)"), a["w_router"]).then_inc(router_in, 16)
            sp.dma_start(b_rt, a["b_router"].partition_broadcast(P)).then_inc(router_in, 16)
            with sp.Fori(1, 3) as i:
                for s in range(4):
                    src = a["w_ada"][bass.ds(i, 1), s].rearrange("a p n -> p (a n)")
                    sp.wait_ge(filled[s], sec.index(f"ada{s}", 0)[1] + i)
                    sp.dma_start(m[:, s, :], src).then_inc(m_in[s], 16)
            for s in range(3):
                sec.ready(sp, f"ada{s}", 2)
                sp.dma_start(m[:, s, :], a["w_in_2"][s]).then_inc(m_in[s], 16)
            sec.ready(sp, "ada3", 2)
            sp.dma_start(m[:, 3, 0:3584], a["heads_2"]).then_inc(heads_in, 16)
            for s, job in ((0, "xm3"), (1, "z1")):
                sec.ready(sp, job)
                sp.dma_start(m[:, s, :], a["w_out_2"][:, s * 4096:(s + 1) * 4096]).then_inc(m_in[s], 16)

            def piece(q, c, expert=None):
                e = bass.ds(4 * q + c // 3, 1) if expert is None else bass.ds(expert, 1)
                return a["experts"][e, :, (c % 3) * 4096:(c % 3 + 1) * 4096].rearrange("a p n -> p (a n)")

            def load(src, c, q, after=True):
                if after:
                    i, kind = divmod(c - 4, 3)
                    sec.ready(sp, ("eG", "eU", "eD1")[kind], 2 * (QUAD * q + i))
                sp.dma_start(m[:, c % 4, :], src).then_inc(piece_in[c % 4], 16)

            sec.ready(sp, "wo3")
            for c in range(4):
                load(piece(0, c), c, 0, after=False)
            with sp.Fori(0, NE // QUAD - 1) as q:
                for c in range(4, 16):
                    src = piece(q, c)
                    load(src, c, q)
            q = NE // QUAD - 1
            for c in range(4, 12):
                load(piece(q, c), c, q)
            sp.wait_ge(table_ready, 1)
            experts = [sp.value_load(table_i[0:1, n:n + 1], min_val=0, max_val=NE - 1) for n in range(OVER)]
            for c in (12, 13):
                load(piece(q, c, experts[0]), c, q)
            with sp.If(sp.value_load(table_i[0:1, OVER:OVER + 1], min_val=0, max_val=OVER) > 0):
                q = NE // QUAD
                for c in range(2, 12):
                    load(piece(q, c, experts[c // 3]), c, q)
            for t in range(NT):
                sp.wait_ge(out_ready, 2 * t + 2)
                sp.dma_start(out[t * P:(t + 1) * P, :], x[:, t, :]).then_inc(out_stored, 16)
            sp.wait_ge(out_stored, 16 * NT)

        @block.tensor
        def _(pe):
            def chain(out_, pairs, first=True, last=True):
                for n, (lhsT, rhs) in enumerate(pairs):
                    ins = pe.matmul(out_, lhsT, rhs, start=first and n == 0, stop=last and n == len(pairs) - 1,
                                    skip_group_check=not (first and last))
                return ins

            def split_chain(out_, pairs, first=True, last=True):
                n = len(pairs)
                for i, ((xh, xl), (wh, wl)) in enumerate(pairs):
                    pe.matmul(out_, xh, wh, start=first and i == 0, stop=False, skip_group_check=True)
                    pe.matmul(out_, xh, wl, start=False, stop=False, skip_group_check=True)
                    ins = pe.matmul(out_, xl, wh, start=False, stop=last and i == n - 1, skip_group_check=True)
                return ins

            pe.wait_ge(const_in, 16)
            with pe.Fori(0, DEPTH) as l:
                res = layer_results(l)

                def to(job):
                    return bank[LAY.at[job][0]]

                def transposes(name, ready):
                    for t in range(NT):
                        pe.wait_ge(xn_ready, ready + t)
                        for b in range(2):
                            job = f"{name}_{t}{b}"
                            res.room(pe, job)
                            for k in range(4):
                                c = (4 * b + k) * P
                                ins = pe.transpose(to(job)[:, k * P:(k + 1) * P], xn[:, t, c:c + P], ident)
                            res.done(ins, job)

                def token_job(name, w, t):
                    job, cols = f"{name}{t}", w.shape[2]
                    res.room(pe, job)
                    res.done(chain(to(job)[:, 0:cols], [(hT[:, k, t * P:(t + 1) * P], w[:, k, :]) for k in range(KD)]), job)

                def feature_job(job, w, c0):
                    res.room(pe, job)
                    for g in range(2):
                        ins = chain(to(job)[:, g * T:(g + 1) * T],
                                    [(w[:, k, c0 + g * P:c0 + (g + 1) * P], hT[:, k, :]) for k in range(KD)])
                    res.done(ins, job)

                def w_view(s):
                    return m[:, s, :].rearrange("p (k n) -> p k n", k=KD)

                transposes("tx1", 4 * l + 1)
                pe.wait_ge(m_in[0], 32 * l + 16)
                for t in range(NT):
                    for b in range(2):
                        res.arrived(pe, f"tx1_{t}{b}")
                    token_job("vqi", w_view(0), t)
                pe.wait_ge(kwi_in, 16 * l + 16)
                for t in range(NT):
                    token_job("kwi", kwi_w[:, :, :], t)
                pe.wait_ge(m_in[2], 16 * l + 16)
                feature_job("da", w_view(2), 0)
                feature_job("dg", w_view(2), 256)

                for t in range(NT):
                    job = f"riT{t}"
                    pe.wait_ge(ri_ready, 2 * l + t + 1)
                    res.room(pe, job)
                    for c in range(3):
                        ins = pe.transpose(to(job)[:, c * P:(c + 1) * P],
                                           ri[:, t, 2 * c:2 * c + 2, :].rearrange("p h d -> p (h d)"), ident)
                    res.done(ins, job)
                pe.wait_ge(m_in[1], 32 * l + 16)
                for t in range(NT):
                    token_job("qk", w_view(1), t)
                for job, t, heads in (("sc0a", 0, (0, 2)), ("sc0b", 0, (1, 3)), ("sc1a", 1, (0, 2)), ("sc1b", 1, (1, 3))):
                    nk = (t + 1) * P
                    for u in range(t + 1):
                        res.arrived(pe, f"riT{u}")
                    res.room(pe, job)
                    for n, j in enumerate(heads):
                        o = HD * (j % 2)
                        ins = pe.matmul(to(job)[:, n * nk:(n + 1) * nk], riT[o:o + HD, j // 2, t * P:(t + 1) * P],
                                        riT[o:o + HD, 2, 0:nk], start=True, stop=True)
                    res.done(ins, job)
                pe.wait_ge(in_lo, (IN_SUBS - 4) * l + 10)
                pe.wait_ge(h1_ready, l + 1)
                wh, wl = (w_l[:, s, :].rearrange("p (k n) -> p k n", k=KD) for s in (2, 3))
                for t in range(NT):
                    res.room(pe, f"guv{t}")
                    res.done(split_chain(to(f"guv{t}")[:, :],
                                         [((h1_h[:, k, t * P:(t + 1) * P], h1_l[:, k, t * P:(t + 1) * P]), (wh[:, k, :], wl[:, k, :]))
                                          for k in range(KD)]), f"guv{t}")
                for job, lo, hi, c0 in (("ab", 0, 4096, 0), ("ac", 0, 4096, 256), ("ah", 4096, 6144, 0)):
                    wh, wl = (fw_l[:, slot, lo:hi].rearrange("p (k n) -> p k n", k=KD) for slot in (1, 0))
                    res.room(pe, job)
                    for g in range(2):
                        at = slice(c0 + g * P, c0 + (g + 1) * P)
                        ins = split_chain(to(job)[:, g * T:(g + 1) * T],
                                          [((wh[:, k, at], wl[:, k, at]), (h1_h[:, k, :], h1_l[:, k, :])) for k in range(KD)])
                    res.done(ins, job)
                for t in range(NT):
                    job = f"rqT{t}"
                    pe.wait_ge(rq_ready, 2 * l + t + 1)
                    res.room(pe, job)
                    for c in range(4):
                        ins = pe.transpose(to(job)[:, c * P:(c + 1) * P],
                                           rq[:, t, 2 * c:2 * c + 2, :].rearrange("p h d -> p (h d)"), ident)
                    res.done(ins, job)
                pe.wait_ge(conv_ready, l + 1)
                res.room(pe, "cvT")
                for t in range(NT):
                    for g in range(2):
                        ins = pe.transpose(to("cvT")[:, t * T + g * P:t * T + (g + 1) * P],
                                           conv[:, g, t * P:(t + 1) * P], ident)
                res.done(ins, "cvT")
                pe.wait_ge(ws_ready, l + 1)
                for t in range(NT):
                    job = f"mix{t}"
                    pe.wait_ge(v_ready, 2 * l + t + 1)
                    res.room(pe, job)
                    for h in range(H):
                        ins = pe.matmul(to(job)[:, h * HD:(h + 1) * HD], wsT[:, h, :],
                                        zg[:, t, G + h * HD:G + (h + 1) * HD], start=True, stop=True)
                    res.done(ins, job)
                for job, t, heads in (("lg0a", 0, (0, 2)), ("lg0b", 0, (1, 3)), ("lg1a", 1, (0, 2)), ("lg1b", 1, (1, 3))):
                    nk = (t + 1) * P
                    for u in range(t + 1):
                        res.arrived(pe, f"rqT{u}")
                    res.room(pe, job)
                    for n, h in enumerate(heads):
                        o = HD * (h % 2)
                        ins = pe.matmul(to(job)[:, n * nk:(n + 1) * nk], rqT[o:o + HD, h // 2, t * P:(t + 1) * P],
                                        rqT[o:o + HD, 2 + h // 2, 0:nk], start=True, stop=True)
                    res.done(ins, job)

                def mixed_rows(job, part, t):
                    for k in range(2):
                        ins = pe.transpose(to(job)[:, k * T + t * P:k * T + (t + 1) * P],
                                           ycat[:, t, part, k * P:(k + 1) * P], ident)
                    return ins

                res.room(pe, "ybT")
                for t in range(NT):
                    pe.wait_ge(yb_ready, 2 * l + t + 1)
                    ins = mixed_rows("ybT", 0, t)
                res.done(ins, "ybT")
                res.arrived(pe, "cvT")
                res.room(pe, "cnT")
                for g in range(2):
                    for t in range(NT):
                        ins = pe.transpose(to("cnT")[:, g * T + t * P:g * T + (t + 1) * P],
                                           conv_n[:, t, g * P:(g + 1) * P], ident)
                res.done(ins, "cnT")

                def out_proj(ks, first, last):
                    for n in range(4):
                        t, c = n // 2, n % 2
                        if first:
                            res.room(pe, f"wo{n}")
                        pairs = []
                        for k in ks:
                            tok, o = slice(t * P, (t + 1) * P), (k % 4) * D + c * 512
                            pairs.append(((y_h[:, k, tok], y_l[:, k, tok]),
                                          (w_l[:, 2 + k // 4, o:o + 512], w_l[:, k // 4, o:o + 512])))
                        ins = split_chain(bank[n][:, :], pairs, first, last)
                        if last:
                            res.done(ins, f"wo{n}")

                pe.wait_ge(in_lo, (IN_SUBS - 4) * l + 14)
                pe.wait_ge(mix_ready, 4 * l + 2)
                out_proj((0, 1, 2, 3), True, False)
                for job, t, u in (("pT0", 0, 0), ("pT1a", 1, 0), ("pT1b", 1, 1)):
                    pe.wait_ge(exp_ready, 8 * l + 4 * t + 4)
                    res.room(pe, job)
                    for h in range(H):
                        ins = pe.transpose(to(job)[:, h * P:(h + 1) * P], lg[t][:, h, u * P:(u + 1) * P], ident)
                    res.done(ins, job)
                for t in range(NT):
                    job = f"av{t}"
                    for p_job in (("pT0",), ("pT1a", "pT1b"))[t]:
                        res.arrived(pe, p_job)
                    res.room(pe, job)
                    for h in range(H):
                        ins = chain(to(job)[:, h * HD:(h + 1) * HD],
                                    [(pT0[:, h, :] if t == 0 else pT1[:, u, h, :], va[:, u, h * HD:(h + 1) * HD])
                                     for u in range(t + 1)])
                    res.done(ins, job)
                pe.wait_ge(out_lo, 4 * l + 4)
                pe.wait_ge(mix_ready, 4 * l + 3)
                out_proj((6,), False, False)
                res.room(pe, "ycT")
                for t in range(NT):
                    res.arrived(pe, f"av{t}")
                    ins = mixed_rows("ycT", 1, t)
                res.done(ins, "ycT")
                out_proj((7,), False, False)
                pe.wait_ge(mix_ready, 4 * l + 4)
                out_proj((4, 5), False, True)

                transposes("tx2", 4 * l + 3)

                def split_by(b, subs):
                    pe.wait_ge(ffn_lo, SUBS * (NFB * l + b) + subs)

                def gate_up(slot, j, i):
                    job = f"gu{j}"
                    res.room(pe, job, i)
                    wh, wl = (w[:, 0:GU].rearrange("p (q k n) -> p q k n", q=2, k=KD)[:, :, :, j * P:(j + 1) * P]
                              for w in (fw_h[:, 1 - slot, :], fw_l[:, slot, :]))
                    for q in range(2):
                        ins = split_chain(to(job)[:, q * T:(q + 1) * T],
                                          [((wh[:, q, k, :], wl[:, q, k, :]), (h_h[:, k, :], h_l[:, k, :])) for k in range(KD)])
                    res.done(ins, job)

                def down(slot, j, i, first=False, last=False):
                    if j == 0:
                        split_by(i, SUBS)
                    res.arrived(pe, f"gu{j}", i)
                    for n in range(4):
                        t, c = n // 2, n % 2
                        if first:
                            res.room(pe, f"y{n}")
                        o = GU + j * D + c * 512
                        ins = split_chain(bank[n][:, :], [((a2[:, 0, j, t * P:(t + 1) * P], a2[:, 1, j, t * P:(t + 1) * P]),
                                                           (fw_h[:, 1 - slot, o:o + 512], fw_l[:, slot, o:o + 512]))], first, last)
                        if last:
                            res.done(ins, f"y{n}")
                    return ins

                split_by(0, 4)
                pe.wait_ge(h_ready, 4 * l + 4)
                gate_up(0, 0, 0)
                gate_up(0, 1, 0)
                down(0, 0, 0, first=True)
                with pe.Fori(0, B1) as r:
                    split_by(2 * r + 1, 4)
                    gate_up(1, 0, 2 * r + 1)
                    down(0, 1, 2 * r).then_inc(block_used[0], 1)
                    gate_up(1, 1, 2 * r + 1)
                    down(1, 0, 2 * r + 1)
                    split_by(2 * r + 2, 4)
                    gate_up(0, 0, 2 * r + 2)
                    down(1, 1, 2 * r + 1).then_inc(block_used[1], 1)
                    gate_up(0, 1, 2 * r + 2)
                    down(0, 0, 2 * r + 2)
                down(0, 1, NFB - 1, last=True)

            def to(job):
                return bank[SEC.at[job][0]]

            pe.wait_ge(cs_ready, 2)
            with pe.Fori(0, 3) as i:
                for s in range(4):
                    pe.wait_ge(ada_lo, 16 * i + 4 * s + 4)
                    sec.room(pe, f"ada{s}", i)
                    wh, wl = (w.rearrange("p (k n) -> p k n", k=KD) for w in (ada_h[s % 2][:, :], w_l[:, s, :]))
                    sec.done(split_chain(bank[s][0:2, :], [((cs2[:, 0, k, :], cs2[:, 1, k, :]), (wh[:, k, :], wl[:, k, :]))
                                                           for k in range(KD)]), f"ada{s}")
            for s in range(4):
                sec.arrived(pe, f"ada{s}", 2)
            sec.room(pe, "modT")
            for n, row in enumerate((0, 1, 3, 4)):
                for k in range(KD):
                    ins = pe.transpose(to("modT")[:, 2 * (KD * n + k):2 * (KD * n + k) + 2],
                                       modrow[:, row * D + k * P:row * D + (k + 1) * P], ident[0:2, 0:2])
            sec.done(ins, "modT")
            pe.wait_ge(gate_rows, 2)
            for n in range(4):
                o = (2 + 3 * (n // 2)) * D + (n % 2) * 512
                sec.room(pe, f"gate{n}")
                sec.done(pe.matmul(bank[n][:, :], ident[0:2, 0:1].to_broadcast([2, P]), modrow[:, o:o + 512],
                                   start=True, stop=True), f"gate{n}")

            def transposes2(name, ready):
                for t in range(NT):
                    pe.wait_ge(xn_ready, ready + t)
                    for n in range(4):
                        if t == 0:
                            sec.room(pe, f"{name}{n}")
                        for k in range(2):
                            c = (2 * n + k) * P
                            ins = pe.transpose(to(f"{name}{n}")[:, k * T + t * P:k * T + (t + 1) * P],
                                               xn2[:, t, c:c + P], ident)
                        if t == NT - 1:
                            sec.done(ins, f"{name}{n}")

            XN = 4 * DEPTH
            transposes2("tc", XN + 1)
            transposes2("tl", XN + 3)
            for n in range(4):
                sec.arrived(pe, f"tc{n}")
                sec.arrived(pe, f"tl{n}")
            M01, M23 = 32 * DEPTH + 48, 16 * DEPTH + 48
            w = [m[:, s, :].rearrange("p (k n) -> p k n", k=KD) for s in range(3)]
            pe.wait_ge(m_in[0], M01 + 16)
            for j in range(MH):
                sec.room(pe, f"xm{j}")
                for q, src in enumerate((hC, hT)):
                    ins = chain(to(f"xm{j}")[:, q * T:(q + 1) * T],
                                [(w[0][:, k, j * P:(j + 1) * P], src[:, k, :]) for k in range(KD)])
                sec.done(ins, f"xm{j}")
            pe.wait_ge(m_in[1], M01 + 16)
            for q in range(2):
                sec.room(pe, f"z{q}")
                for g in range(2):
                    j = 2 * q + g
                    ins = chain(to(f"z{q}")[:, g * T:(g + 1) * T],
                                [(w[1][:, k, j * P:(j + 1) * P], hT[:, k, :]) for k in range(KD)])
                sec.done(ins, f"z{q}")
            pe.wait_ge(heads_in, 16)
            for j in range(MH):
                sec.arrived(pe, f"xm{j}")
            for c in range(4):
                sec.room(pe, f"vt{c}")
                for j in range(MH):
                    ins = pe.matmul(to(f"vt{c}")[:, j * DH:(j + 1) * DH],
                                    xmp[:, j, c // 2, 1 + (c % 2) * P:1 + (c % 2 + 1) * P], bd[:, 2, j, :], start=True, stop=True)
                sec.done(ins, f"vt{c}")
            for n in range(12):
                j, q = n // 3, n % 3
                if q == 0:
                    pe.wait_ge(act_ready, j + 1)
                sec.room(pe, f"qkv{n}")
                src = actT[:, j, :].rearrange("p (s t) -> p s t", s=2) if q < 2 else xmp[:, j, :, 1:1 + CTX]
                sec.done(pe.matmul(to(f"qkv{n}")[:, :].rearrange("p (s t) -> p s t", s=2), bd[:, q, j, :], src,
                                   start=True, stop=True), f"qkv{n}")
            for n in range(12):
                sec.arrived(pe, f"qkv{n}")
            sec.room(pe, "gates")
            sec.done(chain(to("gates")[:, :], [(w_if[:, 4 * q + j, :], qkvT[:, q, j, :]) for j in range(MH) for q in range(3)]),
                     "gates")
            pe.wait_ge(m_in[2], M23 + 16)
            for t in range(NT):
                sec.room(pe, f"u{t}")
                sec.done(chain(to(f"u{t}")[:, :], [(hT[:, k, t * P:(t + 1) * P], w[2][:, k, :]) for k in range(KD)]), f"u{t}")
            for g in range(4):
                sec.room(pe, f"fp{g}")
                for t in range(NT):
                    sec.arrived(pe, f"u{t}")
                sec.done(chain(to(f"fp{g}")[:, :], [(u_rows[:, t, g * P:(g + 1) * P], dft[:, t, :]) for t in range(NT)]), f"fp{g}")
            for p in range(2):
                sec.room(pe, f"ff{p}")
                for g in (2 * p, 2 * p + 1):
                    sec.arrived(pe, f"fp{g}")
                    ins = chain(to(f"ff{p}")[:, (g % 2) * T:(g % 2 + 1) * T],
                                [(ccos, fP[:, g, 0:T]), (nsin, fP[:, g, T:2 * T])])
                sec.done(ins, f"ff{p}")
            for p in range(2):
                sec.arrived(pe, f"ff{p}")
                sec.room(pe, f"fy{p}")
                for g in (2 * p, 2 * p + 1):
                    ins = pe.matmul(to(f"fy{p}")[:, (g % 2) * T:(g % 2 + 1) * T], w_f[:, g, :], fT[:, g, :],
                                    start=True, stop=True)
                sec.done(ins, f"fy{p}")
            pe.wait_ge(scan_ready, 1)
            sec.room(pe, "rT")
            for c in range(4):
                pe.transpose(to("rT")[:, c * ROWS:(c + 1) * ROWS], rr[0:ROWS, c * P:(c + 1) * P], ident[0:ROWS, 0:ROWS])
            for t in range(NT):
                ins = pe.transpose(to("rT")[:, (4 + t) * ROWS:(5 + t) * ROWS], cum[0:ROWS, CTX + t * P:CTX + (t + 1) * P],
                                   ident[0:ROWS, 0:ROWS])
            sec.done(ins, "rT")

            def head_scores(h):
                sec.room(pe, f"rb{h}")
                for d in range(2):
                    r = 32 * d + h
                    ins = pe.matmul(to(f"rb{h}")[:, d * T:(d + 1) * T], ident[0:ROWS, r:r + 1].to_broadcast([ROWS, P]),
                                    rmax[0:ROWS, CTX:S2], start=True, stop=True)
                sec.done(ins, f"rb{h}")
                for job, cc in ((f"qk{h}a", 0), (f"qk{h}b", 2)):
                    sec.room(pe, job)
                    for c in (cc, cc + 1):
                        ins = pe.matmul(to(job)[:, (c - cc) * T:(c - cc + 1) * T], qkvT[:, 1, h, c * P:(c + 1) * P],
                                        qkvT[:, 0, h, CTX:S2], start=True, stop=True)
                    sec.done(ins, job)

            def head_values(h):
                for d in range(2):
                    if d == 0:
                        pe.wait_ge(s_ready, h + 1)
                    else:
                        sec.arrived(pe, f"qk{h}b")
                    job = f"o{h}{d}"
                    sec.room(pe, job)
                    for t in range(NT):
                        seen = ((0, 1, 2), (0, 1, 2, 3))[t] if d == 0 else ((0, 1, 2, 3), (0, 1, 3))[t]
                        ins = chain(to(job)[:, t * (DH + 1):(t + 1) * (DH + 1)],
                                    [(E[:, h % 2, d, c, t * P:(t + 1) * P], vtok[:, c, h, :]) for c in seen])
                    sec.done(ins, job)

            head_scores(0)
            for h in range(MH):
                if h + 1 < MH:
                    head_scores(h + 1)
                head_values(h)
            pe.wait_ge(m_in[0], M01 + 32)
            pe.wait_ge(m_in[1], M01 + 32)

            def out_proj2(ks, first, last):
                for n in range(4):
                    t, c = n // 2, n % 2
                    if first:
                        sec.room(pe, f"wo{n}")
                    ins = chain(bank[n][:, :],
                                [(yT[:, k, t * P:(t + 1) * P],
                                  m[:, k // 4, (k % 4) * D + c * 512:(k % 4) * D + (c + 1) * 512]) for k in ks], first, last)
                    if last:
                        sec.done(ins, f"wo{n}")

            for p in range(2):
                sec.arrived(pe, f"fy{p}")
            out_proj2((4, 5, 6, 7), True, False)
            for p in range(2):
                pe.wait_ge(hn_ready, 1)
                sec.room(pe, f"hT{p}")
                for g in range(2):
                    for t in range(NT):
                        h = 2 * p + g
                        ins = pe.transpose(to(f"hT{p}")[:, g * T + t * P:g * T + (t + 1) * P],
                                           h_rows[:, t, h * DH:(h + 1) * DH], ident)
                sec.done(ins, f"hT{p}")
            for h in range(0, MH, 2):
                pe.wait_ge(y_ready, h + 2)
                out_proj2((h, h + 1), False, h + 2 == MH)
            transposes2("t2", XN + 5)
            for n in range(4):
                sec.arrived(pe, f"t2{n}")
            pe.wait_ge(router_in, 32)
            for t in range(NT):
                sec.room(pe, f"rt{t}")
                sec.done(chain(to(f"rt{t}")[:, 0:NG + NE], [(h_rt[:, k, t * P:(t + 1) * P], w_rt[:, k, :]) for k in range(KD)]),
                         f"rt{t}")
            pe.wait_ge(chosen_ready, 1)
            sec.room(pe, "rank")
            before, ones = const[:, K_BEFORE:K_BEFORE + P], const[:, K_ONES:K_ONES + P]
            chain(to("rank")[:, 0:NE], [(before, chosen[:, 0, :])])
            chain(to("rank")[:, NE:2 * NE], [(ones, chosen[:, 0, :]), (before, chosen[:, 1, :])])
            sec.done(chain(to("rank")[:, 2 * NE:3 * NE], [(ones, chosen[:, t, :]) for t in range(NT)]), "rank")

            def gather(bank_, side, c):
                for kk in range(2):
                    k = 2 * c + kk
                    pairs = [(xn_p[:, t, k * P:(k + 1) * P], choice[:, side, t, :]) for t in range(NT) for xn_p in (xn_h, xn_l)]
                    for n, (lhsT, rhs) in enumerate(pairs):
                        ins = pe.matmul(bank_[:, kk * T:(kk + 1) * T], lhsT, rhs, start=n == 0, stop=n == 3)
                return ins

            def transposed_choice(bank_, side, n, i):
                for t in range(NT):
                    ins = pe.matmul(bank_[:, t * (P + 2):(t + 1) * (P + 2)], choice[:, side, t, n * P:(n + 1) * P],
                                    pick_w[:, i, 2 - 2 * t:P + 4 - 2 * t], start=True, stop=True)
                return ins

            def scatter(i, first=False, last=False):
                for n in range(4):
                    t, c = n // 2, n % 2
                    if first:
                        sec.room(pe, f"ye{n}")
                    for part in range(2):
                        ins = pe.matmul(bank[n][:, :], choice_t[:, i, t * P:(t + 1) * P],
                                        y2[:, part, c * 512:(c + 1) * 512], start=first and part == 0,
                                        stop=last and part == 1, skip_group_check=True)
                    if last:
                        sec.done(ins, f"ye{n}")

            def expert_pass(q, i, final=False):
                p, side = QUAD * q + i, i // 2
                more = not (final and i >= 2)
                for kind, name in enumerate(("eG", "eU")):
                    pe.wait_ge(lo_ready, 12 * p + 4 * kind + 4)
                    if kind == 0 and i % 2 == 0:
                        pe.wait_ge(xg_ready, 4 * (2 * q + side) + 4)
                    sec.room(pe, name, 2 * p)
                    o = (3 * i + kind) % 4
                    wh, wl = (v.rearrange("p (k n) -> p k n", k=KD) for v in (w_h[:, kind, :], w_l[:, o, :]))
                    xs = [xg[:, side, part, :, (i % 2) * P:(i % 2 + 1) * P] for part in range(2)]
                    sec.done(split_chain(to(name)[:, :], [((xs[0][:, k, :], xs[1][:, k, :]), (wh[:, k, :], wl[:, k, :]))
                                                          for k in range(KD)]), name)
                if more:
                    if i % 2 == 0:
                        pe.wait_ge(choice_ready, 2 * q + side + 2)
                    sec.room(pe, "e7", 10 * q + PIECES[i][0])
                    sec.done(gather(to("e7"), 1 - side, 2 * (i % 2)), "e7")
                sec.arrived(pe, "eU", 2 * p)
                sec.room(pe, "e6", 6 * q + HIDDEN_T[i])
                for j in range(4):
                    ins = pe.transpose(to("e6")[:, j * P:(j + 1) * P], hidden[:, j * P:(j + 1) * P], ident)
                sec.done(ins, "e6")
                sec.arrived(pe, "eD1", 2 * p - 2)
                if i in (1, 3):
                    sec.arrived(pe, "e6", 6 * q - 1 + 3 * (i // 2))
                else:
                    sec.arrived(pe, "e7", 10 * q - 6 + 5 * (i // 2))
                scatter((i - 1) % QUAD)
                if more:
                    sec.room(pe, "e7", 10 * q + PIECES[i][1])
                    sec.done(gather(to("e7"), 1 - side, 2 * (i % 2) + 1), "e7")
                pe.wait_ge(lo_ready, 12 * p + 12)
                sec.arrived(pe, "e6", 6 * q + HIDDEN_T[i])
                o = (3 * i + 2) % 4
                for c, name in enumerate(("eD0", "eD1")):
                    sec.room(pe, name, 2 * p)
                    pairs = []
                    for j in range(4):
                        at = slice(j * D + c * 512, j * D + (c + 1) * 512)
                        pairs.append(((aT2[:, 0, j, :], aT2[:, 1, j, :]), (w_h[:, 2, at], w_l[:, o, at])))
                    sec.done(split_chain(to(name)[:, :], pairs), name)
                if more and i % 2:
                    for n, (name, at) in enumerate((("e6", 6 * q + CHOSEN_T6[i]), ("e7", 10 * q + CHOSEN_T7[i]))):
                        sec.room(pe, name, at)
                        sec.done(transposed_choice(to(name), 1 - side, n, (i + 1 + n) % QUAD), name)

            pe.wait_ge(choice_ready, 1)
            for c in range(4):
                sec.room(pe, f"first{c}")
                sec.done(gather(to(f"first{c}"), 0, c), f"first{c}")
            for n in range(2):
                sec.room(pe, f"first_sT{n}")
                sec.done(transposed_choice(to(f"first_sT{n}"), 0, n, n), f"first_sT{n}")
            pe.wait_ge(y_zero, 3)
            scatter(QUAD - 1, first=True)
            with pe.Fori(0, NE // QUAD) as q:
                for i in range(QUAD):
                    expert_pass(q, i)
            pe.wait_ge(table_ready, 1)
            with pe.If(pe.value_load(table_i[0:1, OVER:OVER + 1], min_val=0, max_val=OVER) > 0):
                for i in range(QUAD):
                    expert_pass(NE // QUAD, i, final=True)
                sec.arrived(pe, "eD1", 2 * NPASS - 2)
            sec.arrived(pe, "eD1", 2 * NE - 2)
            scatter(QUAD - 1, last=True)

        @block.scalar
        def _(act):
            act.wait_ge(x_in, 16 * NT)
            with act.Fori(0, DEPTH) as l:
                res = layer_results(l)

                def to(job):
                    return bank[LAY.at[job][0]]

                def copy(job, dst, src, func=ACT.Copy, last=True):
                    ins = act.activation(dst, src, func)
                    if last:
                        res.moved(ins, job)

                def squares(summed):
                    for t in range(NT):
                        summed(t)
                        act.activation(xn[:, t, :], x[:, t, :], ACT.Square, accum_out=ss[:, t:t + 1]).then_inc(ss_ready, 1)

                squares(lambda t: act.wait_ge(drained[2 * t + 1], l * LAY.count[2 * t + 1] + 1))
                act.wait_ge(prm_in, 48 * l + 48)
                for t in range(NT):
                    res.ready(act, f"vqi{t}")
                    copy(None, zi[:, t, 0:256], to(f"vqi{t}")[:, 256:512], last=False)
                    copy(f"vqi{t}", va[:, t, :], to(f"vqi{t}")[:, 0:256])
                for t in range(NT):
                    res.ready(act, f"kwi{t}")
                    act.activation(wi[:, t, :], to(f"kwi{t}")[:, 64:68], ACT.Copy, scale=(H * HD) ** -0.5)
                    copy(f"kwi{t}", zi[:, t, 256:320], to(f"kwi{t}")[:, 0:64])
                for t in range(NT):
                    for b in range(2):
                        res.arrived(act, f"tx1_{t}{b}")
                act.activation(h1_h[:, :, :], hT[:, :, :], ACT.Copy).then_inc(h1_rounded, 1)

                def rounded_in(dst, src, subs):
                    for n in range(subs):
                        at = slice(n * 1024, (n + 1) * 1024)
                        act.activation(dst[:, at], src[:, at], ACT.Copy).then_inc(in_hi, 1)

                act.wait_ge(ab_in, 32 * l + 32)
                rounded_in(fw_l[:, 1, :], blocks_w[:, 0, :], 6)
                res.ready(act, "dg")
                copy("dg", sig, to("dg")[:, :].rearrange("p (g t) -> p g t", g=2), ACT.Sigmoid)
                for t in range(NT):
                    res.ready(act, f"riT{t}")
                    copy(f"riT{t}", riT[:, :, t * P:(t + 1) * P], to(f"riT{t}")[:, 0:3 * P].rearrange("p (c q) -> p c q", c=3))
                act.wait_ge(m_in[3], 16 * l + 16)
                rounded_in(w_l[:, 2, :], m[:, 3, :], 4)
                for t in range(NT):
                    res.ready(act, f"qk{t}")
                    copy(f"qk{t}", zq[:, t, :], to(f"qk{t}")[:, :])
                for job, t, h0 in (("sc0a", 0, 0), ("sc0b", 0, 1), ("sc1a", 1, 0), ("sc1b", 1, 1)):
                    res.ready(act, job)
                    copy(job, rel[t][:, h0::2, :], to(job)[:, 0:2 * (t + 1) * P].rearrange("p (h s) -> p h s", h=2), ACT.Relu)
                for t in range(NT):
                    res.ready(act, f"guv{t}")
                    copy(f"guv{t}", zg[:, t, :], to(f"guv{t}")[:, :])
                for s in range(2):
                    act.wait_ge(m_in[s], 32 * l + 32)
                    rounded_in(w_l[:, 2 + s, :], m[:, s, :], 4)
                res.ready(act, "ac")
                copy("ac", acs, to("ac")[:, :].rearrange("p (g t) -> p g t", g=2))
                for t in range(NT):
                    res.ready(act, f"rqT{t}")
                    copy(f"rqT{t}", rqT[:, :, t * P:(t + 1) * P], to(f"rqT{t}")[:, :].rearrange("p (c q) -> p c q", c=4))
                def rounded_mix(g, job):
                    res.arrived(act, job)
                    act.activation(y_h[:, 2 * g:2 * g + 2, :], yT[:, 2 * g:2 * g + 2, :], ACT.Copy).then_inc(mix_rounded, 1)

                rounded_mix(0, "ab")
                res.ready(act, "ybT")
                copy("ybT", yT[:, 2:4, :], to("ybT")[:, :].rearrange("p (k t) -> p k t", k=2))
                rounded_mix(1, "ybT")
                res.ready(act, "cnT")
                for g in range(2):
                    ins = act.activation(yT[:, 6 + g, :], to("cnT")[:, g * T:(g + 1) * T], ACT.Silu,
                                         scale=prm[:, C_LNG + g:C_LNG + g + 1], bias=prm[:, C_LNB + g:C_LNB + g + 1])
                res.moved(ins, "cnT")
                rounded_mix(3, "cnT")
                for t in range(NT):
                    act.wait_ge(lg_ready, 2 * l + t + 1)
                    for h in range(H):
                        act.activation(lg[t][:, h, :], lg[t][:, h, :], ACT.Exp, scale=HD ** -0.5, bias=nms[:, t, h:h + 1],
                                       accum_out=rsum[:, t, h:h + 1]).then_inc(exp_ready, 1)
                def rounded(slot, r, subs):
                    if 0 in subs:
                        act.wait_ge(gu_in[slot], 16 * ((B0, B1)[slot] * l + r + 1))
                    else:
                        act.wait_ge(down_in[slot], 16 * ((B0, B1)[slot] * l + r + 1))
                    for n in subs:
                        at = slice(n * SUB, (n + 1) * SUB)
                        act.activation(fw_h[:, 1 - slot, at], blocks_w[:, slot, at], ACT.Copy).then_inc(ffn_hi, 1)

                for job, dst in (("pT0", pT0), ("pT1a", pT1[:, 0]), ("pT1b", pT1[:, 1])):
                    res.ready(act, job)
                    copy(job, dst, to(job)[:, :].rearrange("p (h q) -> p h q", h=H))
                rounded(0, 0, range(0, 4))
                res.ready(act, "ycT")
                copy("ycT", yT[:, 4:6, :], to("ycT")[:, :].rearrange("p (k t) -> p k t", k=2))
                rounded_mix(2, "ycT")

                rounded(0, 0, range(4, 6))
                squares(lambda t: res.arrived(act, f"wo{2 * t + 1}"))
                for n in range(4):
                    t, b = n // 2, n % 2
                    res.arrived(act, f"tx2_{t}{b}")
                    part = (slice(None), slice(4 * b, 4 * b + 4), slice(t * P, (t + 1) * P))
                    act.activation(h_h[part], h_full[part], ACT.Copy).then_inc(h_rounded, 1)

                def ffn_silu(j, i):
                    res.ready(act, f"gu{j}", i)
                    act.activation(sga[:, j, :], to(f"gu{j}")[:, 0:T], ACT.Silu).then_inc(silu_ready, 1)

                with act.Fori(0, B1) as r:
                    for s in range(2):
                        ffn_silu(0, 2 * r + s)
                        rounded(1 - s, r + s, range(0, 4))
                        ffn_silu(1, 2 * r + s)
                        rounded(1 - s, r + s, range(4, 6))
                for j in range(2):
                    ffn_silu(j, NFB - 1)

            def to(job):
                return bank[SEC.at[job][0]]

            def copy(job, dst, src):
                sec.ready(act, job)
                sec.moved(act.activation(dst, src, ACT.Copy), job)

            act.wait_ge(prm2_in, 16)
            act.activation(cs.rearrange("p k r -> p r k"), prm2[:, C2_C:C2_C + 2 * KD].rearrange("p (r k) -> p r k", r=2),
                           ACT.Silu).then_inc(silu_c, 1)

            def rounded_chunk(i, s):
                act.wait_ge(m_in[s], 16 * DEPTH * (2 if s < 2 else 1) + 16 * i + 16)
                for j in range(4):
                    at = slice(j * 1024, (j + 1) * 1024)
                    act.activation(ada_h[s % 2][:, at], m[:, s, at], ACT.Copy).then_inc(ada_hi, 1)

            act.wait_ge(block_used[1], B1 * DEPTH + 1)
            rounded_chunk(0, 0)
            act.wait_ge(drained[3], DEPTH * LAY.count[3] + 1)
            for t in range(NT):
                act.activation(xn2[:, t, :], x[:, t, :], ACT.Square, accum_out=ss[:, t:t + 1]).then_inc(ss_ready, 1)
            for s in range(1, 4):
                if s > 1:
                    sec.ready(act, f"ada{s - 2}", 0)
                rounded_chunk(0, s)
            with act.Fori(1, 3) as i:
                for s in range(4):
                    sec.ready(act, f"ada{(s + 2) % 4}", i if s >= 2 else i - 1)
                    rounded_chunk(i, s)
            act.wait_ge(x_ready, 2)
            act.wait_ge(ctx_in, 32)
            for n, (src, o) in enumerate(((ctx_x, 2), (x, 0))):
                act.wait_ge(ss_ready, 4 * DEPTH + 2 + 2 * n)
                for t in range(NT):
                    act.activation(xn2[:, t, :], src[:, t, :], ACT.Square, accum_out=ss[:, o + t:o + t + 1])\
                       .then_inc(ss_ready, 1)
            for n in range(4):
                copy(f"gate{n}", gb[:, n // 2, (n % 2) * 512:(n % 2 + 1) * 512], to(f"gate{n}")[:, :])

            def modulated(name, dst, kind, row):
                for n in range(4):
                    sec.ready(act, f"{name}{n}")
                    for k in range(2):
                        f = 2 * n + k
                        ins = act.activation(dst[:, f, :], to(f"{name}{n}")[:, k * T:(k + 1) * T], ACT.Identity,
                                             scale=modc[:, kind + 1, f, row:row + 1], bias=modc[:, kind, f, row:row + 1])
                    sec.moved(ins, f"{name}{n}")

            act.wait_ge(mod_ready, 1)
            modulated("tc", hC, 0, 1)
            modulated("tl", hT, 0, 0)
            act.wait_ge(zeros_ready, 1)
            for j in range(MH):
                copy(f"xm{j}", xmp[:, j, :, 1:1 + CTX], to(f"xm{j}")[:, :].rearrange("p (s t) -> p s t", s=2))
            for q in range(2):
                sec.ready(act, f"z{q}")
                sec.moved(act.activation(szT[:, 2 * q:2 * q + 2, :], to(f"z{q}")[:, :].rearrange("p (g t) -> p g t", g=2),
                                         ACT.Silu), f"z{q}")
            for j in range(MH):
                act.wait_ge(pre_ready, j + 1)
                act.activation(actT[:, j, :].rearrange("p (s t) -> p s t", s=2), pre[:, j % 2], ACT.Silu,
                               bias=prm2[:, C2_CONVB + j:C2_CONVB + j + 1]).then_inc(act_ready, 1)
            for n in range(12):
                if n % 3 < 2:
                    copy(f"qkv{n}", qkvT[:, n % 3, n // 3, :], to(f"qkv{n}")[:, :])
            sec.ready(act, "gates")
            act.activation(gi[0:ROWS, :], to("gates")[0:ROWS, :], ACT.Identity, bias=prm2[0:ROWS, C2_IG:C2_IG + 1])
            sec.moved(act.activation(gf[0:ROWS, :], to("gates")[64:64 + ROWS, :], ACT.Copy), "gates")
            act.wait_ge(f_abs, 1)
            act.activation(gx[0:ROWS, :], gx[0:ROWS, :], ACT.Exp).then_inc(f_log, 1)
            act.wait_ge(f_log, 1)
            act.activation(gx[0:ROWS, :], gx[0:ROWS, :], ACT.Ln, bias=1.0).then_inc(f_log, 1)
            for t in range(NT):
                copy(f"u{t}", u_rows[:, t, :], to(f"u{t}")[:, :])
            for g in range(4):
                copy(f"fp{g}", fP[:, g, :], to(f"fp{g}")[:, :])
            for p in range(2):
                copy(f"ff{p}", fT[:, 2 * p:2 * p + 2, :], to(f"ff{p}")[:, :].rearrange("p (g t) -> p g t", g=2))
            for p in range(2):
                copy(f"fy{p}", yT[:, 4 + 2 * p:6 + 2 * p, :], to(f"fy{p}")[:, :].rearrange("p (g t) -> p g t", g=2))
            sec.ready(act, "rT")
            act.activation(rcol, to("rT")[:, 0:4 * ROWS].rearrange("p (c r) -> p c r", c=4), ACT.Copy)
            sec.moved(act.activation(emn, to("rT")[:, 4 * ROWS:6 * ROWS].rearrange("p (t r) -> p t r", t=NT), ACT.Exp,
                                     scale=-1.0), "rT")
            sec.arrived(act, "rT")
            act.wait_ge(zeros_ready, 4)
            for h in range(MH):
                sec.ready(act, f"rb{h}")
                for d in range(2):
                    for c in range(4):
                        lo = P if (d, c) == (0, 3) else 0
                        hi = P if (d, c) == (1, 2) else T
                        ins = act.activation(E[:, h % 2, d, c, lo:hi], to(f"rb{h}")[:, d * T + lo:d * T + hi], ACT.Exp,
                                             scale=-1.0, bias=rcol[:, c, 32 * d + h:32 * d + h + 1])
                sec.moved(ins, f"rb{h}")
            for p in range(2):
                sec.ready(act, f"hT{p}")
                for g in range(2):
                    h = 2 * p + g
                    ins = act.activation(hm[:, h, :], to(f"hT{p}")[:, g * T:(g + 1) * T], ACT.Identity,
                                         scale=prm2[:, C2_NORM + h:C2_NORM + h + 1])
                sec.moved(ins, f"hT{p}")

            def result_squares(name):
                for n in range(4):
                    sec.ready(act, f"{name}{n}")
                    act.activation(xn2[:, n // 2, (n % 2) * 512:(n % 2 + 1) * 512], bank[n][:, :], ACT.Square,
                                   accum_out=ss[:, n:n + 1]).then_inc(ss_ready, 1)

            result_squares("wo")
            for t in range(NT):
                act.wait_ge(x_ready, 2 + t + 1)
                act.activation(xn2[:, t, :], x[:, t, :], ACT.Square, accum_out=ss[:, t:t + 1]).then_inc(ss_ready, 1)
            modulated("t2", h_rt, 2, 0)

            def rounded(q, c, subs=range(4)):
                act.wait_ge(piece_in[c % 4], 16 * (3 * q + c // 4) + 16)
                for j in subs:
                    at = slice(j * 1024, (j + 1) * 1024)
                    act.activation(w_h[:, c % 3, at], m[:, c % 4, at], ACT.Copy).then_inc(hi_ready, 1)

            for c in range(2):
                rounded(0, c)
            act.wait_ge(g_diff, 1)
            act.activation(ge, gd, ACT.Exp).then_inc(g_exp, 1)
            act.wait_ge(e_diff, 1)
            act.activation(t3, t3, ACT.Exp).then_inc(e_exp, 1)

            def gathered(name, side, c, n, at):
                sec.ready(act, name, at)
                for kk in range(2):
                    k = 2 * c + kk
                    ins = act.activation(xg_full[:, side, 1, k, :], to(name)[:, kk * T:(kk + 1) * T], ACT.Identity,
                                         scale=modc[:, 3, k, 0:1], bias=modc[:, 2, k, 0:1])
                    if kk == 0:
                        ins.then_inc(xg_moved, 1)
                sec.moved(ins, name)

            def rounded_tokens(name, side, c, n, at):
                act.wait_ge(xg_moved, n + 1)
                sec.arrived(act, name, at)
                act.activation(xg[:, side, 0, 2 * c:2 * c + 2, :], xg_full[:, side, 1, 2 * c:2 * c + 2, :], ACT.Copy)\
                    .then_inc(xg_rounded, 1)

            def choices(name, i, n):
                act.wait_ge(slot_ready, n + 1)
                sec.moved(act.activation(choice_t[:, i, :].rearrange("p (t q) -> p t q", t=NT),
                                         to(name)[:, 0:2 * (P + 4)].rearrange("p (t c) -> p t c", t=NT)[:, :, 0:P], ACT.Copy),
                          name)

            def expert_pass(q, i, final=False):
                p, side = QUAD * q + i, i // 2
                more = not (final and i >= 2)
                rounded(q, 3 * i + 2)
                sec.ready(act, "eG", 2 * p)
                sec.moved(act.activation(hidden, to("eG")[:, :], ACT.Silu), "eG")
                if not (final and i == QUAD - 1):
                    rounded(q, 3 * i + 3)
                sec.ready(act, "e6", 6 * q + HIDDEN_T[i])
                act.activation(aT2[:, 0].rearrange("p j s -> p (j s)"), to("e6")[:, :], ACT.Copy).then_inc(hidden_rounded, 1)
                up = not (final and i == QUAD - 1)
                for c in range(2):
                    if c and up:
                        rounded(q, 3 * i + 4, (0,))
                    if more:
                        tokens = "e7", 1 - side, 2 * (i % 2) + c, 2 * p + 4 + c, 10 * q + PIECES[i][c]
                        gathered(*tokens)
                        rounded_tokens(*tokens)
                act.wait_ge(slot_ready, p + 1)
                for c, name in enumerate(("eD0", "eD1")):
                    if up:
                        rounded(q, 3 * i + 4, ((1,), (2, 3))[c])
                    sec.ready(act, name, 2 * p)
                    act.activation(y2[:, 0, c * 512:(c + 1) * 512], to(name)[:, :], ACT.Copy, scale=slot_w[:, i:i + 1])\
                        .then_inc(y_rounded, 1)
                if more and i % 2:
                    for n, name in enumerate(("e6", "e7")):
                        choices(name, (i + 1 + n) % QUAD, p + 1 + n)

            for c in range(4):
                gathered(f"first{c}", 0, c, c, 0)
                rounded_tokens(f"first{c}", 0, c, c, 0)
            act.wait_ge(y_zero, 3)
            for n in range(2):
                choices(f"first_sT{n}", n, n)
            with act.Fori(0, NE // QUAD) as q:
                for i in range(QUAD):
                    expert_pass(q, i)
            act.wait_ge(table_ready, 1)
            with act.If(act.value_load(table_i[0:1, OVER:OVER + 1], min_val=0, max_val=OVER) > 0):
                for i in range(QUAD):
                    expert_pass(NE // QUAD, i, final=True)
            result_squares("ye")

        @block.vector
        def _(dve):
            dve.memset(half[:, :], -0.5).then_inc(half_ready, 1)
            dve.wait_ge(const_in, 16)
            with dve.Fori(0, DEPTH) as l:
                res = layer_results(l)
                S = Steps(dve, dve_step, l * DVE_STEPS)

                def to(job):
                    return bank[LAY.at[job][0]]

                def col(c):
                    return prm[:, c:c + 1]

                def norm(n):
                    for t in range(NT):
                        dve.wait_ge(rstd_ready, 4 * l + 2 * n + t + 1)
                        dve.tensor_scalar(xn[:, t, :], x[:, t, :], rstd[:, t:t + 1], None, ALU.mult).then_inc(xn_ready, 1)

                def gained_piece(name, gain, dst, n):
                    t, b = n // 2, n % 2
                    job = f"{name}_{t}{b}"
                    res.ready(dve, job)
                    g = prm[:, gain + 4 * b:gain + 4 * b + 4].unsqueeze(2).to_broadcast([P, 4, P])
                    res.moved(dve.tensor_tensor(dst[:, 4 * b:4 * b + 4, t * P:(t + 1) * P],
                                                to(job)[:, :].rearrange("p (k q) -> p k q", k=4), g, ALU.mult), job)

                norm(0)
                dve.wait_ge(prm_in, 48 * l + 48)
                for n in range(4):
                    gained_piece("tx1", C_GMIX, hT, n)
                for t in range(NT):
                    res.arrived(dve, f"kwi{t}")
                    z5 = zi[:, t, :].rearrange("p (h d) -> p h d", h=5)
                    hd = HD // 2
                    S.did(dve.tensor_tensor(ra, z5, cos2[:, t, :].unsqueeze(1).to_broadcast([P, 5, HD]), ALU.mult))
                    S.did(dve.tensor_tensor(rb[:, :, 0:hd], z5[:, :, hd:HD],
                                            sin2[:, t, 0:hd].unsqueeze(1).to_broadcast([P, 5, hd]), ALU.mult))
                    S.then(dve.tensor_tensor(rb[:, :, hd:HD], z5[:, :, 0:hd],
                                             sin2[:, t, hd:HD].unsqueeze(1).to_broadcast([P, 5, hd]), ALU.mult))
                    S.then(dve.tensor_tensor(ri[:, t, 0:5, :], ra, rb, ALU.add))
                    dve.tensor_copy(ri[:, t, 5, :], ri[:, t, 4, :]).then_inc(ri_ready, 1)
                def rest_in(n0, slot_of, h_of, subs):
                    for n in range(subs):
                        at = slice(n * 1024, (n + 1) * 1024)
                        dve.wait_ge(in_hi, IN_SUBS * l + n0 + n + 1)
                        dve.tensor_tensor(slot_of[0][:, at], slot_of[1][:, at], f32(h_of[:, at]), ALU.subtract).then_inc(in_lo, 1)

                rest_in(0, (fw_l[:, 0, :], blocks_w[:, 0, :]), fw_l[:, 1, :], 6)
                S.then(dve.memset(cpad[:, :, 0:LONG - 1], 0.0))
                res.ready(dve, "da")
                res.arrived(dve, "dg")
                res.moved(dve.tensor_tensor(cpad[:, :, LONG - 1:], to("da")[:, :].rearrange("p (g t) -> p g t", g=2), sig,
                                            ALU.mult), "da")
                res.arrived(dve, "da")
                tap_done = [0, 0]

                def taps(ws):
                    for w in ws:
                        for g in range(2):
                            c, shifted = col(C_LONG + 2 * w + g), cpad[:, g, w:w + T]
                            if w == 0:
                                ins = dve.tensor_scalar(conv[:, g, :], shifted, c, col(C_BCONF + g), ALU.mult, ALU.add)
                            else:
                                S.need(tap_done[g])
                                ins = dve.scalar_tensor_tensor(conv[:, g, :], shifted, c, conv[:, g, :], ALU.mult, ALU.add)
                            if (w, g) == (LONG - 1, 1):
                                ins.then_inc(conv_ready, 1)
                            else:
                                tap_done[g] = S.did(ins)

                taps(range(0, 13))
                rest_in(6, (w_l[:, 3, :], m[:, 3, :]), w_l[:, 2, :], 4)
                dve.wait_ge(h1_rounded, l + 1)
                res.ready(dve, "qk1")
                dve.tensor_tensor(h1_l[:, :, :], hT[:, :, :], f32(h1_h[:, :, :]), ALU.subtract).then_inc(h1_ready, 1)
                for t in range(NT):
                    for job in (f"sc{t}a", f"sc{t}b"):
                        res.arrived(dve, job)
                    for j in range(H):
                        w = wi[:, t, j:j + 1]
                        if j == 0:
                            ins = dve.tensor_scalar(score[t], rel[t][:, 0, :], w, None, ALU.mult)
                        else:
                            ins = dve.scalar_tensor_tensor(score[t], rel[t][:, j, :], w, score[t], ALU.mult, ALU.add)
                        if j < H - 1:
                            S.then(ins)
                    ins.then_inc(score_ready, 1)
                taps((13, 14))
                for t in range(NT):
                    dve.wait_ge(score_masked, 2 * l + t + 1)
                settle(dve, passed)
                for r in range(TOPK // 8):
                    src = score if r == 0 else work
                    for t in range(NT):
                        n = S.did(dve.max(mx[:, t, :], src[t]))
                    taps((15 + 2 * r,))
                    S.need(n)
                    settle(dve, passed)
                    for t in range(NT):
                        n = S.did(dve.match_replace(work[t], mx[:, t, :], src[t], TAKEN))
                    taps((16 + 2 * r,))
                    if r == 3:
                        for t in range(NT):
                            res.arrived(dve, f"guv{t}")
                            v_stats = S.did(dve.bn_stats(bnst[:, t, :], zg[:, t, G:2 * G]))
                    if r == 4:
                        S.need(v_stats)
                        settle(dve, passed)
                        for t in range(NT):
                            ins = dve.bn_aggr(bnag[:, t, :], bnst[:, t, :])
                        ins.then_inc(var_ready, 1)
                    if r == 6:
                        dve.wait_ge(norm_rstd, 2 * l + 1)
                        for t in range(NT):
                            dve.tensor_scalar(zg[:, t, G:2 * G], zg[:, t, G:2 * G], bnag[:, t, 0:1], rstd[:, 2 + t:3 + t],
                                              ALU.subtract, ALU.mult).then_inc(v_norm, 1)
                    S.need(n)
                    settle(dve, passed)
                for t in range(NT):
                    dve.tensor_scalar(sel[t], work[t], TAKEN, 1.0, ALU.is_equal, ALU.subtract).then_inc(sel_ready, 1)
                res.ready(dve, "cvT")
                for t in range(NT):
                    n = S.did(dve.bn_stats(bnst[:, 2 + t, :], to("cvT")[:, t * T:(t + 1) * T]))
                S.need(n)
                settle(dve, passed)
                for t in range(NT):
                    ins = dve.bn_aggr(bnag[:, 2 + t, :], bnst[:, 2 + t, :])
                ins.then_inc(var_ready, 1)
                S.then(dve.memset(chp[:, :, 0:SHORT - 1], 0.0))
                res.ready(dve, "ah")
                res.arrived(dve, "ac")
                res.moved(dve.tensor_tensor(chp[:, :, SHORT - 1:], to("ah")[:, :].rearrange("p (g t) -> p g t", g=2), acs,
                                            ALU.mult), "ah")
                res.arrived(dve, "ah")
                for w in range(SHORT):
                    for g in range(2):
                        c, shifted = col(C_SHORT + 2 * w + g), chp[:, g, w:w + T]
                        if w == 0:
                            n = S.did(dve.tensor_scalar(chy[:, g, :], shifted, c, None, ALU.mult))
                        else:
                            S.need(n - 1)
                            n = S.did(dve.scalar_tensor_tensor(chy[:, g, :], shifted, c, chy[:, g, :], ALU.mult, ALU.add))
                S.need(n)
                res.ready(dve, "ab")
                res.moved(dve.tensor_tensor(yT[:, 0:2, :], to("ab")[:, :].rearrange("p (g t) -> p g t", g=2), chy, ALU.mult), "ab")
                dve.wait_ge(norm_rstd, 2 * l + 2)
                for t in range(NT):
                    ins = dve.tensor_scalar(conv_n[:, t, :], to("cvT")[:, t * T:(t + 1) * T], bnag[:, 2 + t, 0:1],
                                            rstd[:, 4 + t:5 + t], ALU.subtract, ALU.mult)
                res.moved(ins, "cvT")

                def rest_of_mix(g, n):
                    dve.wait_ge(mix_rounded, 4 * l + n)
                    part = (slice(None), slice(2 * g, 2 * g + 2), slice(None))
                    dve.tensor_tensor(y_l[part], yT[part], f32(y_h[part]), ALU.subtract).then_inc(mix_ready, 1)

                for t in range(NT):
                    res.ready(dve, f"mix{t}")
                    yb = ycat[:, t, 0, :]
                    res.moved(dve.tensor_tensor(yb.rearrange("p (h d) -> p h d", h=H),
                                                to(f"mix{t}")[:, 0:G].rearrange("p (h d) -> p h d", h=H),
                                                prm[:, C_BS:C_BS + H].unsqueeze(2).to_broadcast([P, H, HD]), ALU.add), f"mix{t}")
                    res.arrived(dve, f"mix{t}")
                    dve.tensor_tensor(yb, yb, zg[:, t, 0:G], ALU.mult).then_inc(yb_ready, 1)
                rest_in(10, (w_l[:, 0, :], m[:, 0, :]), w_l[:, 2, :], 4)
                for n, g in enumerate((0, 1)):
                    rest_of_mix(g, n + 1)
                for t in range(NT):
                    dve.wait_ge(sel_masked, 2 * l + t + 1)
                    nk = (t + 1) * P
                    for job, h0 in ((f"lg{t}a", 0), (f"lg{t}b", 1)):
                        res.ready(dve, job)
                        res.moved(dve.scalar_tensor_tensor(lg[t][:, h0::2, :], sel[t].unsqueeze(1).to_broadcast([P, 2, nk]),
                                                           -NEG, to(job)[:, 0:2 * nk].rearrange("p (h s) -> p h s", h=2),
                                                           ALU.mult, ALU.add), job)
                        res.arrived(dve, job)
                    S.then(dve.tensor_reduce(nmx[:, t, :], lg[t], AX.X, ALU.max, negate=True))
                    dve.tensor_scalar(nms[:, t, :], nmx[:, t, :], HD ** -0.5, None, ALU.mult).then_inc(lg_ready, 1)
                rest_of_mix(3, 3)
                for t in range(NT):
                    dve.wait_ge(exp_ready, 8 * l + 4 * t + 4)
                    S.then(dve.reciprocal(rinv[:, t, :], rsum[:, t, :]))
                    res.ready(dve, f"av{t}")
                    res.moved(dve.tensor_tensor(ycat[:, t, 1, :].rearrange("p (h d) -> p h d", h=H),
                                                to(f"av{t}")[:, 0:G].rearrange("p (h d) -> p h d", h=H),
                                                rinv[:, t, :].unsqueeze(2).to_broadcast([P, H, HD]), ALU.mult), f"av{t}")

                def add_to_x(name):
                    for n in range(4):
                        res.ready(dve, f"{name}{n}")
                        part = x[:, n // 2, (n % 2) * 512:(n % 2 + 1) * 512]
                        res.moved(dve.tensor_tensor(part, part, bank[n][:, :], ALU.add), f"{name}{n}")

                def rest_of_block(slot, b, subs):
                    for n in subs:
                        at = slice(n * SUB, (n + 1) * SUB)
                        dve.wait_ge(ffn_hi, SUBS * (NFB * l + b) + n + 1)
                        dve.tensor_tensor(fw_l[:, slot, at], blocks_w[:, slot, at], f32(fw_h[:, 1 - slot, at]), ALU.subtract)\
                            .then_inc(ffn_lo, 1)

                rest_of_block(0, 0, range(0, 4))
                rest_of_mix(2, 4)
                add_to_x("wo")
                norm(1)
                def rest_of_h(n):
                    t, b = n // 2, n % 2
                    part = (slice(None), slice(4 * b, 4 * b + 4), slice(t * P, (t + 1) * P))
                    dve.wait_ge(h_rounded, 4 * l + n + 1)
                    dve.tensor_tensor(h_l[part], h_full[part], f32(h_h[part]), ALU.subtract).then_inc(h_ready, 1)

                for n in range(4):
                    gained_piece("tx2", C_GFFN, h_full, n)
                    if n:
                        rest_of_h(n - 1)
                rest_of_h(3)
                rest_of_block(0, 0, range(4, 6))

                def ffn_hidden(j, i):
                    dve.wait_ge(silu_ready, 2 * NFB * l + 2 * i + j + 1)
                    dve.tensor_tensor(sga[:, j, :], sga[:, j, :], to(f"gu{j}")[:, T:2 * T], ALU.mult).then_inc(a_step, 1)
                    dve.wait_ge(a_step, 4 * (NFB * l + i) + 2 * j + 1)
                    dve.tensor_copy(a2[:, 0, j, :], sga[:, j, :]).then_inc(a_step, 1)
                    dve.wait_ge(a_step, 4 * (NFB * l + i) + 2 * j + 2)
                    res.moved(dve.tensor_tensor(a2[:, 1, j, :], sga[:, j, :], f32(a2[:, 0, j, :]), ALU.subtract), f"gu{j}")

                with dve.Fori(0, B1) as r:
                    for s in range(2):
                        ffn_hidden(0, 2 * r + s)
                        rest_of_block(1 - s, 2 * r + s + 1, range(0, 4))
                        ffn_hidden(1, 2 * r + s)
                        rest_of_block(1 - s, 2 * r + s + 1, range(4, 6))
                for j in range(2):
                    ffn_hidden(j, NFB - 1)
                add_to_x("y")
                assert S.n == DVE_STEPS, S.n

            S = Steps(dve, dve_step, DEPTH * DVE_STEPS)

            def to(job):
                return bank[SEC.at[job][0]]

            def copy(job, dst, src):
                sec.ready(dve, job)
                sec.moved(dve.tensor_copy(dst, src), job)

            def normed(count, src, o):
                for t in range(NT):
                    dve.wait_ge(rstd_ready, 4 * DEPTH + count + t + 1)
                    dve.tensor_scalar(xn2[:, t, :], src[:, t, :], rstd[:, o + t:o + t + 1], None, ALU.mult).then_inc(xn_ready, 1)

            dve.wait_ge(silu_c, 1)
            dve.tensor_copy(cs2[:, 0], cs).then_inc(cs_ready, 1)
            dve.wait_ge(cs_ready, 1)
            dve.tensor_tensor(cs2[:, 1], cs, f32(cs2[:, 0]), ALU.subtract).then_inc(cs_ready, 1)

            def rest_of_chunk(i, s):
                for j in range(4):
                    at = slice(j * 1024, (j + 1) * 1024)
                    dve.wait_ge(ada_hi, 16 * i + 4 * s + j + 1)
                    dve.tensor_tensor(w_l[:, s, at], m[:, s, at], f32(ada_h[s % 2][:, at]), ALU.subtract).then_inc(ada_lo, 1)

            def add_rows(i, s):
                sec.ready(dve, f"ada{s}", i)
                part = modrow[:, bass.ds(2048 * i + 512 * s, 512)]
                sec.moved(dve.tensor_tensor(part, part, bank[s][0:2, :], ALU.add), f"ada{s}")

            rest_of_chunk(0, 0)
            dve.wait_ge(drained[3], DEPTH * LAY.count[3] + 1)
            dve.wait_ge(pos_in, 32)
            dve.wait_ge(rstd_ready, 4 * DEPTH + 2)
            for t in range(NT):
                S.then(dve.scalar_tensor_tensor(x[:, t, :], x[:, t, :], rstd[:, t:t + 1], gfin, ALU.mult, ALU.mult))
                dve.tensor_tensor(x[:, t, :], x[:, t, :], pos[:, t, :], ALU.add).then_inc(x_ready, 1)
            dve.wait_ge(rows_in, 32)
            with dve.Fori(0, 2) as i:
                for s in range(4):
                    rest_of_chunk(i + (s + 1) // 4, (s + 1) % 4)
                    add_rows(i, s)
            for s in range(4):
                if s < 3:
                    rest_of_chunk(2, s + 1)
                add_rows(2, s)
            for s in range(4):
                sec.arrived(dve, f"ada{s}", 2)
            for q in range(2):
                part = modrow[:, (2 + 3 * q) * D:(3 + 3 * q) * D]
                dve.tensor_tensor(part, part, gpost[:, q * D:(q + 1) * D], ALU.mult).then_inc(gate_rows, 1)
            copy("modT", modc.rearrange("p n k r -> p (n k r)"), to("modT")[:, 0:64])
            sec.arrived(dve, "modT")
            for kind, gain in ((1, C2_PREMIX), (3, C2_PREFFN)):
                S.then(dve.tensor_scalar(modc[:, kind], modc[:, kind], 1.0, None, ALU.add))
                ins = dve.tensor_tensor(modc[:, kind], modc[:, kind],
                                        prm2[:, gain:gain + KD].unsqueeze(2).to_broadcast([P, KD, 2]), ALU.mult)
                if kind == 1:
                    S.then(ins)
            ins.then_inc(mod_ready, 1)
            dve.wait_ge(rstd_ready, 4 * DEPTH + 6)
            normed(2, ctx_x, 2)
            sec.ready(dve, "tc3")
            normed(4, x, 0)
            for j in range(MH):
                sec.arrived(dve, f"xm{j}")
                if j >= 2:
                    dve.wait_ge(act_ready, j - 1)
                for w in range(3):
                    c, shifted = prm2[:, C2_CONV + 4 * w + j:C2_CONV + 4 * w + j + 1], xmp[:, j, :, w:w + CTX]
                    if w == 0:
                        S.then(dve.tensor_scalar(pre[:, j % 2], shifted, c, None, ALU.mult))
                    else:
                        ins = dve.scalar_tensor_tensor(pre[:, j % 2], shifted, c, pre[:, j % 2], ALU.mult, ALU.add)
                        if w == 1:
                            S.then(ins)
                ins.then_inc(pre_ready, 1)
            dve.wait_ge(zeros_ready, 2)
            for c in range(4):
                copy(f"vt{c}", vtok[:, c, :, 0:DH], to(f"vt{c}")[:, :].rearrange("p (h d) -> p h d", h=MH))
            for j in range(MH):
                n = 3 * j + 2
                copy(f"qkv{n}", qkvT[:, 2, j, :], to(f"qkv{n}")[:, :])
            sec.arrived(dve, "gates")
            S.then(dve.tensor_scalar(gf[0:ROWS, :], gf[0:ROWS, :], prm2[0:ROWS, C2_FG:C2_FG + 1], None, ALU.add))
            dve.scalar_tensor_tensor(gx[0:ROWS, :], gf[0:ROWS, :], -1.0, gf[0:ROWS, :], ALU.mult, ALU.min).then_inc(f_abs, 1)
            dve.wait_ge(f_log, 2)
            S.then(dve.scalar_tensor_tensor(gf[0:ROWS, :], gf[0:ROWS, :], 0.0, gx[0:ROWS, :], ALU.min, ALU.subtract))

            def scan(dst, src, op, start):
                S.did(dve.tensor_tensor_scan(dst[0:MH, :], src[0:MH, :], src[0:MH, :], start, op, ALU.bypass))
                b = slice(32, 32 + MH)
                S.then(dve.tensor_tensor_scan(dst[b, CTX - 1::-1], src[b, CTX - 1::-1], src[b, CTX - 1::-1], start, op, ALU.bypass))
                S.then(dve.tensor_tensor_scan(dst[b, S2 - 1:CTX - 1:-1], src[b, S2 - 1:CTX - 1:-1], src[b, S2 - 1:CTX - 1:-1],
                                              dst[b, 0:1], op, ALU.bypass))

            dve.wait_ge(zeros_ready, 3)
            scan(cum, gf, ALU.add, 0.0)
            S.then(dve.tensor_tensor(rr[0:ROWS, :], gi[0:ROWS, :], cum[0:ROWS, :], ALU.subtract))
            scan(rmax, rr, ALU.max, TAKEN)
            dve.tensor_tensor(cum[0:ROWS, CTX:S2], cum[0:ROWS, CTX:S2], rmax[0:ROWS, CTX:S2], ALU.add).then_inc(scan_ready, 1)
            def weigh(h):
                dve.wait_ge(e_masked, 4 * h + 4)
                for d in range(2):
                    for n, job in enumerate((f"qk{h}a", f"qk{h}b")):
                        if d == 0:
                            sec.ready(dve, job)
                        part = E[:, h % 2, d, 2 * n:2 * n + 2, :]
                        ins = dve.scalar_tensor_tensor(part.rearrange("p c t -> p (c t)"), to(job)[:, :], DH ** -0.5,
                                                       part.rearrange("p c t -> p (c t)"), ALU.mult, ALU.mult)
                        if d == 1:
                            sec.moved(ins, job)
                        elif n == 1:
                            ins.then_inc(s_ready, 1)

            def combine(h):
                for d in range(2):
                    job = f"o{h}{d}"
                    sec.ready(dve, job)
                    o = to(job)[:, 0:2 * (DH + 1)].rearrange("p (t c) -> p t c", t=NT)
                    S.then(dve.tensor_tensor(nq, o[:, :, DH], emn[:, :, 32 * d + h], ALU.max))
                    S.then(dve.scalar_tensor_tensor(nq, o[:, :, DH], -1.0, nq, ALU.mult, ALU.max))
                    S.then(dve.reciprocal(rq2, nq))
                    for t in range(NT):
                        dst = h_rows[:, t, h * DH:(h + 1) * DH]
                        if d == 0:
                            ins = dve.tensor_scalar(dst, o[:, t, 0:DH], rq2[:, t:t + 1], None, ALU.mult)
                        else:
                            ins = dve.scalar_tensor_tensor(dst, o[:, t, 0:DH], rq2[:, t:t + 1], dst, ALU.mult, ALU.add)
                    sec.moved(ins, job)
                    sec.arrived(dve, job)

            sec.arrived(dve, "rT")
            weigh(0)
            for h in range(MH):
                if h + 1 < MH:
                    weigh(h + 1)
                combine(h)
            for n in range(8):
                t, h = n // MH, n % MH
                S.then(dve.bn_stats(bst[:, n, :], h_rows[:, t, h * DH:(h + 1) * DH]))
                ins = dve.bn_aggr(bag[:, n, :], bst[:, n, :])
            ins.then_inc(h_var, 1)
            dve.wait_ge(h_rstd, 1)
            for n in range(8):
                t, h = n // MH, n % MH
                part = h_rows[:, t, h * DH:(h + 1) * DH]
                ins = dve.tensor_scalar(part, part, bag[:, n, 0:1], rstd[:, n:n + 1], ALU.subtract, ALU.mult)
            ins.then_inc(hn_ready, 1)
            for h in range(MH):
                sec.arrived(dve, f"hT{h // 2}")
                S.then(dve.scalar_tensor_tensor(hm[:, h, :], actT[:, h, CTX:S2], prm2[:, C2_SKIP + h:C2_SKIP + h + 1], hm[:, h, :],
                                                ALU.mult, ALU.add))
                dve.tensor_tensor(yT[:, h, :], hm[:, h, :], szT[:, h, :], ALU.mult).then_inc(y_ready, 1)

            def gated_add(name, count, q, done):
                halves = [slice(c * 512, (c + 1) * 512) for c in range(2)]
                for t in range(NT):
                    dve.wait_ge(rstd_ready, 4 * DEPTH + count + t + 1)
                    for c in range(2):
                        n = 2 * t + c
                        sec.moved(dve.scalar_tensor_tensor(tmp[:, n, :], bank[n][:, :], rstd[:, t:t + 1], gb[:, q, halves[c]],
                                                           ALU.mult, ALU.mult), f"{name}{n}")
                    for c in range(2):
                        n = 2 * t + c
                        sec.arrived(dve, f"{name}{n}")
                        ins = dve.tensor_tensor(x[:, t, halves[c]], x[:, t, halves[c]], tmp[:, n, :], ALU.add)
                        if done is out_ready or c:
                            ins.then_inc(done, 1)

            def rest_of_piece(q, c, subs=range(4)):
                for j in subs:
                    at = slice(j * 1024, (j + 1) * 1024)
                    dve.wait_ge(hi_ready, 48 * q + 4 * c + j + 1)
                    dve.tensor_tensor(w_l[:, c % 4, at], m[:, c % 4, at], f32(w_h[:, c % 3, at]), ALU.subtract).then_inc(lo_ready, 1)

            gated_add("wo", 6, 0, x_ready)
            normed(8, x, 0)
            for t in range(NT):
                dve.wait_ge(xn_ready, 4 * DEPTH + 4 + t + 1)
                S.then(dve.tensor_copy(xn_h[:, t, :], xn2[:, t, :]))
                S.did(dve.tensor_tensor(xn_l[:, t, :], xn2[:, t, :], f32(xn_h[:, t, :]), ALU.subtract))
            for i in range(QUAD):
                S.did(dve.tensor_copy(pick_w[:, i, 2:2 + P], ident))
            rest_of_piece(0, 0)
            dve.wait_ge(router_in, 32)
            for t in range(NT):
                sec.ready(dve, f"rt{t}")
                ins = dve.tensor_tensor(logit[:, t, :], to(f"rt{t}")[:, 0:NG + NE], b_rt, ALU.add)
                sec.moved(ins, f"rt{t}")
            for t in range(NT):
                sec.arrived(dve, f"rt{t}")

            def over(v, n):
                return v.unsqueeze(2).to_broadcast([P, NT, n])

            def first_max(dst, best, src, n):
                rank = const[:, K_RANK + NE - n:K_RANK + NE].unsqueeze(1).to_broadcast([P, NT, n])
                S.then(dve.tensor_reduce(best, src, AX.X, ALU.max))
                S.then(dve.tensor_tensor(dst, src, over(best, n), ALU.is_equal))
                S.then(dve.tensor_tensor(dst, dst, rank, ALU.mult))
                S.then(dve.tensor_reduce(t4, dst, AX.X, ALU.max))
                S.then(dve.tensor_tensor(dst, dst, over(t4, n), ALU.is_equal))

            first_max(gsel, t1, logit[:, :, 0:NG], NG)
            dve.tensor_tensor(gd, logit[:, :, 0:NG], over(t1, NG), ALU.subtract).then_inc(g_diff, 1)
            el = expert_l[:, :, 0:NE]
            by_group = "p t (g e) -> p t g e"
            for t in range(NT):
                S.then(dve.tensor_tensor(el[:, t].rearrange("p (g e) -> p g e", g=NG),
                                         logit[:, t, NG:].rearrange("p (g e) -> p g e", g=NG),
                                         gsel[:, t].unsqueeze(2).to_broadcast([P, NG, EPG]), ALU.mult))
            S.then(dve.tensor_scalar(gsel, gsel, 1.0, -NEG, ALU.subtract, ALU.mult))
            for t in range(NT):
                S.then(dve.tensor_tensor(el[:, t].rearrange("p (g e) -> p g e", g=NG), el[:, t].rearrange("p (g e) -> p g e", g=NG),
                                         gsel[:, t].unsqueeze(2).to_broadcast([P, NG, EPG]), ALU.add))
            p1, p2 = pick1[:, :, 0:NE], pick2[:, :, 0:NE]
            first_max(p1, t1, el, NE)
            S.then(dve.scalar_tensor_tensor(el, p1, 2 * NEG, el, ALU.mult, ALU.add))
            first_max(p2, t2, el, NE)
            dve.tensor_tensor(chosen, p1, p2, ALU.add).then_inc(chosen_ready, 1)
            dve.tensor_tensor(t3, t2, t1, ALU.subtract).then_inc(e_diff, 1)
            dve.wait_ge(g_exp, 1)
            dve.wait_ge(e_diff, 1)
            S.then(dve.tensor_reduce(t1, ge, AX.X, ALU.add))
            S.then(dve.reciprocal(t1, t1))
            dve.wait_ge(e_exp, 1)
            S.then(dve.tensor_scalar(t2, t3, 1.0, None, ALU.add))
            S.then(dve.reciprocal(t2, t2))
            S.then(dve.tensor_tensor(t1, t1, t2, ALU.mult))
            S.then(dve.tensor_tensor(t2, t3, t1, ALU.mult))
            dve.wait_ge(chosen_ready, 1)
            S.then(dve.tensor_tensor(p1, p1, over(t1, NE), ALU.mult))
            S.then(dve.tensor_tensor(p2, p2, over(t2, NE), ALU.mult))
            S.then(dve.tensor_tensor(comb[:, :, 0:NE], p1, p2, ALU.add))
            sec.ready(dve, "rank")
            S.then(dve.scalar_tensor_tensor(place[:, :, 0:NE], to("rank")[:, 0:2 * NE].rearrange("p (t e) -> p t e", t=NT), 1.0,
                                            chosen, ALU.add, ALU.mult))

            def split_weights(e):
                S.then(dve.tensor_copy(comb_h[:, :, e], comb[:, :, e]))
                S.then(dve.tensor_tensor(comb_l[:, :, e], comb[:, :, e], f32(comb_h[:, :, e]), ALU.subtract))

            split_weights(slice(0, NE))

            def choose(e, i, side):
                for n in range(2):
                    for t in range(NT):
                        dve.tensor_scalar(choice[:, side, t, n * P:(n + 1) * P], const[:, K_SLOT:K_SLOT + P],
                                                place[:, t, bass.ds(e + n, 1)], None, ALU.is_equal)
                        for part, src in enumerate((f32(comb_h[:, :, :]), comb_l)):
                            at = P + 2 - t * (P + 2) + part
                            ins = dve.tensor_copy(pick_w[:, i + n, at:at + 1], src[:, t, bass.ds(e + n, 1)])
                ins.then_inc(choice_ready, 1)

            def slot_weights(name, at, i, n):
                sec.ready(dve, name, at)
                dve.tensor_reduce(slot_w[:, i:i + 1], to(name)[:, P:P + 4], AX.X, ALU.add).then_inc(slot_ready, 1)

            def rest_of_tokens(side, c, n):
                dve.wait_ge(xg_rounded, n + 1)
                at = slice(2 * c, 2 * c + 2)
                dve.tensor_tensor(xg[:, side, 1, at, :], xg_full[:, side, 1, at, :], f32(xg[:, side, 0, at, :]),
                                  ALU.subtract).then_inc(xg_ready, 1)

            def expert_pass(q, i, final=False):
                p, side = QUAD * q + i, i // 2
                more = not (final and i >= 2)
                rest_of_piece(q, 3 * i + 2)
                if i % 2 and not final:
                    choose(p + 3, (i + 3) % QUAD, side)
                ahead = not (final and i == QUAD - 1)

                def ahead_of(c, *subs):
                    if ahead:
                        rest_of_piece(q, 3 * i + c, subs)

                def tokens(c):
                    if more:
                        rest_of_tokens(1 - side, 2 * (i % 2) + c, 2 * p + 4 + c)

                ahead_of(3, 0, 1)
                sec.arrived(dve, "eG", 2 * p)
                sec.ready(dve, "eU", 2 * p)
                sec.moved(dve.tensor_tensor(hidden, hidden, to("eU")[:, :], ALU.mult), "eU")
                ahead_of(3, 2)
                dve.wait_ge(hidden_rounded, p + 1)
                sec.moved(dve.tensor_tensor(aT2[:, 1].rearrange("p j s -> p (j s)"), to("e6")[:, :],
                                            f32(aT2[:, 0].rearrange("p j s -> p (j s)")), ALU.subtract), "e6")
                ahead_of(3, 3)
                tokens(0)
                ahead_of(4, 0)
                tokens(1)
                dve.wait_ge(slot_ready, p + 1)
                ahead_of(4, 1)
                for c, name in enumerate(("eD0", "eD1")):
                    if c:
                        ahead_of(4, 2)
                        if more and i % 2:
                            for n, (bank_, at) in enumerate((("e6", 6 * q + CHOSEN_T6[i]), ("e7", 10 * q + CHOSEN_T7[i]))):
                                slot_weights(bank_, at, (i + 1 + n) % QUAD, p + 1 + n)
                        ahead_of(4, 3)
                    dve.wait_ge(y_rounded, 2 * p + c + 1)
                    at = slice(c * 512, (c + 1) * 512)
                    sec.moved(dve.scalar_tensor_tensor(y2[:, 1, at], to(name)[:, :], slot_w[:, i:i + 1], f32(y2[:, 0, at]),
                                                       ALU.mult, ALU.subtract), name)

            choose(0, 0, 0)
            sec.moved(dve.tensor_scalar(over_e, to("rank")[:, 2 * NE:3 * NE], P + 0.5, None, ALU.is_gt), "rank")
            rest_of_piece(0, 1)
            for c in range(4):
                rest_of_tokens(0, c, c)
            for n in range(2):
                slot_weights(f"first_sT{n}", 0, n, n)
            choose(2, 2, 1)
            sec.arrived(dve, "rank")
            S.then(dve.tensor_tensor_scan(over_n, over_e, over_e, 0.0, ALU.add, ALU.bypass))
            for n in range(OVER):
                S.then(dve.scalar_tensor_tensor(over_1, over_n, n + 1.0, over_e, ALU.is_equal, ALU.mult))
                which = over_1.unsqueeze(1).to_broadcast([P, NT, NE])
                S.then(dve.scalar_tensor_tensor(over_t, place[:, :, 0:NE], -float(P), which, ALU.add, ALU.mult))
                S.then(dve.tensor_reduce(place[:, :, NE + n], over_t, AX.X, ALU.add))
                S.then(dve.tensor_tensor(over_t, comb[:, :, 0:NE], which, ALU.mult))
                S.then(dve.tensor_reduce(comb[:, :, NE + n], over_t, AX.X, ALU.add))
                S.then(dve.tensor_tensor(over_1, over_1, const[:, K_RANK:K_RANK + NE], ALU.mult))
                S.then(dve.tensor_reduce(table[:, n:n + 1], over_1, AX.X, ALU.add))
            S.then(dve.tensor_scalar(table[:, 0:OVER], table[:, 0:OVER], 1.0, -1.0, ALU.max, ALU.mult))
            S.did(dve.tensor_scalar(table[:, 0:OVER], table[:, 0:OVER], float(NE), None, ALU.add))
            S.then(dve.tensor_copy(table[:, OVER:OVER + 1], over_n[:, NE - 1:NE]))
            dve.tensor_copy(table_i[:, :], table).then_inc(table_ready, 1)
            split_weights(slice(NE, NPASS))
            with dve.Fori(0, NE // QUAD) as q:
                for i in range(QUAD):
                    expert_pass(q, i)
            with dve.If(dve.value_load(table_i[0:1, OVER:OVER + 1], min_val=0, max_val=OVER) > 0):
                for i in range(QUAD):
                    expert_pass(NE // QUAD, i, final=True)
            gated_add("ye", 10, 1, out_ready)

        @block.gpsimd
        def _(pool):
            for n in range(8):
                pool.sem_inc(drained[n], 1)
            pool.sem_inc(block_used[1], 1)
            pool.wait_ge(half_ready, 1)
            pool.wait_ge(const_in, 16)

            def root(S, dst, src, n, scale, eps, ready):
                v = ms[:, dst:dst + n]
                settle(pool, passed)
                if scale is None:
                    S.then(pool.tensor_scalar(v, src, eps, None, ALU.add))
                else:
                    S.then(pool.tensor_scalar(v, src, scale, eps, ALU.mult, ALU.add))
                pool.tensor_tensor(rstd[:, dst:dst + n], v, half[:, 0:n], ALU.pow).then_inc(ready, 1)

            def row_roots(S, count, o=0):
                for t in range(NT):
                    pool.wait_ge(ss_ready, count + t + 1)
                    root(S, o + t, ss[:, o + t:o + t + 1], 1, 1.0 / D, EPS, rstd_ready)

            with pool.Fori(0, DEPTH) as l:
                res = layer_results(l)
                S = Steps(pool, pool_step, l * POOL_STEPS)
                row_roots(S, 4 * l)
                pool.wait_ge(prm_in, 48 * l + 48)
                settle(pool, passed)
                pool.affine_select(out=wsT, in_=wsT, pattern=[[0, H], [1, P]], compare_op=ALU.is_ge, fill=0.0, base=0,
                                   channel_multiplier=-1).then_inc(ws_ready, 1)
                for t in range(NT):
                    res.arrived(pool, f"qk{t}")
                    z8 = zq[:, t, :].rearrange("p (h d) -> p h d", h=8)
                    hd = HD // 2
                    S.did(pool.tensor_tensor(ga, z8, cos2[:, t, :].unsqueeze(1).to_broadcast([P, 8, HD]), ALU.mult))
                    S.did(pool.tensor_tensor(gc[:, :, 0:hd], z8[:, :, hd:HD],
                                             sin2[:, t, 0:hd].unsqueeze(1).to_broadcast([P, 8, hd]), ALU.mult))
                    S.then(pool.tensor_tensor(gc[:, :, hd:HD], z8[:, :, 0:hd],
                                              sin2[:, t, hd:HD].unsqueeze(1).to_broadcast([P, 8, hd]), ALU.mult))
                    pool.tensor_tensor(rq[:, t], ga, gc, ALU.add).then_inc(rq_ready, 1)
                    pool.wait_ge(rq_ready, 2 * l + t + 1)
                for t in range(NT):
                    pool.wait_ge(score_ready, 2 * l + t + 1)
                    settle(pool, passed)
                    part = score[t][:, t * P:(t + 1) * P]
                    pool.affine_select(out=part, in_=part, pattern=[[-1, P]], compare_op=ALU.is_ge, fill=NEG, base=0,
                                       channel_multiplier=1).then_inc(score_masked, 1)
                pool.wait_ge(var_ready, 2 * l + 1)
                root(S, 2, bnag[:, 0:2, 1], 2, None, LN_EPS, norm_rstd)

                def rest_of_w_out(subs):
                    for n in subs:
                        at = slice(n * 1024, (n + 1) * 1024)
                        pool.wait_ge(in_hi, IN_SUBS * l + 14 + n + 1)
                        settle(pool, passed)
                        pool.tensor_tensor(w_l[:, 1, at], m[:, 1, at], f32(w_l[:, 3, at]), ALU.subtract).then_inc(out_lo, 1)

                rest_of_w_out((0,))
                for t in range(NT):
                    pool.wait_ge(v_norm, 2 * l + t + 1)
                    v = zg[:, t, G:2 * G]
                    S.then(pool.tensor_tensor(v, v, lnrow[:, 0, :], ALU.mult))
                    pool.tensor_tensor(v, v, lnrow[:, 1, :], ALU.add).then_inc(v_ready, 1)
                for t in range(NT):
                    pool.wait_ge(sel_ready, 2 * l + t + 1)
                    settle(pool, passed)
                    part = sel[t][:, t * P:(t + 1) * P]
                    pool.affine_select(out=part, in_=part, pattern=[[-1, P]], compare_op=ALU.is_ge, fill=-1.0, base=0,
                                       channel_multiplier=1).then_inc(sel_masked, 1)
                pool.wait_ge(var_ready, 2 * l + 2)
                root(S, 4, bnag[:, 2:4, 1], 2, None, LN_EPS, norm_rstd)
                rest_of_w_out((1, 2, 3))
                row_roots(S, 4 * l + 2)
                assert S.n == POOL_STEPS, S.n

            S = Steps(pool, pool_step, DEPTH * POOL_STEPS)
            N = 4 * DEPTH
            row_roots(S, N)
            row_roots(S, N + 2, 2)
            row_roots(S, N + 4)
            sec.ready(pool, "modT")
            S.then(pool.memset(xmp[:, :, :, 0:1], 0.0))
            pool.memset(xmp[:, :, :, CTX + 1:CTX + 2], 0.0).then_inc(zeros_ready, 1)
            sec.arrived(pool, "gate3")
            S.then(pool.memset(cum[0:ROWS, :], 0.0))
            S.then(pool.memset(rmax[0:ROWS, :], 0.0))
            pool.memset(vtok[:, :, :, DH:DH + 1], 1.0).then_inc(zeros_ready, 1)
            S.then(pool.memset(nq, 0.0))
            pool.memset(rq2, 0.0).then_inc(zeros_ready, 1)
            sec.ready(pool, "u1")
            S.then(pool.memset(E[:, :, 0, 3, 0:P], 0.0))
            pool.memset(E[:, :, 1, 2, P:T], 0.0).then_inc(zeros_ready, 1)
            for h in range(MH):
                sec.arrived(pool, f"rb{h}")
                for d in range(2):
                    for c in (2, 3):
                        part = E[:, h % 2, d, c, (c - 2) * P:(c - 1) * P]
                        s = 1 if d == 0 else -1
                        pool.affine_select(out=part, in_=part, pattern=[[s, P]], compare_op=ALU.is_ge, fill=0.0, base=0,
                                           channel_multiplier=-s).then_inc(e_masked, 1)
            pool.wait_ge(h_var, 1)
            root(S, 0, bag[:, :, 1], 8, None, EPS, h_rstd)

            def result_root(count):
                for t in range(NT):
                    pool.wait_ge(ss_ready, N + count + 2 * t + 2)
                    S.then(pool.tensor_tensor(ms[:, 6 + t:7 + t], ss[:, 2 * t:2 * t + 1], ss[:, 2 * t + 1:2 * t + 2], ALU.add))
                    root(S, t, ms[:, 6 + t:7 + t], 1, 1.0 / D, EPS, rstd_ready)

            result_root(6)
            row_roots(S, N + 10)
            sec.ready(pool, "wo3")
            pool.tensor_scalar(y2[:, 0, :], half[:, 0:1].to_broadcast([P, D]), 0.0, None, ALU.mult).then_inc(y_zero, 1)
            pool.tensor_scalar(y2[:, 1, :], half[:, 0:1].to_broadcast([P, D]), 0.0, None, ALU.mult).then_inc(y_zero, 1)
            pool.tensor_scalar(choice_t[:, QUAD - 1, :], half[:, 0:1].to_broadcast([P, T]), 0.0, None, ALU.mult)\
                .then_inc(y_zero, 1)
            result_root(12)


def constants():
    c = np.zeros((P, N_CONST), np.float64)
    c[:, K_ID:K_ID + P] = np.eye(P)
    angle = np.arange(T, dtype=np.float32)[:, None] * (np.float32(ROPE_THETA) ** (-np.arange(0, HD, 2, dtype=np.float32) / HD))
    angle = angle.astype(np.float32).astype(np.float64).reshape(NT, P, HD // 2).transpose(1, 0, 2)
    cos, sin = np.cos(angle), np.sin(angle)
    c[:, K_COS:K_COS + 2 * HD] = np.concatenate([cos, cos], -1).reshape(P, -1)
    c[:, K_SIN:K_SIN + 2 * HD] = np.concatenate([-sin, sin], -1).reshape(P, -1)
    w = 2 * np.pi * (np.outer(np.arange(P), np.arange(P)) % P) / P
    c[:, K_CC:K_CC + P] = np.cos(w) / P ** 0.5
    c[:, K_SC:K_SC + P] = -np.sin(w) / P ** 0.5
    w = 2 * np.pi * (np.outer(np.arange(T), np.arange(T)) % T) / T
    w = np.concatenate([np.cos(w), np.sin(w)], 1) / T ** 0.5
    c[:, K_DFT:K_RANK] = w.reshape(NT, P, 2 * T).transpose(1, 0, 2).reshape(P, -1)
    c[:, K_RANK:K_SLOT] = np.arange(NE, 0, -1)
    c[:, K_SLOT:K_BEFORE] = np.arange(1, P + 1)
    c[:, K_BEFORE:K_ONES] = np.triu(np.ones((P, P)), 1)
    c[:, K_ONES:] = 1
    quarter = D // 4
    freq = (1.0 / (np.float32(POS_BASE) ** (np.arange(quarter, dtype=np.float32) / np.float32(quarter)))).astype(np.float32)

    def table(n):
        v = (np.arange(n, dtype=np.float32)[:, None] * freq).astype(np.float64)
        return np.concatenate([np.sin(v), np.cos(v)], -1)

    rows = T // GRID_W
    pos = np.concatenate([np.repeat(table(rows), GRID_W, 0), np.tile(table(GRID_W), (rows, 1))], -1)
    return c.astype(np.float32), by_partition(pos.astype(np.float32))


def by_partition(w):
    *lead, k, n = w.shape
    w = w.reshape(*lead, k // P, P, n)
    return np.ascontiguousarray(np.moveaxis(w, -3, -2)).reshape(*lead, P, k // P * n)


def columns(*vectors):
    return np.concatenate([np.swapaxes(v.reshape(-1, P), 0, 1) for v in vectors], 1)


def layouts(i):
    cuts = np.cumsum([256] * 9 + [64, 4, 256, 256])[:-1]
    ab, ac, ah, gu, gv, q, k, v, qi, ki, wi, da, dg = np.split(i["w_in"], cuts, axis=2)
    groups = {"vqi": (v, qi), "kwi": (ki, wi), "dadg": (da, dg), "qk": (q, k), "guv": (gu, gv), "abac": (ab, ac), "ah": (ah,)}
    a = {}
    a["x"] = i["x"][0]
    a["w_in"] = np.concatenate([by_partition(np.concatenate(groups[n], 2)) for n in IN_COLS], 2)
    a["prm"] = np.stack([np.concatenate([
        columns(i["g_mix"][l], i["g_ffn"][l], i["w_conv_a"][l], i["w_conf"][l], i["b_conf"][l], i["conf_ln_g"][l],
                i["conf_ln_b"][l]), i["b_s"][l].T], 1) for l in range(DEPTH)])
    a["gmlp_ln"] = np.concatenate([i["gmlp_ln_g"], i["gmlp_ln_b"]], 1)
    a["w_s"] = i["w_s"].transpose(0, 3, 1, 2).reshape(DEPTH, P, H * P)
    a["w_out"] = by_partition(i["w_out"])

    def in_blocks(w, n):
        *lead, k, c = w.shape
        return by_partition(np.moveaxis(w.reshape(*lead, k, c // n, n), -2, -3))

    a["ffn"] = np.concatenate([in_blocks(i["w_gate"], FB), in_blocks(i["w_up"], FB),
                               by_partition(i["w_down"].reshape(DEPTH, NFB, FB, D))], 3)
    a["g_final"] = i["g_final"]
    pad = np.zeros((P, 2), np.float32)
    for d, name in enumerate(("b_if_fwd_2", "b_if_bwd_2")):
        for q in range(2):
            pad[32 * d:32 * d + MH, q] = i[name][0, q * MH:(q + 1) * MH]
    a["prm2"] = np.concatenate([columns(i["g_pre_mix_2"], i["g_pre_ffn_2"], i["conv_w_2"], i["conv_b_2"], i["mlstm_norm_w_2"],
                                        i["mlstm_skip_2"], i["c_2"], i["c_ctx_2"]), pad], 1)
    a["w_ada"] = in_blocks(i["w_ada_2"][0], 512).reshape(3, 4, P, 4096)
    a["b_ada"] = i["b_ada_2"][0]
    a["g_post"] = np.concatenate([i["g_post_mix_2"][0], i["g_post_ffn_2"][0]])
    a["ctx"] = i["ctx_2"][0]
    a["w_in_2"] = in_blocks(i["w_in_2"][0], 512)
    n = P // 4
    bd = np.zeros((3, MH, n, 4, n, 4), np.float32)
    for q, name in enumerate(("w_q_2", "w_k_2", "w_v_2")):
        for b in range(n):
            bd[q, :, b, :, b, :] = i[name][0].reshape(MH, n, 4, 4)[:, b]
    w_if = np.zeros((12, P, P), np.float32)
    for d, name in enumerate(("w_if_fwd_2", "w_if_bwd_2")):
        for q in range(2):
            w_if[:, :, 64 * q + 32 * d:64 * q + 32 * d + MH] = i[name][0].reshape(12, P, 2, MH)[:, :, q]
    a["heads_2"] = np.concatenate([bd.reshape(12, P, P), w_if, i["w_fourier_2"][0]]).transpose(1, 0, 2).reshape(P, -1)
    a["w_out_2"] = by_partition(i["w_out_2"][0])
    a["w_router"] = by_partition(np.concatenate([i["w_router_group_2"][0], i["w_router_expert_2"][0]], 1))
    a["b_router"] = np.concatenate([i["b_router_group_2"][0], i["b_router_expert_2"][0]])
    a["experts"] = np.concatenate([by_partition(i["w_gate_2"][0]), by_partition(i["w_up_2"][0]), by_partition(i["w_down_2"][0])], 2)
    a["const"], a["pos"] = constants()
    return {f"in_{k}": np.ascontiguousarray(v) for k, v in a.items()}


def kernel(**inputs):
    import concourse.bacc as bacc
    from concourse.bass_utils import run_bass_kernel_spmd

    arrays = layouts({k: np.asarray(v) for k, v in inputs.items()})
    nc = bacc.Bacc("TRN2", target_bir_lowering=False, num_devices=1)
    args = {n[3:]: nc.dram_tensor(n, v.shape, F32, kind="ExternalInput").ap() for n, v in arrays.items()}
    out = nc.dram_tensor("out", (T, D), F32, kind="ExternalOutput").ap()
    build(nc, args, out)
    return run_bass_kernel_spmd(nc, [arrays], core_ids=[0]).results[0]["out"].reshape(1, T, D)
```

```python
from contextlib import ExitStack

import numpy as np

import concourse.bass as bass
from concourse import mybir

F32, F32R, I32 = mybir.dt.float32, mybir.dt.float32r, mybir.dt.int32
ALU = mybir.AluOpType
ACT = mybir.ActivationFunctionType
AX = mybir.AxisListType

P = 128
T = 256
NT = T // P
D = 1024
KD = D // P
DEPTH = 2
G = 256
H = 4
HD = G // H
TOPK = 64
SHORT, LONG = 3, 31
FFN = 2816
FB = 256
NFB = FFN // FB
NEG = -1e30
TAKEN = -3e38
EPS, LN_EPS = 1e-6, 1e-5

CTX = 256
S2 = CTX + T
MW = 512
MH = 4
DH = MW // MH
NMOD = 6
ADA = 6
NE, EPG, NG = 16, 4, 4
DE = 512
QUAD = 4
OVER = QUAD
NPASS = NE + OVER
GRID_W, POS_BASE, ROPE_THETA = 64, 10000.0, 10000.0

C_GMIX, C_GFFN, C_SHORT = 0, KD, 2 * KD
C_LONG = C_SHORT + 2 * SHORT
C_BCONF = C_LONG + 2 * LONG
C_LNG, C_LNB, C_BS = C_BCONF + 2, C_BCONF + 4, C_BCONF + 6
N_PRM = C_BS + H
C2_PREMIX, C2_PREFFN, C2_CONV = 0, KD, 2 * KD
C2_CONVB = C2_CONV + 3 * MH
C2_NORM, C2_SKIP, C2_C = C2_CONVB + MH, C2_CONVB + 2 * MH, C2_CONVB + 3 * MH
C2_IG, C2_FG = C2_C + 2 * KD, C2_C + 2 * KD + 1
N_PRM2 = C2_FG + 1
ROWS = 32 + MH
K_ID, K_COS, K_SIN = 0, P, P + 2 * HD
K_CC = K_SIN + 2 * HD
K_SC = K_CC + P
K_DFT = K_SC + P
K_RANK = K_DFT + NT * 2 * T
K_SLOT = K_RANK + NE
K_BEFORE = K_SLOT + P
K_ONES = K_BEFORE + P
N_CONST = K_ONES + P

IN_COLS = {"vqi": 512, "kwi": 68, "dadg": 512, "qk": 512, "guv": 512, "abac": 512, "ah": 256}
IN_AT = dict(zip(IN_COLS, np.cumsum([0] + [KD * w for w in IN_COLS.values()])[:-1].tolist()))
BLOCK = 3 * KD * FB
GU = 2 * KD * FB
SUBS, SUB = 6, BLOCK // 6

TAPS_FIRST = 18
IN_SUBS = 18
DVE_STEPS, POOL_STEPS = 123, 14
N_SCRATCH = 13400


class Banks:

    def __init__(self):
        self.count, self.at = [0] * 8, {}

    def add(self, bank, *names, times=1):
        for name in names:
            self.at[name] = (bank, self.count[bank])
            self.count[bank] += times


def layer_banks():
    b = Banks()
    for bank, name in [
        (0, "tx1_00"), (1, "tx1_01"), (2, "tx1_10"), (3, "tx1_11"), (4, "vqi0"), (5, "vqi1"), (6, "kwi0"),
        (7, "kwi1"), (0, "da"), (1, "dg"), (2, "riT0"), (3, "riT1"), (4, "qk0"), (5, "qk1"), (2, "sc0a"),
        (0, "sc0b"), (3, "sc1a"), (6, "sc1b"), (7, "guv0"), (6, "guv1"), (0, "cvT"), (1, "ab"), (4, "ac"), (5, "ah"),
        (2, "rqT0"), (3, "rqT1"), (6, "mix0"), (7, "mix1"), (4, "lg0a"), (2, "lg0b"), (5, "lg1a"), (6, "lg1b"), (0, "ybT"),
        (7, "cnT"), (0, "wo0"), (1, "wo1"), (2, "wo2"), (3, "wo3"), (7, "pT0"), (4, "pT1a"), (5, "pT1b"),
        (6, "av0"), (7, "av1"), (4, "ycT"), (4, "tx2_00"), (5, "tx2_01"), (6, "tx2_10"), (7, "tx2_11"),
    ]:
        b.add(bank, name)
    b.add(4, "gu0", times=NFB)
    b.add(5, "gu1", times=NFB)
    for n in range(4):
        b.add(n, f"y{n}")
    return b


def second_banks():
    b = Banks()
    for s in range(ADA):
        b.add(s, f"ada{s}", times=NMOD * D // 512 // ADA)
    b.add(6, "modT")
    for s in range(4):
        b.add(s, f"gate{s}")
    for n in range(4):
        b.add(4 + n, f"tc{n}")
    for n in range(4):
        b.add(n, f"tl{n}")
    for j in range(4):
        b.add(4 + j, f"xm{j}")
    b.add(0, "z0")
    b.add(1, "z1")
    for n in range(4):
        b.add(n, f"vt{n}")
    for n in range(12):
        b.add(4 + n % 4, f"qkv{n}")
    b.add(4, "gates")
    b.add(2, "u0")
    b.add(3, "u1")
    for g in range(4):
        b.add(g, f"fp{g}")
    b.add(6, "ff0")
    b.add(7, "ff1")
    b.add(6, "fy0")
    b.add(7, "fy1")
    b.add(5, "rT")
    for h in range(MH):
        b.add(6 + h % 2, f"rb{h}")
        b.add(2 * (h % 2), f"qk{h}a")
        b.add(2 * (h % 2) + 1, f"qk{h}b")
        b.add(4, f"o{h}0")
        b.add(5, f"o{h}1")
    for n in range(4):
        b.add(n, f"wo{n}")
    b.add(6, "hT0")
    b.add(7, "hT1")
    for n in range(4):
        b.add(4 + n, f"t2{n}")
    b.add(0, "rt0")
    b.add(1, "rt1")
    b.add(2, "rank")
    for n in range(4):
        b.add(4 + n, f"first{n}")
    b.add(6, "first_sT0")
    b.add(7, "first_sT1")
    b.add(4, "eG")
    b.add(4, "eD0", times=2 * NPASS - 1)
    b.add(5, "eU")
    b.add(5, "eD1", times=2 * NPASS - 1)
    b.add(6, "e6", times=6 * NPASS // QUAD)
    b.add(7, "e7", times=10 * NPASS // QUAD)
    for n in range(4):
        b.add(n, f"ye{n}")
    return b



LAY, SEC = layer_banks(), second_banks()


class Results:

    def __init__(self, filled, drained, plan, base):
        self.filled, self.drained, self.plan, self.base = filled, drained, plan, base

    def index(self, name, i):
        bank, n = self.plan.at[name]
        return bank, self.base[bank] + n + i

    def room(self, eng, name, i=0):
        bank, n = self.index(name, i)
        eng.wait_ge(self.drained[bank], n + 1)

    def done(self, ins, name):
        ins.then_inc(self.filled[self.plan.at[name][0]], 1)

    def ready(self, eng, name, i=0):
        bank, n = self.index(name, i)
        eng.wait_ge(self.filled[bank], n + 1)

    def moved(self, ins, name):
        ins.then_inc(self.drained[self.plan.at[name][0]], 1)

    def arrived(self, eng, name, i=0):
        bank, n = self.index(name, i)
        eng.wait_ge(self.drained[bank], n + 2)


HIDDEN_T, CHOSEN_T6 = (0, 1, 3, 4), {1: 2, 3: 5}
PIECES, CHOSEN_T7 = ((0, 1), (2, 3), (5, 6), (7, 8)), {1: 4, 3: 9}


def f32(ap):
    return ap.bitcast(F32)


def settle(eng, passed):
    eng.sem_inc(passed, 1)


class Steps:

    def __init__(self, eng, sem, base):
        self.eng, self.sem, self.base, self.n = eng, sem, base, 0

    def did(self, ins):
        self.n += 1
        ins.then_inc(self.sem, 1)
        return self.n

    def need(self, n):
        self.eng.wait_ge(self.sem, self.base + n)

    def then(self, ins):
        self.need(self.did(ins))



def build(nc, a, out):
    ctx = ExitStack()
    with ctx:
        placed = {}

        def sb(name, shape):
            placed[name] = -(-nc.sbuf_base // 32) * 32
            return ctx.enter_context(nc.sbuf_tensor(name, shape, F32))

        def rounded_place(name, of, at, *shape):
            return nc.alloc_sbuf_tensor_at(name, [P, *shape], F32R, offset=placed[of] + 4 * at)

        def sem(name):
            return ctx.enter_context(nc.semaphore(name))

        bank = [ctx.enter_context(nc.psum_tensor(f"bank{n}", [P, 512], F32)) for n in range(8)]

        blocks_w = sb("blocks_w", [P, 2, BLOCK])
        m = sb("m", [P, 4, 4096])
        kwi_w = sb("kwi_w", [P, KD, 68])
        const = sb("const", [P, N_CONST])
        prm = sb("prm", [P, N_PRM])
        prm2 = sb("prm2", [P, N_PRM2])
        x = sb("x", [P, NT, D])
        acts = sb("acts", [P, 3, KD, T])
        hT = acts[:, 0]
        hC = acts[:, 1]
        yT = acts[:, 2]
        for n, name in enumerate(("hT", "hC", "yT")):
            placed[name] = placed["acts"] + 4 * n * KD * T
        ss = sb("ss", [P, 4])
        ms = sb("ms", [P, 8])
        rstd = sb("rstd", [P, 8])
        table_i = ctx.enter_context(nc.sbuf_tensor("table_i", [P, QUAD + 1], I32))
        half = sb("half", [P, 8])
        scratch = sb("scratch", [P, N_SCRATCH])

        class Region:

            def __init__(self, mem, size, at=0):
                self.mem, self.size, self.at = mem, size, at

            def take(self, *shape):
                n = int(np.prod(shape))
                v = self.mem[:, self.at:self.at + n]
                self.at += n
                assert self.at <= self.size, (self.at, self.size)
                names = "abcd"[:len(shape)]
                if len(shape) == 1:
                    return v
                return v.rearrange(f"p ({' '.join(names)}) -> p {' '.join(names)}",
                                   **{k: s for k, s in zip(names[1:], shape[1:])})

        ident = const[:, K_ID:K_ID + P]
        cos2 = const[:, K_COS:K_COS + 2 * HD].rearrange("p (t d) -> p t d", t=NT)
        sin2 = const[:, K_SIN:K_SIN + 2 * HD].rearrange("p (t d) -> p t d", t=NT)
        ccos = const[:, K_CC:K_CC + P]
        nsin = const[:, K_SC:K_SC + P]
        dft = const[:, K_DFT:K_RANK].rearrange("p (t c) -> p t c", t=NT)

        lay = Region(scratch, 2 * BLOCK)
        xn = lay.take(NT, D)
        keep = Region(scratch, N_SCRATCH, 2 * BLOCK)
        lnrow = keep.take(2, G)
        wsT = keep.take(H, P)
        zi_at = lay.at
        zi = lay.take(NT, 320)
        wi = lay.take(NT, H)
        va = lay.take(NT, G)
        ra, rb = lay.take(5, HD), lay.take(5, HD)
        ga, gc = lay.take(8, HD), lay.take(8, HD)
        ri = lay.take(NT, 6, HD)
        riT_at = lay.at
        riT = lay.take(3, T)
        rqT = lay.take(4, T)
        rel_at = lay.at
        rel = [lay.take(H, P), lay.take(H, T)]
        score = [lay.take(P), lay.take(T)]
        work = [lay.take(P), lay.take(T)]
        sel = [lay.take(P), lay.take(T)]
        mx = lay.take(NT, 8)
        cpad = lay.take(2, LONG - 1 + T)
        conv = lay.take(2, T)
        ycat = lay.take(NT, 2, G)
        nmx, nms, rsum, rinv = (lay.take(NT, H) for _ in range(4))
        bnst, bnag = keep.take(4, 6), keep.take(4, 2)
        again = Region(scratch, N_SCRATCH, rel_at)
        lg = [again.take(H, P), again.take(H, T)]
        chp = Region(scratch, N_SCRATCH, zi_at).take(2, SHORT - 1 + T)
        conv_n = conv
        rq = xn[:, :, 0:512].rearrange("p t (h d) -> p t h d", h=8)
        acs, sig = xn[:, :, 512:768], xn[:, :, 768:1024]
        chy = sig
        zz = hT[:, :, :].rearrange("p k t -> p (k t)")
        zq = zz[:, 0:1024].rearrange("p (t c) -> p t c", t=NT)
        zg = zz[:, 1024:2048].rearrange("p (t c) -> p t c", t=NT)
        pT0 = zz[:, 0:512].rearrange("p (h q) -> p h q", h=H)
        pT1 = zz[:, 1024:2048].rearrange("p (s h q) -> p s h q", s=2, h=H)
        h1_h, h1_l = rounded_place("h1_h", "yT", 0, KD, T), rounded_place("h1_l", "hC", 0, KD, T)
        y_h, y_l = rounded_place("y_h", "hC", 0, KD, T), rounded_place("y_l", "yT", 0, KD, T)
        w_l = rounded_place("w_l", "m", 0, 4, 4096)
        fw_h = rounded_place("fw_h", "scratch", 0, 2, BLOCK)
        fw_l = rounded_place("fw_l", "blocks_w", 0, 2, BLOCK)
        vqi_h = fw_l[:, 1, 0:4096]
        dadg_h = rounded_place("dadg_h", "scratch", riT_at, 4096)
        h_h, h_l = rounded_place("h_h", "hT", 0, KD, T), rounded_place("h_l", "hC", 0, KD, T)
        h_full = hC
        sga = Region(yT[:, :, :].rearrange("p k t -> p (k t)"), D).take(2, T)
        a2 = rounded_place("a2", "yT", 2 * T, 2, 2, T)

        again = Region(scratch, keep.at)
        gb = again.take(2, D)
        cb_at = again.at
        xmp = again.take(MH, 2, CTX + 2)
        actT = again.take(MH, S2)
        ctx_at = again.at
        h_rows = again.take(NT, MW)
        pre_at = again.at
        pre = again.take(2, 2, CTX)
        xn2_at = again.at
        xn2 = again.take(NT, D)
        ft_at = again.at
        fT = again.take(4, T)
        modc = again.take(4, KD, 2)
        w_rt = again.take(KD, NG + NE)
        b_rt = again.take(NG + NE)
        bst, bag = again.take(8, 6), again.take(8, 2)
        emn, rcol = again.take(NT, ROWS), again.take(4, ROWS)
        nq, rq2 = again.take(NT), again.take(NT)
        logit, expert_l, pick1, pick2 = (again.take(NT, NG + NE) for _ in range(4))
        gd, ge, gsel = (again.take(NT, NG) for _ in range(3))
        t1, t2, t3, t4 = (again.take(NT) for _ in range(4))
        chosen, comb, place = again.take(NT, NE), again.take(NT, NPASS), again.take(NT, NPASS)
        comb_at = again.at = -(-again.at // 8) * 8
        again.take(NT, NPASS)
        comb_h, comb_l = rounded_place("comb_h", "scratch", comb_at, NT, NPASS), again.take(NT, NPASS)
        over_e, over_n, over_1 = again.take(NE), again.take(NE), again.take(NE)
        over_t = again.take(NT, NE)
        table = again.take(QUAD + 1)
        pick_at = again.at = -(-again.at // 8) * 8
        again.take(QUAD, P + 4)
        pick_w = rounded_place("pick_w", "scratch", pick_at, QUAD, P + 4)
        slot_w = again.take(QUAD)
        cs = keep.take(KD, 2)
        xg = rounded_place("xg", "scratch", cb_at, 2, 2, KD, 2 * P)
        xg_full = Region(scratch, N_SCRATCH, cb_at).take(2, 2, KD, 2 * P)
        w_h = rounded_place("w_h", "blocks_w", 0, 3, 4096)
        xn_h, xn_l = rounded_place("xn_h", "hC", 0, NT, D), rounded_place("xn_l", "hT", 0, NT, D)
        choice = rounded_place("choice", "scratch", 0, 2, NT, 2 * P)
        wo_a, wo_b = rounded_place("wo_a", "hT", 0, 2, D), rounded_place("wo_b", "scratch", xn2_at, 2, D)
        fy_h = rounded_place("fy_h", "scratch", ft_at, 4, T)
        choice_t = rounded_place("choice_t", "scratch", ft_at, QUAD, T)
        hidden = const[:, K_COS:K_COS + DE]
        aT2 = rounded_place("aT2", "const", K_COS + DE, 2, 4, P)
        y2 = rounded_place("y2", "yT", 0, 2, D)
        ctx_x = Region(scratch, N_SCRATCH, ctx_at).take(NT, D)
        tmp = Region(scratch, N_SCRATCH, ctx_at).take(4, 512)
        hm = Region(scratch, N_SCRATCH, pre_at).take(MH, T)
        rest_flat = fw_l[:, :, :].rearrange("p s n -> p (s n)")
        hc_h = rounded_place("hc_h", "scratch", ctx_at, KD, T)
        hl_l = rounded_place("hl_l", "hT", 0, KD, T)
        xm_h, z_h, u_h = rest_flat[:, 8192:12288], rest_flat[:, 0:4096], w_l[:, 0, :]
        h_rt = Region(scratch, N_SCRATCH, ctx_at).take(KD, T)
        ada_h = [rounded_place("ada_h0", "scratch", cb_at, 4096), rounded_place("ada_h1", "blocks_w", 0, 4096)]
        cs_at = keep.at = -(-keep.at // 8) * 8
        keep.take(2, KD, 2)
        cs2 = rounded_place("cs2", "scratch", cs_at, 2, KD, 2)
        gfin = fT.rearrange("p a b -> p (a b)")
        fP = Region(scratch, N_SCRATCH, xn2_at).take(4, 512)
        pos = Region(scratch, N_SCRATCH).take(NT, D)
        szT = hC[:, 0:4, :]
        u_rows = hC[:, 4:8, :].rearrange("p k t -> p (k t)").rearrange("p (t c) -> p t c", t=NT)
        w3 = Region(m[:, 3, :], 4096)
        bd = w3.take(3, MH, P)
        w_if = w3.take(3 * MH, P)
        w_f = w3.take(4, P)
        E = Region(m[:, 2, :], 4096).take(2, 2, 4, T)
        flat = blocks_w[:, :, :].rearrange("p s n -> p (s n)")
        modrow = acts[0:2].rearrange("p n k t -> p (n k t)")
        gpost = [xn2[0:2, 1, :], scratch[0:2, 2 * BLOCK:2 * BLOCK + D]]
        ada_w = [m[:, n, :] for n in range(4)] + [flat[:, 8192:12288], flat[:, 4096:8192]]
        ada_l = [w_l[:, n, :] for n in range(4)] + [rest_flat[:, 8192:12288], rest_flat[:, 4096:8192]]
        wide = Region(flat, 2 * BLOCK)
        qkvT = wide.take(3, MH, S2)
        vtok = wide.take(4, MH, DH + 1)
        gi, gf, gx, cum, rr, rmax = (wide.take(S2) for _ in range(6))

        filled = [sem(f"filled{n}") for n in range(8)]
        drained = [sem(f"drained{n}") for n in range(8)]
        dve_step, pool_step, passed = sem("dve_step"), sem("pool_step"), sem("passed")
        const_in, x_in, prm2_in = sem("const_in"), sem("x_in"), sem("prm2_in")
        prm_in, rows_ws_in, kwi_in, ab_in = sem("prm_in"), sem("rows_ws_in"), sem("kwi_in"), sem("ab_in")
        m_in = [sem(f"m{n}_in") for n in range(4)]
        ada_in, before_ada = m_in + [sem("ada4_in"), sem("ada5_in")], (2 * DEPTH, 2 * DEPTH, DEPTH, DEPTH, 0, 0)
        gu_in, down_in = ([sem(f"{w}{n}_in") for n in range(2)] for w in ("gu", "down"))
        in_hi, in_lo, h1_rounded, h1_ready = sem("in_hi"), sem("in_lo"), sem("h1_rounded"), sem("h1_ready")
        w1_hi, w1_lo, w1_pool, ab_lo, out_lo = sem("w1_hi"), sem("w1_lo"), sem("w1_pool"), sem("ab_lo"), sem("out_lo")
        mix_rounded, mix_ready = sem("mix_rounded"), sem("mix_ready")
        ffn_hi, ffn_lo, h_rounded, h_ready = sem("ffn_hi"), sem("ffn_lo"), sem("h_rounded"), sem("h_ready")
        block_used = [sem(f"block{n}_used") for n in range(2)]
        half_ready = sem("half_ready")
        ss_ready, rstd_ready, xn_ready = sem("ss_ready"), sem("rstd_ready"), sem("xn_ready")
        ri_ready, rq_ready, ws_ready = sem("ri_ready"), sem("rq_ready"), sem("ws_ready")
        score_ready, score_masked = sem("score_ready"), sem("score_masked")
        sel_ready, sel_masked = sem("sel_ready"), sem("sel_masked")
        conv_ready, var_ready, norm_rstd = sem("conv_ready"), sem("var_ready"), sem("norm_rstd")
        v_norm, v_ready = sem("v_norm"), sem("v_ready")
        yb_ready, lg_ready, exp_ready, silu_ready = sem("yb_ready"), sem("lg_ready"), sem("exp_ready"), sem("silu_ready")
        gains_in = sem("gains_in")
        w2_hi, w2_lo, w2_first, h2_rounded, h2_ready = (sem("w2_hi"), sem("w2_lo"), sem("w2_first"), sem("h2_rounded"),
                                                        sem("h2_ready"))
        rows_in, pos_in, ctx_in, heads_in, router_in = (sem("rows_in"), sem("pos_in"), sem("ctx_in"), sem("heads_in"),
                                                     sem("router_in"))
        ada_hi, ada_lo, ada_first, cs_ready = sem("ada_hi"), sem("ada_lo"), sem("ada_first"), sem("cs_ready")
        a_step, silu_c, mod_ready, gate_rows = sem("a_step"), sem("silu_c"), sem("mod_ready"), sem("gate_rows")
        x_ready, zeros_ready, pre_ready, act_ready = sem("x_ready"), sem("zeros_ready"), sem("pre_ready"), sem("act_ready")
        f_abs, f_log, scan_ready, e_masked, s_ready = (sem("f_abs"), sem("f_log"), sem("scan_ready"), sem("e_masked"),
                                                       sem("s_ready"))
        h_var, h_rstd, hn_ready, y_ready = sem("h_var"), sem("h_rstd"), sem("hn_ready"), sem("y_ready")
        wo_hi, wo_lo, y_hi, y_lo = sem("wo_hi"), sem("wo_lo"), sem("y_hi"), sem("y_lo")
        g_diff, g_exp, e_diff, e_exp, first_weights = (sem("g_diff"), sem("g_exp"), sem("e_diff"), sem("e_exp"),
                                                       sem("first_weights"))
        piece_in = [sem(f"piece{n}_in") for n in range(4)]
        chosen_ready, choice_ready, table_ready = sem("chosen_ready"), sem("choice_ready"), sem("table_ready")
        hi_ready, lo_ready, xg_ready = sem("hi_ready"), sem("lo_ready"), sem("xg_ready")
        xg_moved, xg_rounded, hidden_rounded = sem("xg_moved"), sem("xg_rounded"), sem("hidden_rounded")
        slot_ready, y_rounded, y_zero = sem("slot_ready"), sem("y_rounded"), sem("y_zero")
        out_ready, out_stored = sem("out_ready"), sem("out_stored")
        block = ctx.enter_context(nc.Block())

        def layer_results(l):
            return Results(filled, drained, LAY, [l * n for n in LAY.count])

        M01, M23 = 32 * DEPTH + 32, 16 * DEPTH + 32
        sec = Results(filled, drained, SEC, [DEPTH * n for n in LAY.count])
        B1, B0 = NFB // 2, (NFB + 1) // 2

        @block.sync
        def _(sp):
            for t in range(NT):
                sp.dma_start(x[:, t, :], a["x"][t * P:(t + 1) * P, :]).then_inc(x_in, 16)
            sp.dma_start(const[:, :], a["const"]).then_inc(const_in, 16)
            with sp.Fori(0, DEPTH) as l:
                res = layer_results(l)

                def w_in(name):
                    return a["w_in"][bass.ds(l, 1), :, IN_AT[name]:IN_AT[name] + KD * IN_COLS[name]]\
                        .rearrange("a p n -> p (a n)")

                def ffn_part(b, lo, hi):
                    return a["ffn"][bass.ds(l, 1), bass.ds(b, 1), :, lo:hi].rearrange("a b p n -> p (a b n)")

                sp.dma_start(prm[:, :], a["prm"][bass.ds(l, 1)].rearrange("a p n -> p (a n)")).then_inc(prm_in, 16)
                sp.dma_start(kwi_w[:, :, :].rearrange("p k n -> p (k n)"), w_in("kwi")).then_inc(kwi_in, 16)
                sp.dma_start(m[:, 2, :], w_in("dadg")).then_inc(m_in[2], 16)
                sp.dma_start(m[:, 0, :], w_in("vqi")).then_inc(m_in[0], 16)
                sp.dma_start(m[:, 1, :], w_in("qk")).then_inc(m_in[1], 16)
                sp.dma_start(lnrow.rearrange("p r n -> p (r n)"), a["gmlp_ln"][bass.ds(l, 1)]
                             .rearrange("a n -> (a n)").partition_broadcast(P)).then_inc(rows_ws_in, 16)
                sp.dma_start(wsT.rearrange("p h n -> p (h n)"), a["w_s"][bass.ds(l, 1)]
                             .rearrange("a p n -> p (a n)")).then_inc(rows_ws_in, 16)
                sp.dma_start(m[:, 3, :], w_in("guv")).then_inc(m_in[3], 16)
                src = w_in("abac")
                sp.wait_ge(drained[3], l * LAY.count[3] + 1)
                sp.dma_start(blocks_w[:, 0, 0:4096], src).then_inc(ab_in, 16)
                sp.dma_start(blocks_w[:, 0, 4096:6144], w_in("ah")).then_inc(ab_in, 16)
                for s, job in ((0, "vqi1"), (1, "qk1")):
                    src = a["w_out"][bass.ds(l, 1), :, s * 4096:(s + 1) * 4096].rearrange("a p n -> p (a n)")
                    res.ready(sp, job)
                    sp.dma_start(m[:, s, :], src).then_inc(m_in[s], 16)
                src = ffn_part(0, 0, GU)
                res.ready(sp, "ah")
                settle(sp, passed)
                sp.dma_start(blocks_w[:, 0, 0:GU], src).then_inc(gu_in[0], 16)
                sp.dma_start(blocks_w[:, 0, GU:], ffn_part(0, GU, BLOCK)).then_inc(down_in[0], 16)
                sp.dma_start(blocks_w[:, 1, 0:GU], ffn_part(1, 0, GU)).then_inc(gu_in[1], 16)
                sp.dma_start(blocks_w[:, 1, GU:], ffn_part(1, GU, BLOCK)).then_inc(down_in[1], 16)

                def next_block(b, slot, used):
                    src = ffn_part(b, 0, GU)
                    res.ready(sp, "gu1", b - 2)
                    sp.dma_start(blocks_w[:, slot, 0:GU], src).then_inc(gu_in[slot], 16)
                    src = ffn_part(b, GU, BLOCK)
                    sp.wait_ge(block_used[slot], used)
                    sp.dma_start(blocks_w[:, slot, GU:], src).then_inc(down_in[slot], 16)

                with sp.Fori(0, B1 - 1) as r:
                    next_block(2 * r + 2, 0, B1 * l + r + 1)
                    next_block(2 * r + 3, 1, B1 * l + r + 2)
                next_block(NFB - 1, 0, B1 * l + B1)

            sp.dma_start(prm2[:, :], a["prm2"]).then_inc(prm2_in, 16)
            for s in range(ADA):
                if s == 4:
                    sp.wait_ge(block_used[1], B1 * DEPTH + 1)
                if s == 5:
                    sp.wait_ge(filled[3], DEPTH * LAY.count[3])
                    sp.dma_start(modrow, a["b_ada"].partition_broadcast(2)).then_inc(rows_in, 16)
                sp.dma_start(ada_w[s], a["w_ada"][0, s]).then_inc(ada_in[s], 16)
            sp.dma_start(pos.rearrange("p t d -> p (t d)"), a["pos"]).then_inc(pos_in, 16)
            sp.wait_ge(drained[3], DEPTH * LAY.count[3] + 1)
            sp.dma_start(gfin, a["g_final"].partition_broadcast(P)).then_inc(pos_in, 16)
            for t in range(NT):
                sp.dma_start(ctx_x[:, t, :], a["ctx"][t * P:(t + 1) * P, :]).then_inc(ctx_in, 16)
            sp.dma_start(w_rt.rearrange("p k n -> p (k n)"), a["w_router"]).then_inc(router_in, 16)
            sp.dma_start(b_rt, a["b_router"].partition_broadcast(P)).then_inc(router_in, 16)
            for q in range(2):
                sp.dma_start(gpost[q], a["g_post"][q * D:(q + 1) * D].partition_broadcast(2)).then_inc(gains_in, 16)
            for s in range(ADA):
                sec.ready(sp, f"ada{s}", 0)
                sp.dma_start(ada_w[s], a["w_ada"][1, s]).then_inc(ada_in[s], 16)
            for s in range(3):
                sec.ready(sp, f"ada{s}", 1)
                sp.dma_start(m[:, s, :], a["w_in_2"][s]).then_inc(m_in[s], 16)
            sec.ready(sp, "ada3", 1)
            sp.dma_start(m[:, 3, 0:3584], a["heads_2"]).then_inc(heads_in, 16)
            for s, job in ((1, "z1"), (0, "u1")):
                sec.ready(sp, job)
                sp.dma_start(m[:, s, :], a["w_out_2"][:, s * 4096:(s + 1) * 4096]).then_inc(m_in[s], 16)

            def piece(q, c, expert=None):
                e = bass.ds(4 * q + c // 3, 1) if expert is None else bass.ds(expert, 1)
                return a["experts"][e, :, (c % 3) * 4096:(c % 3 + 1) * 4096].rearrange("a p n -> p (a n)")

            def load(src, c, q, after=True):
                if after:
                    i, kind = divmod(c - 4, 3)
                    sec.ready(sp, ("eG", "eU", "eD1")[kind], 2 * (QUAD * q + i))
                sp.dma_start(m[:, c % 4, :], src).then_inc(piece_in[c % 4], 16)

            sec.ready(sp, "wo3")
            for c in range(4):
                load(piece(0, c), c, 0, after=False)
            with sp.Fori(0, NE // QUAD - 1) as q:
                for c in range(4, 16):
                    src = piece(q, c)
                    load(src, c, q)
            q = NE // QUAD - 1
            for c in range(4, 12):
                load(piece(q, c), c, q)
            sp.wait_ge(table_ready, 1)
            experts = [sp.value_load(table_i[0:1, n:n + 1], min_val=0, max_val=NE - 1) for n in range(OVER)]
            for c in (12, 13):
                load(piece(q, c, experts[0]), c, q)
            with sp.If(sp.value_load(table_i[0:1, OVER:OVER + 1], min_val=0, max_val=OVER) > 0):
                q = NE // QUAD
                for c in range(2, 12):
                    load(piece(q, c, experts[c // 3]), c, q)
            for t in range(NT):
                sp.wait_ge(out_ready, 2 * t + 2)
                sp.dma_start(out[t * P:(t + 1) * P, :], x[:, t, :]).then_inc(out_stored, 16)
            sp.wait_ge(out_stored, 16 * NT)

        @block.tensor
        def _(pe):
            def chain(out_, pairs, first=True, last=True):
                for n, (lhsT, rhs) in enumerate(pairs):
                    ins = pe.matmul(out_, lhsT, rhs, start=first and n == 0, stop=last and n == len(pairs) - 1,
                                    skip_group_check=not (first and last))
                return ins

            def split_chain(out_, pairs, first=True, last=True):
                n = len(pairs)
                for i, ((xh, xl), (wh, wl)) in enumerate(pairs):
                    pe.matmul(out_, xh, wh, start=first and i == 0, stop=False, skip_group_check=True)
                    pe.matmul(out_, xh, wl, start=False, stop=False, skip_group_check=True)
                    ins = pe.matmul(out_, xl, wh, start=False, stop=last and i == n - 1, skip_group_check=True)
                return ins

            pe.wait_ge(const_in, 16)
            with pe.Fori(0, DEPTH) as l:
                res = layer_results(l)

                def to(job):
                    return bank[LAY.at[job][0]]

                def transposes(name, ready):
                    for t in range(NT):
                        pe.wait_ge(xn_ready, ready + t)
                        for b in range(2):
                            job = f"{name}_{t}{b}"
                            res.room(pe, job)
                            for k in range(4):
                                c = (4 * b + k) * P
                                ins = pe.transpose(to(job)[:, k * P:(k + 1) * P], xn[:, t, c:c + P], ident)
                            res.done(ins, job)

                def token_job(name, w, t):
                    job, cols = f"{name}{t}", w.shape[2]
                    res.room(pe, job)
                    res.done(chain(to(job)[:, 0:cols], [(hT[:, k, t * P:(t + 1) * P], w[:, k, :]) for k in range(KD)]), job)

                transposes("tx1", 4 * l + 1)
                for t in range(NT):
                    for b in range(2):
                        res.arrived(pe, f"tx1_{t}{b}")
                pe.wait_ge(kwi_in, 16 * l + 16)
                for t in range(NT):
                    token_job("kwi", kwi_w[:, :, :], t)
                def split_view(high, low):
                    return (w.rearrange("p (k n) -> p k n", k=KD) for w in (high, low))

                def split_tokens(name, high, low, t):
                    wh, wl = split_view(high, low)
                    tok = slice(t * P, (t + 1) * P)
                    res.room(pe, f"{name}{t}")
                    res.done(split_chain(to(f"{name}{t}")[:, :], [((h1_h[:, k, tok], h1_l[:, k, tok]), (wh[:, k, :], wl[:, k, :]))
                                                                  for k in range(KD)]), f"{name}{t}")

                def split_features(job, high, low, c0):
                    wh, wl = split_view(high, low)
                    res.room(pe, job)
                    for g in range(2):
                        at = slice(c0 + g * P, c0 + (g + 1) * P)
                        ins = split_chain(to(job)[:, g * T:(g + 1) * T],
                                          [((wh[:, k, at], wl[:, k, at]), (h1_h[:, k, :], h1_l[:, k, :])) for k in range(KD)])
                    res.done(ins, job)

                pe.wait_ge(h1_ready, 4 * l + 4)
                for n, name in enumerate(("da", "dg", "vqi", "qk")):
                    if name != "dg":
                        i = max(n - 1, 0)
                        pe.wait_ge(w1_pool, 6 * l + 2 * i + 2)
                        pe.wait_ge(w1_lo, 6 * l + 2 * i + 2)
                    if n < 2:
                        split_features(name, dadg_h[:, :], w_l[:, 2, :], n * T)
                    else:
                        for t in range(NT):
                            split_tokens(name, *((vqi_h, w_l[:, 0, :]) if name == "vqi" else (dadg_h[:, :], w_l[:, 1, :])), t)

                for t in range(NT):
                    job = f"riT{t}"
                    pe.wait_ge(ri_ready, 2 * l + t + 1)
                    res.room(pe, job)
                    for c in range(3):
                        ins = pe.transpose(to(job)[:, c * P:(c + 1) * P],
                                           ri[:, t, 2 * c:2 * c + 2, :].rearrange("p h d -> p (h d)"), ident)
                    res.done(ins, job)
                for job, t, heads in (("sc0a", 0, (0, 2)), ("sc0b", 0, (1, 3)), ("sc1a", 1, (0, 2)), ("sc1b", 1, (1, 3))):
                    nk = (t + 1) * P
                    for u in range(t + 1):
                        res.arrived(pe, f"riT{u}")
                    res.room(pe, job)
                    for n, j in enumerate(heads):
                        o = HD * (j % 2)
                        ins = pe.matmul(to(job)[:, n * nk:(n + 1) * nk], riT[o:o + HD, j // 2, t * P:(t + 1) * P],
                                        riT[o:o + HD, 2, 0:nk], start=True, stop=True)
                    res.done(ins, job)
                pe.wait_ge(in_lo, 6 * l + 4)
                for t in range(NT):
                    split_tokens("guv", w_l[:, 2, :], w_l[:, 3, :], t)
                pe.wait_ge(ab_lo, 6 * l + 6)
                split_features("ab", vqi_h, fw_l[:, 0, 0:4096], 0)
                split_features("ac", vqi_h, fw_l[:, 0, 0:4096], 256)
                split_features("ah", fw_l[:, 1, 4096:6144], fw_l[:, 0, 4096:6144], 0)
                pe.wait_ge(conv_ready, l + 1)
                res.room(pe, "cvT")
                for t in range(NT):
                    for g in range(2):
                        ins = pe.transpose(to("cvT")[:, t * T + g * P:t * T + (g + 1) * P],
                                           conv[:, g, t * P:(t + 1) * P], ident)
                res.done(ins, "cvT")
                for t in range(NT):
                    job = f"rqT{t}"
                    pe.wait_ge(rq_ready, 2 * l + t + 1)
                    res.room(pe, job)
                    for c in range(4):
                        ins = pe.transpose(to(job)[:, c * P:(c + 1) * P],
                                           rq[:, t, 2 * c:2 * c + 2, :].rearrange("p h d -> p (h d)"), ident)
                    res.done(ins, job)
                pe.wait_ge(ws_ready, l + 1)
                for t in range(NT):
                    job = f"mix{t}"
                    pe.wait_ge(v_ready, 2 * l + t + 1)
                    res.room(pe, job)
                    for h in range(H):
                        ins = pe.matmul(to(job)[:, h * HD:(h + 1) * HD], wsT[:, h, :],
                                        zg[:, t, G + h * HD:G + (h + 1) * HD], start=True, stop=True)
                    res.done(ins, job)
                for job, t, heads in (("lg0a", 0, (0, 2)), ("lg0b", 0, (1, 3)), ("lg1a", 1, (0, 2)), ("lg1b", 1, (1, 3))):
                    nk = (t + 1) * P
                    for u in range(t + 1):
                        res.arrived(pe, f"rqT{u}")
                    res.room(pe, job)
                    for n, h in enumerate(heads):
                        o = HD * (h % 2)
                        ins = pe.matmul(to(job)[:, n * nk:(n + 1) * nk], rqT[o:o + HD, h // 2, t * P:(t + 1) * P],
                                        rqT[o:o + HD, 2 + h // 2, 0:nk], start=True, stop=True)
                    res.done(ins, job)

                def mixed_rows(job, part, t):
                    for k in range(2):
                        ins = pe.transpose(to(job)[:, k * T + t * P:k * T + (t + 1) * P],
                                           ycat[:, t, part, k * P:(k + 1) * P], ident)
                    return ins

                res.room(pe, "ybT")
                for t in range(NT):
                    pe.wait_ge(yb_ready, 2 * l + t + 1)
                    ins = mixed_rows("ybT", 0, t)
                res.done(ins, "ybT")
                res.arrived(pe, "cvT")
                res.room(pe, "cnT")
                for g in range(2):
                    for t in range(NT):
                        ins = pe.transpose(to("cnT")[:, g * T + t * P:g * T + (t + 1) * P],
                                           conv_n[:, t, g * P:(g + 1) * P], ident)
                res.done(ins, "cnT")

                def out_proj(ks, first, last):
                    for n in range(4):
                        t, c = n // 2, n % 2
                        if first:
                            res.room(pe, f"wo{n}")
                        pairs = []
                        for k in ks:
                            tok, o = slice(t * P, (t + 1) * P), (k % 4) * D + c * 512
                            pairs.append(((y_h[:, k, tok], y_l[:, k, tok]),
                                          (w_l[:, 2 + k // 4, o:o + 512], w_l[:, k // 4, o:o + 512])))
                        ins = split_chain(bank[n][:, :], pairs, first, last)
                        if last:
                            res.done(ins, f"wo{n}")

                pe.wait_ge(out_lo, 6 * l + 2)
                pe.wait_ge(in_lo, 6 * l + 6)
                pe.wait_ge(mix_ready, 4 * l + 2)
                out_proj((0, 1, 2, 3), True, False)
                for job, t, u in (("pT0", 0, 0), ("pT1a", 1, 0), ("pT1b", 1, 1)):
                    pe.wait_ge(exp_ready, 8 * l + 4 * t + 4)
                    res.room(pe, job)
                    for h in range(H):
                        ins = pe.transpose(to(job)[:, h * P:(h + 1) * P], lg[t][:, h, u * P:(u + 1) * P], ident)
                    res.done(ins, job)
                for t in range(NT):
                    job = f"av{t}"
                    for p_job in (("pT0",), ("pT1a", "pT1b"))[t]:
                        res.arrived(pe, p_job)
                    res.room(pe, job)
                    for h in range(H):
                        ins = chain(to(job)[:, h * HD:(h + 1) * HD],
                                    [(pT0[:, h, :] if t == 0 else pT1[:, u, h, :], va[:, u, h * HD:(h + 1) * HD])
                                     for u in range(t + 1)])
                    res.done(ins, job)
                pe.wait_ge(out_lo, 6 * l + 6)
                pe.wait_ge(mix_ready, 4 * l + 3)
                out_proj((6,), False, False)
                res.room(pe, "ycT")
                for t in range(NT):
                    res.arrived(pe, f"av{t}")
                    ins = mixed_rows("ycT", 1, t)
                res.done(ins, "ycT")
                out_proj((7,), False, False)
                pe.wait_ge(mix_ready, 4 * l + 4)
                out_proj((4, 5), False, True)

                transposes("tx2", 4 * l + 3)

                def split_by(b, subs):
                    pe.wait_ge(ffn_lo, SUBS * (NFB * l + b) + subs)

                def gate_up(slot, j, i):
                    job = f"gu{j}"
                    res.room(pe, job, i)
                    wh, wl = (w[:, 0:GU].rearrange("p (q k n) -> p q k n", q=2, k=KD)[:, :, :, j * P:(j + 1) * P]
                              for w in (fw_h[:, 1 - slot, :], fw_l[:, slot, :]))
                    for q in range(2):
                        ins = split_chain(to(job)[:, q * T:(q + 1) * T],
                                          [((wh[:, q, k, :], wl[:, q, k, :]), (h_h[:, k, :], h_l[:, k, :])) for k in range(KD)])
                    res.done(ins, job)

                def down(slot, j, i, first=False, last=False):
                    if j == 0:
                        split_by(i, SUBS)
                    res.arrived(pe, f"gu{j}", i)
                    for n in range(4):
                        t, c = n // 2, n % 2
                        if first:
                            res.room(pe, f"y{n}")
                        o = GU + j * D + c * 512
                        ins = split_chain(bank[n][:, :], [((a2[:, 0, j, t * P:(t + 1) * P], a2[:, 1, j, t * P:(t + 1) * P]),
                                                           (fw_h[:, 1 - slot, o:o + 512], fw_l[:, slot, o:o + 512]))], first, last)
                        if last:
                            res.done(ins, f"y{n}")
                    return ins

                split_by(0, 4)
                pe.wait_ge(h_ready, 4 * l + 4)
                gate_up(0, 0, 0)
                gate_up(0, 1, 0)
                down(0, 0, 0, first=True)
                with pe.Fori(0, B1) as r:
                    split_by(2 * r + 1, 4)
                    gate_up(1, 0, 2 * r + 1)
                    down(0, 1, 2 * r).then_inc(block_used[0], 1)
                    gate_up(1, 1, 2 * r + 1)
                    down(1, 0, 2 * r + 1)
                    split_by(2 * r + 2, 4)
                    gate_up(0, 0, 2 * r + 2)
                    down(1, 1, 2 * r + 1).then_inc(block_used[1], 1)
                    gate_up(0, 1, 2 * r + 2)
                    down(0, 0, 2 * r + 2)
                down(0, 1, NFB - 1, last=True)

            def to(job):
                return bank[SEC.at[job][0]]

            pe.wait_ge(cs_ready, 2)
            with pe.Fori(0, 2) as i:
                for s in range(ADA):
                    sec.room(pe, f"ada{s}", i)
                    wh, wl = (w.rearrange("p (k n) -> p k n", k=KD) for w in (ada_h[s % 2][:, :], ada_l[s]))
                    for j in (1, 2, 3, 0):
                        if j:
                            pe.wait_ge(ada_lo, 3 * (ADA * i + s) + j)
                        else:
                            pe.wait_ge(ada_first, ADA * i + s + 1)
                        ins = split_chain(bank[s][0:2, :], [((cs2[:, 0, k, :], cs2[:, 1, k, :]), (wh[:, k, :], wl[:, k, :]))
                                                            for k in (2 * j, 2 * j + 1)], j == 1, j == 0)
                    sec.done(ins, f"ada{s}")
            for s in range(ADA):
                sec.arrived(pe, f"ada{s}", 1)
            sec.room(pe, "modT")
            for n, row in enumerate((0, 1, 3, 4)):
                for k in range(KD):
                    ins = pe.transpose(to("modT")[:, 2 * (KD * n + k):2 * (KD * n + k) + 2],
                                       modrow[:, row * D + k * P:row * D + (k + 1) * P], ident[0:2, 0:2])
            sec.done(ins, "modT")
            def gate(q):
                pe.wait_ge(gate_rows, q + 1)
                for n in (2 * q, 2 * q + 1):
                    o = (2 + 3 * q) * D + (n % 2) * 512
                    sec.room(pe, f"gate{n}")
                    sec.done(pe.matmul(bank[n][:, :], ident[0:2, 0:1].to_broadcast([2, P]), modrow[:, o:o + 512],
                                       start=True, stop=True), f"gate{n}")

            def transposes2(name, ready, rows):
                for t in range(NT):
                    pe.wait_ge(xn_ready, ready + t)
                    for n in range(4):
                        if t == 0:
                            sec.room(pe, f"{name}{n}")
                        for k in range(2):
                            c = (2 * n + k) * P
                            ins = pe.transpose(to(f"{name}{n}")[:, k * T + t * P:k * T + (t + 1) * P],
                                               rows[:, t, c:c + P], ident)
                        if t == NT - 1:
                            sec.done(ins, f"{name}{n}")

            XN = 4 * DEPTH
            gate(0)
            gate(1)
            transposes2("tc", XN + 1, ctx_x)
            transposes2("tl", XN + 3, xn2)

            def columns(s, high):
                return (w.rearrange("p (k n) -> p k n", k=KD) for w in (high, w_l[:, s, :]))

            wh, wl = columns(0, xm_h)
            pe.wait_ge(w2_first, 2)
            pe.wait_ge(w2_lo, 2)
            for q, (hh, hl) in enumerate(((hc_h, h_l), (h1_h, hl_l))):
                for j in range(MH):
                    at = slice(j * P, (j + 1) * P)
                    if q == 0:
                        sec.room(pe, f"xm{j}")
                    for n in range(4):
                        if j == 0:
                            pe.wait_ge(h2_ready, 4 * q + n + 1)
                        ins = split_chain(to(f"xm{j}")[:, q * T:(q + 1) * T],
                                          [((wh[:, k, at], wl[:, k, at]), (hh[:, k, :], hl[:, k, :])) for k in (2 * n, 2 * n + 1)],
                                          n == 0, n == 3)
                    if q == 1:
                        sec.done(ins, f"xm{j}")
            wh, wl = columns(1, z_h)
            pe.wait_ge(w2_lo, 6)
            for q in range(2):
                sec.room(pe, f"z{q}")
                for g in range(2):
                    at = slice((2 * q + g) * P, (2 * q + g + 1) * P)
                    ins = split_chain(to(f"z{q}")[:, g * T:(g + 1) * T],
                                      [((wh[:, k, at], wl[:, k, at]), (h1_h[:, k, :], hl_l[:, k, :])) for k in range(KD)])
                sec.done(ins, f"z{q}")
            pe.wait_ge(heads_in, 16)
            for j in range(MH):
                sec.arrived(pe, f"xm{j}")
            for c in range(4):
                sec.room(pe, f"vt{c}")
                for j in range(MH):
                    ins = pe.matmul(to(f"vt{c}")[:, j * DH:(j + 1) * DH],
                                    xmp[:, j, c // 2, 1 + (c % 2) * P:1 + (c % 2 + 1) * P], bd[:, 2, j, :], start=True, stop=True)
                sec.done(ins, f"vt{c}")
            for n in range(12):
                j, q = n // 3, n % 3
                if q == 0:
                    pe.wait_ge(act_ready, j + 1)
                sec.room(pe, f"qkv{n}")
                src = actT[:, j, :].rearrange("p (s t) -> p s t", s=2) if q < 2 else xmp[:, j, :, 1:1 + CTX]
                sec.done(pe.matmul(to(f"qkv{n}")[:, :].rearrange("p (s t) -> p s t", s=2), bd[:, q, j, :], src,
                                   start=True, stop=True), f"qkv{n}")
            for n in range(12):
                sec.arrived(pe, f"qkv{n}")
            sec.room(pe, "gates")
            sec.done(chain(to("gates")[:, :], [(w_if[:, 4 * q + j, :], qkvT[:, q, j, :]) for j in range(MH) for q in range(3)]),
                     "gates")
            wh, wl = columns(2, u_h)
            pe.wait_ge(w2_lo, 10)
            for t in range(NT):
                tok = slice(t * P, (t + 1) * P)
                sec.room(pe, f"u{t}")
                sec.done(split_chain(to(f"u{t}")[:, :], [((h1_h[:, k, tok], hl_l[:, k, tok]), (wh[:, k, :], wl[:, k, :]))
                                                         for k in range(KD)]), f"u{t}")
            for g in range(4):
                sec.room(pe, f"fp{g}")
                for t in range(NT):
                    sec.arrived(pe, f"u{t}")
                sec.done(chain(to(f"fp{g}")[:, :], [(u_rows[:, t, g * P:(g + 1) * P], dft[:, t, :]) for t in range(NT)]), f"fp{g}")
            for p in range(2):
                sec.room(pe, f"ff{p}")
                for g in (2 * p, 2 * p + 1):
                    sec.arrived(pe, f"fp{g}")
                    ins = chain(to(f"ff{p}")[:, (g % 2) * T:(g % 2 + 1) * T],
                                [(ccos, fP[:, g, 0:T]), (nsin, fP[:, g, T:2 * T])])
                sec.done(ins, f"ff{p}")
            for p in range(2):
                sec.arrived(pe, f"ff{p}")
                sec.room(pe, f"fy{p}")
                for g in (2 * p, 2 * p + 1):
                    ins = pe.matmul(to(f"fy{p}")[:, (g % 2) * T:(g % 2 + 1) * T], w_f[:, g, :], fT[:, g, :],
                                    start=True, stop=True)
                sec.done(ins, f"fy{p}")
            pe.wait_ge(scan_ready, 1)
            sec.room(pe, "rT")
            for c in range(4):
                pe.transpose(to("rT")[:, c * ROWS:(c + 1) * ROWS], rr[0:ROWS, c * P:(c + 1) * P], ident[0:ROWS, 0:ROWS])
            for t in range(NT):
                ins = pe.transpose(to("rT")[:, (4 + t) * ROWS:(5 + t) * ROWS], cum[0:ROWS, CTX + t * P:CTX + (t + 1) * P],
                                   ident[0:ROWS, 0:ROWS])
            sec.done(ins, "rT")

            def head_scores(h):
                sec.room(pe, f"rb{h}")
                for d in range(2):
                    r = 32 * d + h
                    ins = pe.matmul(to(f"rb{h}")[:, d * T:(d + 1) * T], ident[0:ROWS, r:r + 1].to_broadcast([ROWS, P]),
                                    rmax[0:ROWS, CTX:S2], start=True, stop=True)
                sec.done(ins, f"rb{h}")
                for job, cc in ((f"qk{h}a", 0), (f"qk{h}b", 2)):
                    sec.room(pe, job)
                    for c in (cc, cc + 1):
                        ins = pe.matmul(to(job)[:, (c - cc) * T:(c - cc + 1) * T], qkvT[:, 1, h, c * P:(c + 1) * P],
                                        qkvT[:, 0, h, CTX:S2], start=True, stop=True)
                    sec.done(ins, job)

            def head_values(h):
                for d in range(2):
                    if d == 0:
                        pe.wait_ge(s_ready, h + 1)
                    else:
                        sec.arrived(pe, f"qk{h}b")
                    job = f"o{h}{d}"
                    sec.room(pe, job)
                    for t in range(NT):
                        seen = ((0, 1, 2), (0, 1, 2, 3))[t] if d == 0 else ((0, 1, 2, 3), (0, 1, 3))[t]
                        ins = chain(to(job)[:, t * (DH + 1):(t + 1) * (DH + 1)],
                                    [(E[:, h % 2, d, c, t * P:(t + 1) * P], vtok[:, c, h, :]) for c in seen])
                    sec.done(ins, job)

            head_scores(0)
            for h in range(MH):
                if h + 1 < MH:
                    head_scores(h + 1)
                head_values(h)

            def w_out2(k, c):
                at, slot_at = slice(c * 512, (c + 1) * 512), slice((k % 4) * D + c * 512, (k % 4) * D + (c + 1) * 512)
                high = w_l[:, 3, slot_at] if k >= 4 else (wo_a, wo_b)[k // 2][:, k % 2, at]
                return high, w_l[:, k // 4, slot_at]

            def out_proj2(ks, first, last):
                for n in range(4):
                    t, c = n // 2, n % 2
                    if first:
                        sec.room(pe, f"wo{n}")
                    tok = slice(t * P, (t + 1) * P)
                    pairs = [((fy_h[:, k - 4, tok] if k >= 4 else y_h[:, 4 + k, tok], y_l[:, k, tok]), w_out2(k, c)) for k in ks]
                    ins = split_chain(bank[n][:, :], pairs, first, last)
                    if last:
                        sec.done(ins, f"wo{n}")

            pe.wait_ge(wo_lo, 5)
            out_proj2((4, 5, 6, 7), True, False)
            for p in range(2):
                pe.wait_ge(hn_ready, 1)
                sec.room(pe, f"hT{p}")
                for g in range(2):
                    for t in range(NT):
                        h = 2 * p + g
                        ins = pe.transpose(to(f"hT{p}")[:, g * T + t * P:g * T + (t + 1) * P],
                                           h_rows[:, t, h * DH:(h + 1) * DH], ident)
                sec.done(ins, f"hT{p}")
            pe.wait_ge(wo_lo, 9)
            for h in range(0, MH, 2):
                pe.wait_ge(y_lo, h + 2)
                out_proj2((h, h + 1), False, h + 2 == MH)
            transposes2("t2", XN + 5, xn2)
            for n in range(4):
                sec.arrived(pe, f"t2{n}")
            pe.wait_ge(router_in, 32)
            for t in range(NT):
                sec.room(pe, f"rt{t}")
                sec.done(chain(to(f"rt{t}")[:, 0:NG + NE], [(h_rt[:, k, t * P:(t + 1) * P], w_rt[:, k, :]) for k in range(KD)]),
                         f"rt{t}")
            pe.wait_ge(chosen_ready, 1)
            sec.room(pe, "rank")
            before, ones = const[:, K_BEFORE:K_BEFORE + P], const[:, K_ONES:K_ONES + P]
            chain(to("rank")[:, 0:NE], [(before, chosen[:, 0, :])])
            chain(to("rank")[:, NE:2 * NE], [(ones, chosen[:, 0, :]), (before, chosen[:, 1, :])])
            sec.done(chain(to("rank")[:, 2 * NE:3 * NE], [(ones, chosen[:, t, :]) for t in range(NT)]), "rank")

            def gather(bank_, side, c):
                for kk in range(2):
                    k = 2 * c + kk
                    pairs = [(xn_p[:, t, k * P:(k + 1) * P], choice[:, side, t, :]) for t in range(NT) for xn_p in (xn_h, xn_l)]
                    for n, (lhsT, rhs) in enumerate(pairs):
                        ins = pe.matmul(bank_[:, kk * T:(kk + 1) * T], lhsT, rhs, start=n == 0, stop=n == 3)
                return ins

            def transposed_choice(bank_, side, n, i):
                for t in range(NT):
                    ins = pe.matmul(bank_[:, t * (P + 2):(t + 1) * (P + 2)], choice[:, side, t, n * P:(n + 1) * P],
                                    pick_w[:, i, 2 - 2 * t:P + 4 - 2 * t], start=True, stop=True)
                return ins

            def scatter(i, results=range(4), first=False, last=False):
                for n in results:
                    t, c = n // 2, n % 2
                    if first:
                        sec.room(pe, f"ye{n}")
                    for part in range(2):
                        ins = pe.matmul(bank[n][:, :], choice_t[:, i, t * P:(t + 1) * P],
                                        y2[:, part, c * 512:(c + 1) * 512], start=first and part == 0,
                                        stop=last and part == 1, skip_group_check=True)
                    if last:
                        sec.done(ins, f"ye{n}")

            def expert_pass(q, i, final=False):
                p, side = QUAD * q + i, i // 2
                more = not (final and i >= 2)
                for kind, name in enumerate(("eG", "eU")):
                    pe.wait_ge(lo_ready, 12 * p + 4 * kind + 4)
                    if kind == 0 and i % 2 == 0:
                        pe.wait_ge(xg_ready, 4 * (2 * q + side) + 4)
                    sec.room(pe, name, 2 * p)
                    o = (3 * i + kind) % 4
                    wh, wl = (v.rearrange("p (k n) -> p k n", k=KD) for v in (w_h[:, kind, :], w_l[:, o, :]))
                    xs = [xg[:, side, part, :, (i % 2) * P:(i % 2 + 1) * P] for part in range(2)]
                    sec.done(split_chain(to(name)[:, :], [((xs[0][:, k, :], xs[1][:, k, :]), (wh[:, k, :], wl[:, k, :]))
                                                          for k in range(KD)]), name)
                if more:
                    if i % 2 == 0:
                        pe.wait_ge(choice_ready, 2 * q + side + 2)
                    sec.room(pe, "e7", 10 * q + PIECES[i][0])
                    sec.done(gather(to("e7"), 1 - side, 2 * (i % 2)), "e7")
                sec.arrived(pe, "eD1", 2 * p - 2)
                if i in (1, 3):
                    sec.arrived(pe, "e6", 6 * q - 1 + 3 * (i // 2))
                else:
                    sec.arrived(pe, "e7", 10 * q - 6 + 5 * (i // 2))
                scatter((i - 1) % QUAD, (0, 1))
                sec.arrived(pe, "eU", 2 * p)
                sec.room(pe, "e6", 6 * q + HIDDEN_T[i])
                for j in range(4):
                    ins = pe.transpose(to("e6")[:, j * P:(j + 1) * P], hidden[:, j * P:(j + 1) * P], ident)
                sec.done(ins, "e6")
                scatter((i - 1) % QUAD, (2, 3))
                if more:
                    sec.room(pe, "e7", 10 * q + PIECES[i][1])
                    sec.done(gather(to("e7"), 1 - side, 2 * (i % 2) + 1), "e7")
                pe.wait_ge(lo_ready, 12 * p + 12)
                sec.arrived(pe, "e6", 6 * q + HIDDEN_T[i])
                o = (3 * i + 2) % 4
                for c, name in enumerate(("eD0", "eD1")):
                    sec.room(pe, name, 2 * p)
                    pairs = []
                    for j in range(4):
                        at = slice(j * D + c * 512, j * D + (c + 1) * 512)
                        pairs.append(((aT2[:, 0, j, :], aT2[:, 1, j, :]), (w_h[:, 2, at], w_l[:, o, at])))
                    sec.done(split_chain(to(name)[:, :], pairs), name)
                if more and i % 2:
                    for n, (name, at) in enumerate((("e6", 6 * q + CHOSEN_T6[i]), ("e7", 10 * q + CHOSEN_T7[i]))):
                        sec.room(pe, name, at)
                        sec.done(transposed_choice(to(name), 1 - side, n, (i + 1 + n) % QUAD), name)

            pe.wait_ge(choice_ready, 1)
            for c in range(4):
                sec.room(pe, f"first{c}")
                sec.done(gather(to(f"first{c}"), 0, c), f"first{c}")
            pe.wait_ge(first_weights, 1)
            for n in range(2):
                sec.room(pe, f"first_sT{n}")
                sec.done(transposed_choice(to(f"first_sT{n}"), 0, n, n), f"first_sT{n}")
            pe.wait_ge(y_zero, 3)
            scatter(QUAD - 1, first=True)
            pe.wait_ge(lo_ready, 8)
            with pe.Fori(0, NE // QUAD) as q:
                for i in range(QUAD):
                    expert_pass(q, i)
            pe.wait_ge(table_ready, 1)
            with pe.If(pe.value_load(table_i[0:1, OVER:OVER + 1], min_val=0, max_val=OVER) > 0):
                for i in range(QUAD):
                    expert_pass(NE // QUAD, i, final=True)
                sec.arrived(pe, "eD1", 2 * NPASS - 2)
            sec.arrived(pe, "eD1", 2 * NE - 2)
            scatter(QUAD - 1, last=True)

        @block.scalar
        def _(act):
            act.wait_ge(x_in, 16 * NT)
            with act.Fori(0, DEPTH) as l:
                res = layer_results(l)

                def to(job):
                    return bank[LAY.at[job][0]]

                def copy(job, dst, src, func=ACT.Copy, last=True):
                    ins = act.activation(dst, src, func)
                    if last:
                        res.moved(ins, job)

                def squares(summed):
                    for t in range(NT):
                        summed(t)
                        act.activation(xn[:, t, :], x[:, t, :], ACT.Square, accum_out=ss[:, t:t + 1]).then_inc(ss_ready, 1)

                def rounded_first(dst, src):
                    for n in range(4):
                        at = slice(n * 1024, (n + 1) * 1024)
                        act.activation(dst[:, at], src[:, at], ACT.Copy).then_inc(w1_hi, 1)

                def rounded_in(dst, src, subs):
                    for n in subs:
                        at = slice(n * 1024, (n + 1) * 1024)
                        act.activation(dst[:, at], src[:, at], ACT.Copy).then_inc(in_hi, 1)

                squares(lambda t: act.wait_ge(drained[2 * t + 1], l * LAY.count[2 * t + 1] + 1))
                act.wait_ge(m_in[2], 16 * l + 16)
                rounded_first(dadg_h, m[:, 2, :])
                for n in range(4):
                    t, b = n // 2, n % 2
                    part = (slice(None), slice(4 * b, 4 * b + 4), slice(t * P, (t + 1) * P))
                    res.arrived(act, f"tx1_{t}{b}")
                    act.activation(h1_h[part], hT[part], ACT.Copy).then_inc(h1_rounded, 1)
                act.wait_ge(m_in[0], 32 * l + 16)
                rounded_first(vqi_h, m[:, 0, :])
                act.wait_ge(prm_in, 16 * l + 16)
                for t in range(NT):
                    res.ready(act, f"kwi{t}")
                    act.activation(wi[:, t, :], to(f"kwi{t}")[:, 64:68], ACT.Copy, scale=(H * HD) ** -0.5)
                    copy(f"kwi{t}", zi[:, t, 256:320], to(f"kwi{t}")[:, 0:64])
                res.ready(act, "dg")
                copy("dg", sig, to("dg")[:, :].rearrange("p (g t) -> p g t", g=2), ACT.Sigmoid)
                act.wait_ge(m_in[1], 32 * l + 16)
                rounded_first(dadg_h, m[:, 1, :])

                def vqi_copy(t):
                    res.ready(act, f"vqi{t}")
                    copy(None, zi[:, t, 0:256], to(f"vqi{t}")[:, 256:512], last=False)
                    copy(f"vqi{t}", va[:, t, :], to(f"vqi{t}")[:, 0:256])

                vqi_copy(0)
                act.wait_ge(ab_in, 32 * l + 32)
                rounded_in(fw_l[:, 1, :], blocks_w[:, 0, :], range(4, 6))
                vqi_copy(1)
                rounded_in(fw_l[:, 1, :], blocks_w[:, 0, :], range(4))

                def qk_copy(t):
                    res.ready(act, f"qk{t}")
                    copy(f"qk{t}", zq[:, t, :], to(f"qk{t}")[:, :])

                qk_copy(0)
                act.wait_ge(m_in[3], 16 * l + 16)
                rounded_in(w_l[:, 2, :], m[:, 3, :], range(4))
                qk_copy(1)
                for t in range(NT):
                    res.ready(act, f"riT{t}")
                    copy(f"riT{t}", riT[:, :, t * P:(t + 1) * P], to(f"riT{t}")[:, 0:3 * P].rearrange("p (c q) -> p c q", c=3))
                for job, t, h0 in (("sc0a", 0, 0), ("sc0b", 0, 1), ("sc1a", 1, 0), ("sc1b", 1, 1)):
                    res.ready(act, job)
                    copy(job, rel[t][:, h0::2, :], to(job)[:, 0:2 * (t + 1) * P].rearrange("p (h s) -> p h s", h=2), ACT.Relu)
                for t in range(NT):
                    res.ready(act, f"guv{t}")
                    copy(f"guv{t}", zg[:, t, :], to(f"guv{t}")[:, :])
                for s in range(2):
                    act.wait_ge(m_in[s], 32 * l + 32)
                    rounded_in(w_l[:, 2 + s, :], m[:, s, :], range(4))
                res.ready(act, "ac")
                copy("ac", acs, to("ac")[:, :].rearrange("p (g t) -> p g t", g=2))
                for t in range(NT):
                    res.ready(act, f"rqT{t}")
                    copy(f"rqT{t}", rqT[:, :, t * P:(t + 1) * P], to(f"rqT{t}")[:, :].rearrange("p (c q) -> p c q", c=4))
                def rounded_mix(g, job):
                    res.arrived(act, job)
                    act.activation(y_h[:, 2 * g:2 * g + 2, :], yT[:, 2 * g:2 * g + 2, :], ACT.Copy).then_inc(mix_rounded, 1)

                rounded_mix(0, "ab")
                res.ready(act, "ybT")
                copy("ybT", yT[:, 2:4, :], to("ybT")[:, :].rearrange("p (k t) -> p k t", k=2))
                rounded_mix(1, "ybT")
                res.ready(act, "cnT")
                for g in range(2):
                    ins = act.activation(yT[:, 6 + g, :], to("cnT")[:, g * T:(g + 1) * T], ACT.Silu,
                                         scale=prm[:, C_LNG + g:C_LNG + g + 1], bias=prm[:, C_LNB + g:C_LNB + g + 1])
                res.moved(ins, "cnT")
                rounded_mix(3, "cnT")
                for t in range(NT):
                    act.wait_ge(lg_ready, 2 * l + t + 1)
                    for h in range(H):
                        act.activation(lg[t][:, h, :], lg[t][:, h, :], ACT.Exp, scale=HD ** -0.5, bias=nms[:, t, h:h + 1],
                                       accum_out=rsum[:, t, h:h + 1]).then_inc(exp_ready, 1)
                def rounded(slot, r, subs):
                    if 0 in subs:
                        act.wait_ge(gu_in[slot], 16 * ((B0, B1)[slot] * l + r + 1))
                    else:
                        act.wait_ge(down_in[slot], 16 * ((B0, B1)[slot] * l + r + 1))
                    for n in subs:
                        at = slice(n * SUB, (n + 1) * SUB)
                        act.activation(fw_h[:, 1 - slot, at], blocks_w[:, slot, at], ACT.Copy).then_inc(ffn_hi, 1)

                for job, dst in (("pT0", pT0), ("pT1a", pT1[:, 0]), ("pT1b", pT1[:, 1])):
                    res.ready(act, job)
                    copy(job, dst, to(job)[:, :].rearrange("p (h q) -> p h q", h=H))
                rounded(0, 0, range(0, 4))
                res.ready(act, "ycT")
                copy("ycT", yT[:, 4:6, :], to("ycT")[:, :].rearrange("p (k t) -> p k t", k=2))
                rounded_mix(2, "ycT")

                rounded(0, 0, range(4, 6))
                squares(lambda t: res.arrived(act, f"wo{2 * t + 1}"))
                for n in range(4):
                    t, b = n // 2, n % 2
                    res.arrived(act, f"tx2_{t}{b}")
                    part = (slice(None), slice(4 * b, 4 * b + 4), slice(t * P, (t + 1) * P))
                    act.activation(h_h[part], h_full[part], ACT.Copy).then_inc(h_rounded, 1)

                def ffn_silu(j, i):
                    res.ready(act, f"gu{j}", i)
                    act.activation(sga[:, j, :], to(f"gu{j}")[:, 0:T], ACT.Silu).then_inc(silu_ready, 1)

                with act.Fori(0, B1) as r:
                    for s in range(2):
                        ffn_silu(0, 2 * r + s)
                        rounded(1 - s, r + s, range(0, 4))
                        ffn_silu(1, 2 * r + s)
                        rounded(1 - s, r + s, range(4, 6))
                for j in range(2):
                    ffn_silu(j, NFB - 1)

            def to(job):
                return bank[SEC.at[job][0]]

            def copy(job, dst, src):
                sec.ready(act, job)
                sec.moved(act.activation(dst, src, ACT.Copy), job)

            act.wait_ge(prm2_in, 16)
            act.activation(cs.rearrange("p k r -> p r k"), prm2[:, C2_C:C2_C + 2 * KD].rearrange("p (r k) -> p r k", r=2),
                           ACT.Silu).then_inc(silu_c, 1)

            def rounded_chunk(i, s):
                act.wait_ge(ada_in[s], 16 * before_ada[s] + 16 * i + 16)
                for j in range(4):
                    at = slice(j * 1024, (j + 1) * 1024)
                    act.activation(ada_h[s % 2][:, at], ada_w[s][:, at], ACT.Copy).then_inc(ada_hi, 1)

            act.wait_ge(block_used[1], B1 * DEPTH + 1)
            for n in range(2 * ADA):
                if n == 1:
                    act.wait_ge(drained[3], DEPTH * LAY.count[3] + 1)
                    for t in range(NT):
                        act.activation(xn2[:, 0, :], x[:, t, :], ACT.Square, accum_out=ss[:, t:t + 1]).then_inc(ss_ready, 1)
                        act.wait_ge(ss_ready, 4 * DEPTH + t + 1)
                if n >= 2:
                    sec.ready(act, f"ada{(n - 2) % ADA}", (n - 2) // ADA)
                rounded_chunk(n // ADA, n % ADA)
            act.wait_ge(x_ready, 2)
            act.wait_ge(ctx_in, 32)
            for n, (src, o) in enumerate(((ctx_x, 2), (x, 0))):
                for t in range(NT):
                    act.activation(xn2[:, 0, :], src[:, t, :], ACT.Square, accum_out=ss[:, o + t:o + t + 1])\
                       .then_inc(ss_ready, 1)
                    act.wait_ge(ss_ready, 4 * DEPTH + 2 + 2 * n + t + 1)

            def rounded_columns(s, high):
                act.wait_ge(m_in[s], (M01, M01, M23)[s] + 16)
                for j in range(4):
                    at = slice(j * 1024, (j + 1) * 1024)
                    act.activation(high[:, at], m[:, s, at], ACT.Copy).then_inc(w2_hi, 1)

            sec.ready(act, "ada4", 1)
            rounded_columns(0, xm_h)

            def gate(q):
                for n in (2 * q, 2 * q + 1):
                    copy(f"gate{n}", gb[:, q, (n % 2) * 512:(n % 2 + 1) * 512], to(f"gate{n}")[:, :])

            gate(0)
            gate(1)

            def modulated(name, dst, kind, row, high=None, pieces=range(4)):

                def rounded_rows(n):
                    sec.arrived(act, f"{name}{n}")
                    act.activation(high[:, 2 * n:2 * n + 2, :], dst[:, 2 * n:2 * n + 2, :], ACT.Copy).then_inc(h2_rounded, 1)

                for n in pieces:
                    sec.ready(act, f"{name}{n}")
                    for k in range(2):
                        f = 2 * n + k
                        ins = act.activation(dst[:, f, :], to(f"{name}{n}")[:, k * T:(k + 1) * T], ACT.Identity,
                                             scale=modc[:, kind + 1, f, row:row + 1], bias=modc[:, kind, f, row:row + 1])
                    sec.moved(ins, f"{name}{n}")
                    if high is not None and n:
                        if n == 1:
                            sec.ready(act, f"{name}3")
                        rounded_rows(n - 1)
                if high is not None:
                    rounded_rows(3)

            act.wait_ge(mod_ready, 1)
            modulated("tc", hC, 0, 1, hc_h)
            modulated("tl", hT, 0, 0, h1_h)
            sec.ready(act, "ada5", 1)
            rounded_columns(1, z_h)
            act.wait_ge(zeros_ready, 1)
            for j in range(MH):
                copy(f"xm{j}", xmp[:, j, :, 1:1 + CTX], to(f"xm{j}")[:, :].rearrange("p (s t) -> p s t", s=2))
            for q in range(2):
                sec.ready(act, f"z{q}")
                sec.moved(act.activation(szT[:, 2 * q:2 * q + 2, :], to(f"z{q}")[:, :].rearrange("p (g t) -> p g t", g=2),
                                         ACT.Silu), f"z{q}")
            for j in range(MH):
                act.wait_ge(pre_ready, j + 1)
                act.activation(actT[:, j, :].rearrange("p (s t) -> p s t", s=2), pre[:, j % 2], ACT.Silu,
                               bias=prm2[:, C2_CONVB + j:C2_CONVB + j + 1]).then_inc(act_ready, 1)
            for n in range(12):
                if n % 3 < 2:
                    copy(f"qkv{n}", qkvT[:, n % 3, n // 3, :], to(f"qkv{n}")[:, :])
            rounded_columns(2, u_h)
            sec.ready(act, "gates")
            act.activation(gi[0:ROWS, :], to("gates")[0:ROWS, :], ACT.Identity, bias=prm2[0:ROWS, C2_IG:C2_IG + 1])
            sec.moved(act.activation(gf[0:ROWS, :], to("gates")[64:64 + ROWS, :], ACT.Copy), "gates")
            act.wait_ge(f_abs, 1)
            act.activation(gx[0:ROWS, :], gx[0:ROWS, :], ACT.Exp).then_inc(f_log, 1)
            act.wait_ge(f_log, 1)
            act.activation(gx[0:ROWS, :], gx[0:ROWS, :], ACT.Ln, bias=1.0).then_inc(f_log, 1)
            for t in range(NT):
                copy(f"u{t}", u_rows[:, t, :], to(f"u{t}")[:, :])
            for g in range(4):
                copy(f"fp{g}", fP[:, g, :], to(f"fp{g}")[:, :])
            for p in range(2):
                copy(f"ff{p}", fT[:, 2 * p:2 * p + 2, :], to(f"ff{p}")[:, :].rearrange("p (g t) -> p g t", g=2))
            for p in range(2):
                copy(f"fy{p}", yT[:, 4 + 2 * p:6 + 2 * p, :], to(f"fy{p}")[:, :].rearrange("p (g t) -> p g t", g=2))
            sec.ready(act, "rT")
            act.activation(rcol, to("rT")[:, 0:4 * ROWS].rearrange("p (c r) -> p c r", c=4), ACT.Copy)
            sec.moved(act.activation(emn, to("rT")[:, 4 * ROWS:6 * ROWS].rearrange("p (t r) -> p t r", t=NT), ACT.Exp,
                                     scale=-1.0), "rT")
            sec.arrived(act, "rT")
            act.wait_ge(zeros_ready, 4)
            for h in range(MH):
                sec.ready(act, f"rb{h}")
                for d in range(2):
                    for c in range(4):
                        lo = P if (d, c) == (0, 3) else 0
                        hi = P if (d, c) == (1, 2) else T
                        ins = act.activation(E[:, h % 2, d, c, lo:hi], to(f"rb{h}")[:, d * T + lo:d * T + hi], ACT.Exp,
                                             scale=-1.0, bias=rcol[:, c, 32 * d + h:32 * d + h + 1])
                sec.moved(ins, f"rb{h}")
                if h == 1:
                    for p in range(2):
                        sec.arrived(act, f"fy{p}")
                    act.activation(fy_h[:, :, :], yT[:, 4:8, :], ACT.Copy).then_inc(wo_hi, 1)
                    act.wait_ge(m_in[1], M01 + 32)
                    for j in range(4):
                        act.activation(w_l[:, 3, j * D:(j + 1) * D], m[:, 1, j * D:(j + 1) * D], ACT.Copy).then_inc(wo_hi, 1)
            act.wait_ge(m_in[0], M01 + 32)
            for j in range(4):
                act.activation((wo_a, wo_b)[j // 2][:, j % 2, :], m[:, 0, j * D:(j + 1) * D], ACT.Copy).then_inc(wo_hi, 1)
            for p in range(2):
                sec.ready(act, f"hT{p}")
                for g in range(2):
                    h = 2 * p + g
                    ins = act.activation(hm[:, h, :], to(f"hT{p}")[:, g * T:(g + 1) * T], ACT.Identity,
                                         scale=prm2[:, C2_NORM + h:C2_NORM + h + 1])
                sec.moved(ins, f"hT{p}")
            for h in range(MH):
                act.wait_ge(y_ready, h + 1)
                act.activation(y_h[:, 4 + h, :], yT[:, h, :], ACT.Copy).then_inc(y_hi, 1)

            def result_squares(name, squares):
                for n in range(4):
                    sec.ready(act, f"{name}{n}")
                    act.activation(squares[n], bank[n][:, :], ACT.Square, accum_out=ss[:, n:n + 1]).then_inc(ss_ready, 1)

            result_squares("wo", [qkvT[:, 0, n, :] for n in range(4)])
            for t in range(NT):
                act.wait_ge(x_ready, 2 + t + 1)
                act.activation(xn2[:, t, :], x[:, t, :], ACT.Square, accum_out=ss[:, t:t + 1]).then_inc(ss_ready, 1)
            modulated("t2", h_rt, 2, 0, pieces=(0, 1))

            def rounded(q, c, subs=range(4)):
                act.wait_ge(piece_in[c % 4], 16 * (3 * q + c // 4) + 16)
                for j in subs:
                    at = slice(j * 1024, (j + 1) * 1024)
                    act.activation(w_h[:, c % 3, at], m[:, c % 4, at], ACT.Copy).then_inc(hi_ready, 1)

            for c in range(2):
                rounded(0, c)
            act.wait_ge(g_diff, 1)
            act.activation(ge, gd, ACT.Exp).then_inc(g_exp, 1)
            act.wait_ge(e_diff, 1)
            act.activation(t3, t3, ACT.Exp).then_inc(e_exp, 1)

            def gathered(name, side, c, n, at):
                sec.ready(act, name, at)
                for kk in range(2):
                    k = 2 * c + kk
                    ins = act.activation(xg_full[:, side, 1, k, :], to(name)[:, kk * T:(kk + 1) * T], ACT.Identity,
                                         scale=modc[:, 3, k, 0:1], bias=modc[:, 2, k, 0:1])
                    if kk == 0:
                        ins.then_inc(xg_moved, 1)
                sec.moved(ins, name)

            def rounded_tokens(name, side, c, n, at):
                act.wait_ge(xg_moved, n + 1)
                sec.arrived(act, name, at)
                act.activation(xg[:, side, 0, 2 * c:2 * c + 2, :], xg_full[:, side, 1, 2 * c:2 * c + 2, :], ACT.Copy)\
                    .then_inc(xg_rounded, 1)

            def choices(name, i, n):
                act.wait_ge(slot_ready, n + 1)
                sec.moved(act.activation(choice_t[:, i, :].rearrange("p (t q) -> p t q", t=NT),
                                         to(name)[:, 0:2 * (P + 4)].rearrange("p (t c) -> p t c", t=NT)[:, :, 0:P], ACT.Copy),
                          name)

            def expert_pass(q, i, final=False):
                p, side = QUAD * q + i, i // 2
                more = not (final and i >= 2)
                rounded(q, 3 * i + 2)
                sec.ready(act, "eG", 2 * p)
                sec.moved(act.activation(hidden, to("eG")[:, :], ACT.Silu), "eG")
                if not (final and i == QUAD - 1):
                    rounded(q, 3 * i + 3)
                up = not (final and i == QUAD - 1)
                for c in range(2):
                    tokens = "e7", 1 - side, 2 * (i % 2) + c, 2 * p + 4 + c, 10 * q + PIECES[i][c]
                    if c and up:
                        rounded(q, 3 * i + 4, (0,))
                    if more:
                        gathered(*tokens)
                    if c == 0:
                        sec.ready(act, "e6", 6 * q + HIDDEN_T[i])
                        act.activation(aT2[:, 0].rearrange("p j s -> p (j s)"), to("e6")[:, :], ACT.Copy)\
                            .then_inc(hidden_rounded, 1)
                    if more:
                        rounded_tokens(*tokens)
                act.wait_ge(slot_ready, p + 1)
                for c, name in enumerate(("eD0", "eD1")):
                    if up:
                        rounded(q, 3 * i + 4, ((1,), (2, 3))[c])
                    sec.ready(act, name, 2 * p)
                    act.activation(y2[:, 0, c * 512:(c + 1) * 512], to(name)[:, :], ACT.Copy, scale=slot_w[:, i:i + 1])\
                        .then_inc(y_rounded, 1)
                if more and i % 2:
                    for n, name in enumerate(("e6", "e7")):
                        choices(name, (i + 1 + n) % QUAD, p + 1 + n)

            for c in range(4):
                gathered(f"first{c}", 0, c, c, 0)
                rounded_tokens(f"first{c}", 0, c, c, 0)
            act.wait_ge(y_zero, 3)
            for n in range(2):
                choices(f"first_sT{n}", n, n)
            with act.Fori(0, NE // QUAD) as q:
                for i in range(QUAD):
                    expert_pass(q, i)
            act.wait_ge(table_ready, 1)
            with act.If(act.value_load(table_i[0:1, OVER:OVER + 1], min_val=0, max_val=OVER) > 0):
                for i in range(QUAD):
                    expert_pass(NE // QUAD, i, final=True)
            result_squares("ye", [xn2[:, n // 2, (n % 2) * 512:(n % 2 + 1) * 512] for n in range(4)])

        @block.vector
        def _(dve):
            dve.memset(half[:, :], -0.5).then_inc(half_ready, 1)
            dve.wait_ge(const_in, 16)
            with dve.Fori(0, DEPTH) as l:
                res = layer_results(l)
                S = Steps(dve, dve_step, l * DVE_STEPS)

                def to(job):
                    return bank[LAY.at[job][0]]

                def col(c):
                    return prm[:, c:c + 1]

                def norm(n):
                    for t in range(NT):
                        dve.wait_ge(rstd_ready, 4 * l + 2 * n + t + 1)
                        dve.tensor_scalar(xn[:, t, :], x[:, t, :], rstd[:, t:t + 1], None, ALU.mult).then_inc(xn_ready, 1)

                def gained_piece(name, gain, dst, n):
                    t, b = n // 2, n % 2
                    job = f"{name}_{t}{b}"
                    res.ready(dve, job)
                    g = prm[:, gain + 4 * b:gain + 4 * b + 4].unsqueeze(2).to_broadcast([P, 4, P])
                    res.moved(dve.tensor_tensor(dst[:, 4 * b:4 * b + 4, t * P:(t + 1) * P],
                                                to(job)[:, :].rearrange("p (k q) -> p k q", k=4), g, ALU.mult), job)

                def rest_first(n0, s, high):
                    for n in (2, 3):
                        at = slice(n * 1024, (n + 1) * 1024)
                        dve.wait_ge(w1_hi, 12 * l + n0 + n + 1)
                        dve.tensor_tensor(w_l[:, s, at], m[:, s, at], f32(high[:, at]), ALU.subtract).then_inc(w1_lo, 1)

                def rest_of_h1(n):
                    t, b = n // 2, n % 2
                    part = (slice(None), slice(4 * b, 4 * b + 4), slice(t * P, (t + 1) * P))
                    dve.wait_ge(h1_rounded, 4 * l + n + 1)
                    dve.tensor_tensor(h1_l[part], hT[part], f32(h1_h[part]), ALU.subtract).then_inc(h1_ready, 1)

                norm(0)
                dve.wait_ge(prm_in, 16 * l + 16)
                for n in range(4):
                    gained_piece("tx1", C_GMIX, hT, n)
                rest_first(0, 2, dadg_h)
                for n in range(4):
                    rest_of_h1(n)
                rest_first(4, 0, vqi_h)
                def rest_in(n0, slot_of, h_of, subs):
                    for i, n in enumerate(subs):
                        at = slice(n * 1024, (n + 1) * 1024)
                        dve.wait_ge(in_hi, IN_SUBS * l + n0 + i + 1)
                        dve.tensor_tensor(slot_of[0][:, at], slot_of[1][:, at], f32(h_of[:, at]), ALU.subtract).then_inc(in_lo, 1)

                S.then(dve.memset(cpad[:, :, 0:LONG - 1], 0.0))
                res.ready(dve, "da")
                res.arrived(dve, "dg")
                res.moved(dve.tensor_tensor(cpad[:, :, LONG - 1:], to("da")[:, :].rearrange("p (g t) -> p g t", g=2), sig,
                                            ALU.mult), "da")
                res.arrived(dve, "da")
                tap_done = [0, 0]

                def taps(ws):
                    for w in ws:
                        for g in range(2):
                            c, shifted = col(C_LONG + 2 * w + g), cpad[:, g, w:w + T]
                            if w == 0:
                                ins = dve.tensor_scalar(conv[:, g, :], shifted, c, col(C_BCONF + g), ALU.mult, ALU.add)
                            else:
                                S.need(tap_done[g])
                                ins = dve.scalar_tensor_tensor(conv[:, g, :], shifted, c, conv[:, g, :], ALU.mult, ALU.add)
                            if (w, g) == (LONG - 1, 1):
                                ins.then_inc(conv_ready, 1)
                            else:
                                tap_done[g] = S.did(ins)

                def rotate(t):
                    res.arrived(dve, f"kwi{t}")
                    res.arrived(dve, f"vqi{t}")
                    z5 = zi[:, t, :].rearrange("p (h d) -> p h d", h=5)
                    hd = HD // 2
                    S.did(dve.tensor_tensor(ra, z5, cos2[:, t, :].unsqueeze(1).to_broadcast([P, 5, HD]), ALU.mult))
                    S.did(dve.tensor_tensor(rb[:, :, 0:hd], z5[:, :, hd:HD],
                                            sin2[:, t, 0:hd].unsqueeze(1).to_broadcast([P, 5, hd]), ALU.mult))
                    S.then(dve.tensor_tensor(rb[:, :, hd:HD], z5[:, :, 0:hd],
                                             sin2[:, t, hd:HD].unsqueeze(1).to_broadcast([P, 5, hd]), ALU.mult))
                    S.then(dve.tensor_tensor(ri[:, t, 0:5, :], ra, rb, ALU.add))
                    dve.tensor_copy(ri[:, t, 5, :], ri[:, t, 4, :]).then_inc(ri_ready, 1)

                taps(range(0, 4))
                rest_first(8, 1, dadg_h)
                rotate(0)
                taps(range(4, 8))
                rotate(1)
                taps(range(8, 11))
                rest_in(6, (w_l[:, 3, :], m[:, 3, :]), w_l[:, 2, :], range(4))
                taps(range(11, TAPS_FIRST))
                for t in range(NT):
                    for job in (f"sc{t}a", f"sc{t}b"):
                        res.arrived(dve, job)
                    for j in range(H):
                        w = wi[:, t, j:j + 1]
                        if j == 0:
                            ins = dve.tensor_scalar(score[t], rel[t][:, 0, :], w, None, ALU.mult)
                        else:
                            ins = dve.scalar_tensor_tensor(score[t], rel[t][:, j, :], w, score[t], ALU.mult, ALU.add)
                        if j < H - 1:
                            S.then(ins)
                    ins.then_inc(score_ready, 1)
                for t in range(NT):
                    dve.wait_ge(score_masked, 2 * l + t + 1)
                settle(dve, passed)
                for r in range(TOPK // 8):
                    src = score if r == 0 else work
                    for t in range(NT):
                        n = S.did(dve.max(mx[:, t, :], src[t]))
                    taps(range(TAPS_FIRST, LONG)[2 * r:2 * r + 1])
                    S.need(n)
                    settle(dve, passed)
                    for t in range(NT):
                        n = S.did(dve.match_replace(work[t], mx[:, t, :], src[t], TAKEN))
                    taps(range(TAPS_FIRST, LONG)[2 * r + 1:2 * r + 2])
                    if r == 3:
                        for t in range(NT):
                            res.arrived(dve, f"guv{t}")
                            v_stats = S.did(dve.bn_stats(bnst[:, t, :], zg[:, t, G:2 * G]))
                    if r == 4:
                        S.need(v_stats)
                        settle(dve, passed)
                        for t in range(NT):
                            ins = dve.bn_aggr(bnag[:, t, :], bnst[:, t, :])
                        ins.then_inc(var_ready, 1)
                    if r == 6:
                        dve.wait_ge(norm_rstd, 2 * l + 1)
                        for t in range(NT):
                            dve.tensor_scalar(zg[:, t, G:2 * G], zg[:, t, G:2 * G], bnag[:, t, 0:1], rstd[:, 2 + t:3 + t],
                                              ALU.subtract, ALU.mult).then_inc(v_norm, 1)
                    S.need(n)
                    settle(dve, passed)
                for t in range(NT):
                    dve.tensor_scalar(sel[t], work[t], TAKEN, 1.0, ALU.is_equal, ALU.subtract).then_inc(sel_ready, 1)
                res.ready(dve, "cvT")
                for t in range(NT):
                    n = S.did(dve.bn_stats(bnst[:, 2 + t, :], to("cvT")[:, t * T:(t + 1) * T]))
                S.need(n)
                settle(dve, passed)
                for t in range(NT):
                    ins = dve.bn_aggr(bnag[:, 2 + t, :], bnst[:, 2 + t, :])
                ins.then_inc(var_ready, 1)
                S.then(dve.memset(chp[:, :, 0:SHORT - 1], 0.0))
                res.ready(dve, "ah")
                res.arrived(dve, "ac")
                res.moved(dve.tensor_tensor(chp[:, :, SHORT - 1:], to("ah")[:, :].rearrange("p (g t) -> p g t", g=2), acs,
                                            ALU.mult), "ah")
                res.arrived(dve, "ah")
                for w in range(SHORT):
                    for g in range(2):
                        c, shifted = col(C_SHORT + 2 * w + g), chp[:, g, w:w + T]
                        if w == 0:
                            n = S.did(dve.tensor_scalar(chy[:, g, :], shifted, c, None, ALU.mult))
                        else:
                            S.need(n - 1)
                            n = S.did(dve.scalar_tensor_tensor(chy[:, g, :], shifted, c, chy[:, g, :], ALU.mult, ALU.add))
                S.need(n)
                res.ready(dve, "ab")
                res.moved(dve.tensor_tensor(yT[:, 0:2, :], to("ab")[:, :].rearrange("p (g t) -> p g t", g=2), chy, ALU.mult), "ab")
                dve.wait_ge(norm_rstd, 2 * l + 2)
                for t in range(NT):
                    ins = dve.tensor_scalar(conv_n[:, t, :], to("cvT")[:, t * T:(t + 1) * T], bnag[:, 2 + t, 0:1],
                                            rstd[:, 4 + t:5 + t], ALU.subtract, ALU.mult)
                res.moved(ins, "cvT")

                def rest_of_mix(g, n):
                    dve.wait_ge(mix_rounded, 4 * l + n)
                    part = (slice(None), slice(2 * g, 2 * g + 2), slice(None))
                    dve.tensor_tensor(y_l[part], yT[part], f32(y_h[part]), ALU.subtract).then_inc(mix_ready, 1)

                for t in range(NT):
                    res.ready(dve, f"mix{t}")
                    yb = ycat[:, t, 0, :]
                    res.moved(dve.tensor_tensor(yb.rearrange("p (h d) -> p h d", h=H),
                                                to(f"mix{t}")[:, 0:G].rearrange("p (h d) -> p h d", h=H),
                                                prm[:, C_BS:C_BS + H].unsqueeze(2).to_broadcast([P, H, HD]), ALU.add), f"mix{t}")
                    res.arrived(dve, f"mix{t}")
                    dve.tensor_tensor(yb, yb, zg[:, t, 0:G], ALU.mult).then_inc(yb_ready, 1)
                rest_in(12, (w_l[:, 0, :], m[:, 0, :]), w_l[:, 2, :], (2, 3))
                for n, g in enumerate((0, 1)):
                    rest_of_mix(g, n + 1)
                for t in range(NT):
                    dve.wait_ge(sel_masked, 2 * l + t + 1)
                    nk = (t + 1) * P
                    for job, h0 in ((f"lg{t}a", 0), (f"lg{t}b", 1)):
                        res.ready(dve, job)
                        res.moved(dve.scalar_tensor_tensor(lg[t][:, h0::2, :], sel[t].unsqueeze(1).to_broadcast([P, 2, nk]),
                                                           -NEG, to(job)[:, 0:2 * nk].rearrange("p (h s) -> p h s", h=2),
                                                           ALU.mult, ALU.add), job)
                        res.arrived(dve, job)
                    S.then(dve.tensor_reduce(nmx[:, t, :], lg[t], AX.X, ALU.max, negate=True))
                    dve.tensor_scalar(nms[:, t, :], nmx[:, t, :], HD ** -0.5, None, ALU.mult).then_inc(lg_ready, 1)
                rest_of_mix(3, 3)
                for t in range(NT):
                    dve.wait_ge(exp_ready, 8 * l + 4 * t + 4)
                    S.then(dve.reciprocal(rinv[:, t, :], rsum[:, t, :]))
                    res.ready(dve, f"av{t}")
                    res.moved(dve.tensor_tensor(ycat[:, t, 1, :].rearrange("p (h d) -> p h d", h=H),
                                                to(f"av{t}")[:, 0:G].rearrange("p (h d) -> p h d", h=H),
                                                rinv[:, t, :].unsqueeze(2).to_broadcast([P, H, HD]), ALU.mult), f"av{t}")

                def add_to_x(name):
                    for n in range(4):
                        res.ready(dve, f"{name}{n}")
                        part = x[:, n // 2, (n % 2) * 512:(n % 2 + 1) * 512]
                        res.moved(dve.tensor_tensor(part, part, bank[n][:, :], ALU.add), f"{name}{n}")

                def rest_of_block(slot, b, subs):
                    for n in subs:
                        at = slice(n * SUB, (n + 1) * SUB)
                        dve.wait_ge(ffn_hi, SUBS * (NFB * l + b) + n + 1)
                        dve.tensor_tensor(fw_l[:, slot, at], blocks_w[:, slot, at], f32(fw_h[:, 1 - slot, at]), ALU.subtract)\
                            .then_inc(ffn_lo, 1)

                rest_of_block(0, 0, range(0, 4))
                rest_of_mix(2, 4)
                add_to_x("wo")
                norm(1)
                def rest_of_h(n):
                    t, b = n // 2, n % 2
                    part = (slice(None), slice(4 * b, 4 * b + 4), slice(t * P, (t + 1) * P))
                    dve.wait_ge(h_rounded, 4 * l + n + 1)
                    dve.tensor_tensor(h_l[part], h_full[part], f32(h_h[part]), ALU.subtract).then_inc(h_ready, 1)

                for n in range(4):
                    gained_piece("tx2", C_GFFN, h_full, n)
                    if n:
                        rest_of_h(n - 1)
                rest_of_h(3)
                rest_of_block(0, 0, range(4, 6))

                def ffn_hidden(j, i):
                    dve.wait_ge(silu_ready, 2 * NFB * l + 2 * i + j + 1)
                    dve.tensor_tensor(sga[:, j, :], sga[:, j, :], to(f"gu{j}")[:, T:2 * T], ALU.mult).then_inc(a_step, 1)
                    dve.wait_ge(a_step, 4 * (NFB * l + i) + 2 * j + 1)
                    dve.tensor_copy(a2[:, 0, j, :], sga[:, j, :]).then_inc(a_step, 1)
                    dve.wait_ge(a_step, 4 * (NFB * l + i) + 2 * j + 2)
                    res.moved(dve.tensor_tensor(a2[:, 1, j, :], sga[:, j, :], f32(a2[:, 0, j, :]), ALU.subtract), f"gu{j}")

                with dve.Fori(0, B1) as r:
                    for s in range(2):
                        ffn_hidden(0, 2 * r + s)
                        rest_of_block(1 - s, 2 * r + s + 1, range(0, 4))
                        ffn_hidden(1, 2 * r + s)
                        rest_of_block(1 - s, 2 * r + s + 1, range(4, 6))
                for j in range(2):
                    ffn_hidden(j, NFB - 1)
                add_to_x("y")
                assert S.n == DVE_STEPS, S.n

            S = Steps(dve, dve_step, DEPTH * DVE_STEPS)

            def to(job):
                return bank[SEC.at[job][0]]

            def copy(job, dst, src):
                sec.ready(dve, job)
                sec.moved(dve.tensor_copy(dst, src), job)

            def normed(count, src, dst, o):
                for t in range(NT):
                    dve.wait_ge(rstd_ready, 4 * DEPTH + count + t + 1)
                    dve.tensor_scalar(dst[:, t, :], src[:, t, :], rstd[:, o + t:o + t + 1], None, ALU.mult).then_inc(xn_ready, 1)

            dve.wait_ge(silu_c, 1)
            dve.tensor_copy(cs2[:, 0], cs).then_inc(cs_ready, 1)
            dve.wait_ge(cs_ready, 1)
            dve.tensor_tensor(cs2[:, 1], cs, f32(cs2[:, 0]), ALU.subtract).then_inc(cs_ready, 1)

            def rest_of_chunk(i, s):
                for j in range(1, 4):
                    at = slice(j * 1024, (j + 1) * 1024)
                    dve.wait_ge(ada_hi, 4 * (ADA * i + s) + j + 1)
                    dve.tensor_tensor(ada_l[s][:, at], ada_w[s][:, at], f32(ada_h[s % 2][:, at]), ALU.subtract).then_inc(ada_lo, 1)

            def add_rows(i, s):
                sec.ready(dve, f"ada{s}", i)
                part = modrow[:, (ADA * i + s) * 512:(ADA * i + s + 1) * 512]
                sec.moved(dve.tensor_tensor(part, part, bank[s][0:2, :], ALU.add), f"ada{s}")

            rest_of_chunk(0, 0)
            dve.wait_ge(rows_in, 16)
            for n in range(2 * ADA):
                if n + 1 < 2 * ADA:
                    rest_of_chunk((n + 1) // ADA, (n + 1) % ADA)
                if n == 3:
                    dve.wait_ge(drained[3], DEPTH * LAY.count[3] + 1)
                    dve.wait_ge(pos_in, 32)
                    dve.wait_ge(rstd_ready, 4 * DEPTH + 2)
                    for t in range(NT):
                        S.then(dve.scalar_tensor_tensor(x[:, t, :], x[:, t, :], rstd[:, t:t + 1], gfin, ALU.mult, ALU.mult))
                        dve.tensor_tensor(x[:, t, :], x[:, t, :], pos[:, t, :], ALU.add).then_inc(x_ready, 1)
                add_rows(n // ADA, n % ADA)
            for s in range(ADA):
                sec.arrived(dve, f"ada{s}", 1)
            dve.wait_ge(gains_in, 32)
            for q in range(2):
                part = modrow[:, (2 + 3 * q) * D:(3 + 3 * q) * D]
                dve.tensor_tensor(part, part, gpost[q], ALU.mult).then_inc(gate_rows, 1)
            copy("modT", modc.rearrange("p n k r -> p (n k r)"), to("modT")[:, 0:64])
            sec.arrived(dve, "modT")
            for kind, gain in ((1, C2_PREMIX), (3, C2_PREFFN)):
                S.then(dve.tensor_scalar(modc[:, kind], modc[:, kind], 1.0, None, ALU.add))
                ins = dve.tensor_tensor(modc[:, kind], modc[:, kind],
                                        prm2[:, gain:gain + KD].unsqueeze(2).to_broadcast([P, KD, 2]), ALU.mult)
                if kind == 1:
                    S.then(ins)
            ins.then_inc(mod_ready, 1)
            normed(2, ctx_x, ctx_x, 2)
            dve.wait_ge(rstd_ready, 4 * DEPTH + 6)
            normed(4, x, xn2, 0)

            def rest_of_columns(s, high, subs=range(4)):
                for j in subs:
                    at = slice(j * 1024, (j + 1) * 1024)
                    dve.wait_ge(w2_hi, 4 * s + j + 1)
                    dve.tensor_tensor(w_l[:, s, at], m[:, s, at], f32(high[:, at]), ALU.subtract).then_inc(w2_lo, 1)

            def rest_of_rows(q, dst, src, high):
                for n in range(4):
                    part = (slice(None), slice(2 * n, 2 * n + 2), slice(None))
                    dve.wait_ge(h2_rounded, 4 * q + n + 1)
                    dve.tensor_tensor(dst[part], src[part], f32(high[part]), ALU.subtract).then_inc(h2_ready, 1)

            rest_of_columns(0, xm_h, (2, 3))
            rest_of_rows(0, h_l, hC, hc_h)
            rest_of_rows(1, hl_l, hT, h1_h)
            rest_of_columns(1, z_h)
            for j in range(MH):
                sec.arrived(dve, f"xm{j}")
                if j >= 2:
                    dve.wait_ge(act_ready, j - 1)
                for w in range(3):
                    c, shifted = prm2[:, C2_CONV + 4 * w + j:C2_CONV + 4 * w + j + 1], xmp[:, j, :, w:w + CTX]
                    if w == 0:
                        S.then(dve.tensor_scalar(pre[:, j % 2], shifted, c, None, ALU.mult))
                    else:
                        ins = dve.scalar_tensor_tensor(pre[:, j % 2], shifted, c, pre[:, j % 2], ALU.mult, ALU.add)
                        if w == 1:
                            S.then(ins)
                ins.then_inc(pre_ready, 1)
            dve.wait_ge(zeros_ready, 2)
            for c in range(4):
                copy(f"vt{c}", vtok[:, c, :, 0:DH], to(f"vt{c}")[:, :].rearrange("p (h d) -> p h d", h=MH))
            for j in range(MH):
                n = 3 * j + 2
                copy(f"qkv{n}", qkvT[:, 2, j, :], to(f"qkv{n}")[:, :])
            rest_of_columns(2, u_h)
            sec.arrived(dve, "gates")
            S.then(dve.tensor_scalar(gf[0:ROWS, :], gf[0:ROWS, :], prm2[0:ROWS, C2_FG:C2_FG + 1], None, ALU.add))
            dve.scalar_tensor_tensor(gx[0:ROWS, :], gf[0:ROWS, :], -1.0, gf[0:ROWS, :], ALU.mult, ALU.min).then_inc(f_abs, 1)
            dve.wait_ge(f_log, 2)
            S.then(dve.scalar_tensor_tensor(gf[0:ROWS, :], gf[0:ROWS, :], 0.0, gx[0:ROWS, :], ALU.min, ALU.subtract))

            def scan(dst, src, op, start):
                S.did(dve.tensor_tensor_scan(dst[0:MH, :], src[0:MH, :], src[0:MH, :], start, op, ALU.bypass))
                b = slice(32, 32 + MH)
                S.then(dve.tensor_tensor_scan(dst[b, CTX - 1::-1], src[b, CTX - 1::-1], src[b, CTX - 1::-1], start, op, ALU.bypass))
                S.then(dve.tensor_tensor_scan(dst[b, S2 - 1:CTX - 1:-1], src[b, S2 - 1:CTX - 1:-1], src[b, S2 - 1:CTX - 1:-1],
                                              dst[b, 0:1], op, ALU.bypass))

            dve.wait_ge(zeros_ready, 3)
            scan(cum, gf, ALU.add, 0.0)
            S.then(dve.tensor_tensor(rr[0:ROWS, :], gi[0:ROWS, :], cum[0:ROWS, :], ALU.subtract))
            scan(rmax, rr, ALU.max, TAKEN)
            dve.tensor_tensor(cum[0:ROWS, CTX:S2], cum[0:ROWS, CTX:S2], rmax[0:ROWS, CTX:S2], ALU.add).then_inc(scan_ready, 1)
            def weigh(h):
                dve.wait_ge(e_masked, 4 * h + 4)
                for d in range(2):
                    for n, job in enumerate((f"qk{h}a", f"qk{h}b")):
                        if d == 0:
                            sec.ready(dve, job)
                        part = E[:, h % 2, d, 2 * n:2 * n + 2, :]
                        ins = dve.scalar_tensor_tensor(part.rearrange("p c t -> p (c t)"), to(job)[:, :], DH ** -0.5,
                                                       part.rearrange("p c t -> p (c t)"), ALU.mult, ALU.mult)
                        if d == 1:
                            sec.moved(ins, job)
                        elif n == 1:
                            ins.then_inc(s_ready, 1)

            def combine(h):
                for d in range(2):
                    job = f"o{h}{d}"
                    sec.ready(dve, job)
                    o = to(job)[:, 0:2 * (DH + 1)].rearrange("p (t c) -> p t c", t=NT)
                    S.then(dve.tensor_tensor(nq, o[:, :, DH], emn[:, :, 32 * d + h], ALU.max))
                    S.then(dve.scalar_tensor_tensor(nq, o[:, :, DH], -1.0, nq, ALU.mult, ALU.max))
                    S.then(dve.reciprocal(rq2, nq))
                    for t in range(NT):
                        dst = h_rows[:, t, h * DH:(h + 1) * DH]
                        if d == 0:
                            ins = dve.tensor_scalar(dst, o[:, t, 0:DH], rq2[:, t:t + 1], None, ALU.mult)
                        else:
                            ins = dve.scalar_tensor_tensor(dst, o[:, t, 0:DH], rq2[:, t:t + 1], dst, ALU.mult, ALU.add)
                    sec.moved(ins, job)
                    sec.arrived(dve, job)

            sec.arrived(dve, "rT")
            weigh(0)
            for h in range(MH):
                if h + 1 < MH:
                    weigh(h + 1)
                combine(h)
            for n in range(8):
                t, h = n // MH, n % MH
                S.then(dve.bn_stats(bst[:, n, :], h_rows[:, t, h * DH:(h + 1) * DH]))
                ins = dve.bn_aggr(bag[:, n, :], bst[:, n, :])
            ins.then_inc(h_var, 1)
            dve.wait_ge(h_rstd, 1)
            for n in range(8):
                t, h = n // MH, n % MH
                part = h_rows[:, t, h * DH:(h + 1) * DH]
                ins = dve.tensor_scalar(part, part, bag[:, n, 0:1], rstd[:, n:n + 1], ALU.subtract, ALU.mult)
            ins.then_inc(hn_ready, 1)
            for h in range(MH):
                sec.arrived(dve, f"hT{h // 2}")
                S.then(dve.scalar_tensor_tensor(hm[:, h, :], actT[:, h, CTX:S2], prm2[:, C2_SKIP + h:C2_SKIP + h + 1], hm[:, h, :],
                                                ALU.mult, ALU.add))
                dve.tensor_tensor(yT[:, h, :], hm[:, h, :], szT[:, h, :], ALU.mult).then_inc(y_ready, 1)
                if h % 2:
                    for g in (h - 1, h):
                        dve.wait_ge(y_hi, g + 1)
                        dve.tensor_tensor(y_l[:, g, :], yT[:, g, :], f32(y_h[:, 4 + g, :]), ALU.subtract).then_inc(y_lo, 1)

            def gated_add(name, count, q, done):
                halves = [slice(c * 512, (c + 1) * 512) for c in range(2)]
                for t in range(NT):
                    dve.wait_ge(rstd_ready, 4 * DEPTH + count + t + 1)
                    for c in range(2):
                        n = 2 * t + c
                        sec.moved(dve.scalar_tensor_tensor(tmp[:, n, :], bank[n][:, :], rstd[:, t:t + 1], gb[:, q, halves[c]],
                                                           ALU.mult, ALU.mult), f"{name}{n}")
                    for c in range(2):
                        n = 2 * t + c
                        sec.arrived(dve, f"{name}{n}")
                        ins = dve.tensor_tensor(x[:, t, halves[c]], x[:, t, halves[c]], tmp[:, n, :], ALU.add)
                        if done is out_ready or c:
                            ins.then_inc(done, 1)

            def rest_of_piece(q, c, subs=range(4)):
                for j in subs:
                    at = slice(j * 1024, (j + 1) * 1024)
                    dve.wait_ge(hi_ready, 48 * q + 4 * c + j + 1)
                    dve.tensor_tensor(w_l[:, c % 4, at], m[:, c % 4, at], f32(w_h[:, c % 3, at]), ALU.subtract).then_inc(lo_ready, 1)

            gated_add("wo", 6, 0, x_ready)
            normed(8, x, xn2, 0)
            for t in range(NT):
                dve.wait_ge(xn_ready, 4 * DEPTH + 4 + t + 1)
                S.then(dve.tensor_copy(xn_h[:, t, :], xn2[:, t, :]))
                S.did(dve.tensor_tensor(xn_l[:, t, :], xn2[:, t, :], f32(xn_h[:, t, :]), ALU.subtract))
                if t == 0:
                    for n in (2, 3):
                        sec.ready(dve, f"t2{n}")
                        for f in (2 * n, 2 * n + 1):
                            ins = dve.tensor_scalar(h_rt[:, f, :], to(f"t2{n}")[:, f % 2 * T:(f % 2 + 1) * T],
                                                    modc[:, 3, f, 0:1], modc[:, 2, f, 0:1], ALU.mult, ALU.add)
                        sec.moved(ins, f"t2{n}")
            for i in range(QUAD):
                S.did(dve.tensor_copy(pick_w[:, i, 2:2 + P], ident))
            rest_of_piece(0, 0)
            dve.wait_ge(router_in, 32)
            for t in range(NT):
                sec.ready(dve, f"rt{t}")
                ins = dve.tensor_tensor(logit[:, t, :], to(f"rt{t}")[:, 0:NG + NE], b_rt, ALU.add)
                sec.moved(ins, f"rt{t}")
            for t in range(NT):
                sec.arrived(dve, f"rt{t}")

            def over(v, n):
                return v.unsqueeze(2).to_broadcast([P, NT, n])

            def first_max(dst, best, src, n):
                rank = const[:, K_RANK + NE - n:K_RANK + NE].unsqueeze(1).to_broadcast([P, NT, n])
                S.then(dve.tensor_reduce(best, src, AX.X, ALU.max))
                S.then(dve.tensor_tensor(dst, src, over(best, n), ALU.is_equal))
                S.then(dve.tensor_tensor(dst, dst, rank, ALU.mult))
                S.then(dve.tensor_reduce(t4, dst, AX.X, ALU.max))
                S.then(dve.tensor_tensor(dst, dst, over(t4, n), ALU.is_equal))

            first_max(gsel, t1, logit[:, :, 0:NG], NG)
            dve.tensor_tensor(gd, logit[:, :, 0:NG], over(t1, NG), ALU.subtract).then_inc(g_diff, 1)
            el = expert_l[:, :, 0:NE]
            by_group = "p t (g e) -> p t g e"
            for t in range(NT):
                S.then(dve.tensor_tensor(el[:, t].rearrange("p (g e) -> p g e", g=NG),
                                         logit[:, t, NG:].rearrange("p (g e) -> p g e", g=NG),
                                         gsel[:, t].unsqueeze(2).to_broadcast([P, NG, EPG]), ALU.mult))
            S.then(dve.tensor_scalar(gsel, gsel, 1.0, -NEG, ALU.subtract, ALU.mult))
            for t in range(NT):
                S.then(dve.tensor_tensor(el[:, t].rearrange("p (g e) -> p g e", g=NG), el[:, t].rearrange("p (g e) -> p g e", g=NG),
                                         gsel[:, t].unsqueeze(2).to_broadcast([P, NG, EPG]), ALU.add))
            p1, p2 = pick1[:, :, 0:NE], pick2[:, :, 0:NE]
            first_max(p1, t1, el, NE)
            S.then(dve.scalar_tensor_tensor(el, p1, 2 * NEG, el, ALU.mult, ALU.add))
            first_max(p2, t2, el, NE)
            dve.tensor_tensor(chosen, p1, p2, ALU.add).then_inc(chosen_ready, 1)
            dve.tensor_tensor(t3, t2, t1, ALU.subtract).then_inc(e_diff, 1)
            dve.wait_ge(g_exp, 1)
            dve.wait_ge(e_diff, 1)
            S.then(dve.tensor_reduce(t1, ge, AX.X, ALU.add))
            S.then(dve.reciprocal(t1, t1))
            dve.wait_ge(e_exp, 1)
            S.then(dve.tensor_scalar(t2, t3, 1.0, None, ALU.add))
            S.then(dve.reciprocal(t2, t2))
            S.then(dve.tensor_tensor(t1, t1, t2, ALU.mult))
            S.then(dve.tensor_tensor(t2, t3, t1, ALU.mult))
            dve.wait_ge(chosen_ready, 1)
            S.then(dve.tensor_tensor(p1, p1, over(t1, NE), ALU.mult))
            S.then(dve.tensor_tensor(p2, p2, over(t2, NE), ALU.mult))
            S.then(dve.tensor_tensor(comb[:, :, 0:NE], p1, p2, ALU.add))
            sec.ready(dve, "rank")
            S.then(dve.scalar_tensor_tensor(place[:, :, 0:NE], to("rank")[:, 0:2 * NE].rearrange("p (t e) -> p t e", t=NT), 1.0,
                                            chosen, ALU.add, ALU.mult))

            def split_weights(e):
                S.then(dve.tensor_copy(comb_h[:, :, e], comb[:, :, e]))
                S.then(dve.tensor_tensor(comb_l[:, :, e], comb[:, :, e], f32(comb_h[:, :, e]), ALU.subtract))

            def slots(e, side):
                for n in range(2):
                    for t in range(NT):
                        ins = dve.tensor_scalar(choice[:, side, t, n * P:(n + 1) * P], const[:, K_SLOT:K_SLOT + P],
                                                place[:, t, bass.ds(e + n, 1)], None, ALU.is_equal)
                return ins

            def weights(e, i):
                for n in range(2):
                    for t in range(NT):
                        for part, src in enumerate((f32(comb_h[:, :, :]), comb_l)):
                            at = P + 2 - t * (P + 2) + part
                            ins = dve.tensor_copy(pick_w[:, i + n, at:at + 1], src[:, t, bass.ds(e + n, 1)])
                return ins

            def choose(e, i, side):
                slots(e, side)
                weights(e, i).then_inc(choice_ready, 1)

            def slot_weights(name, at, i, n):
                sec.ready(dve, name, at)
                dve.tensor_reduce(slot_w[:, i:i + 1], to(name)[:, P:P + 4], AX.X, ALU.add).then_inc(slot_ready, 1)

            def rest_of_tokens(side, c, n):
                dve.wait_ge(xg_rounded, n + 1)
                at = slice(2 * c, 2 * c + 2)
                dve.tensor_tensor(xg[:, side, 1, at, :], xg_full[:, side, 1, at, :], f32(xg[:, side, 0, at, :]),
                                  ALU.subtract).then_inc(xg_ready, 1)

            def expert_pass(q, i, final=False):
                p, side = QUAD * q + i, i // 2
                more = not (final and i >= 2)
                rest_of_piece(q, 3 * i + 2)
                if i % 2 and not final:
                    choose(p + 3, (i + 3) % QUAD, side)
                ahead = not (final and i == QUAD - 1)

                def ahead_of(c, *subs):
                    if ahead:
                        rest_of_piece(q, 3 * i + c, subs)

                def tokens(c):
                    if more:
                        rest_of_tokens(1 - side, 2 * (i % 2) + c, 2 * p + 4 + c)

                ahead_of(3, 0)
                sec.arrived(dve, "eG", 2 * p)
                sec.ready(dve, "eU", 2 * p)
                sec.moved(dve.tensor_tensor(hidden, hidden, to("eU")[:, :], ALU.mult), "eU")
                ahead_of(3, 1, 2)
                dve.wait_ge(hidden_rounded, p + 1)
                sec.moved(dve.tensor_tensor(aT2[:, 1].rearrange("p j s -> p (j s)"), to("e6")[:, :],
                                            f32(aT2[:, 0].rearrange("p j s -> p (j s)")), ALU.subtract), "e6")
                ahead_of(3, 3)
                tokens(0)
                ahead_of(4, 0)
                tokens(1)
                dve.wait_ge(slot_ready, p + 1)
                ahead_of(4, 1)
                for c, name in enumerate(("eD0", "eD1")):
                    if c:
                        ahead_of(4, 2)
                        if more and i % 2:
                            for n, (bank_, at) in enumerate((("e6", 6 * q + CHOSEN_T6[i]), ("e7", 10 * q + CHOSEN_T7[i]))):
                                slot_weights(bank_, at, (i + 1 + n) % QUAD, p + 1 + n)
                        ahead_of(4, 3)
                    dve.wait_ge(y_rounded, 2 * p + c + 1)
                    at = slice(c * 512, (c + 1) * 512)
                    sec.moved(dve.scalar_tensor_tensor(y2[:, 1, at], to(name)[:, :], slot_w[:, i:i + 1], f32(y2[:, 0, at]),
                                                       ALU.mult, ALU.subtract), name)

            slots(0, 0).then_inc(choice_ready, 1)
            split_weights(slice(0, NE))
            weights(0, 0).then_inc(first_weights, 1)
            sec.moved(dve.tensor_scalar(over_e, to("rank")[:, 2 * NE:3 * NE], P + 0.5, None, ALU.is_gt), "rank")
            sec.arrived(dve, "rank")
            S.then(dve.tensor_tensor_scan(over_n, over_e, over_e, 0.0, ALU.add, ALU.bypass))

            def overflow(n):
                S.then(dve.scalar_tensor_tensor(over_1, over_n, n + 1.0, over_e, ALU.is_equal, ALU.mult))
                which = over_1.unsqueeze(1).to_broadcast([P, NT, NE])
                S.then(dve.scalar_tensor_tensor(over_t, place[:, :, 0:NE], -float(P), which, ALU.add, ALU.mult))
                S.then(dve.tensor_reduce(place[:, :, NE + n], over_t, AX.X, ALU.add))
                S.then(dve.tensor_tensor(over_t, comb[:, :, 0:NE], which, ALU.mult))
                S.then(dve.tensor_reduce(comb[:, :, NE + n], over_t, AX.X, ALU.add))
                S.then(dve.tensor_tensor(over_1, over_1, const[:, K_RANK:K_RANK + NE], ALU.mult))
                S.then(dve.tensor_reduce(table[:, n:n + 1], over_1, AX.X, ALU.add))

            for c in range(4):
                rest_of_tokens(0, c, c)
                if c < 2:
                    overflow(c)
            for n in range(2):
                slot_weights(f"first_sT{n}", 0, n, n)
            choose(2, 2, 1)
            for n in range(2, OVER):
                overflow(n)
            S.then(dve.tensor_scalar(table[:, 0:OVER], table[:, 0:OVER], 1.0, -1.0, ALU.max, ALU.mult))
            S.did(dve.tensor_scalar(table[:, 0:OVER], table[:, 0:OVER], float(NE), None, ALU.add))
            S.then(dve.tensor_copy(table[:, OVER:OVER + 1], over_n[:, NE - 1:NE]))
            dve.tensor_copy(table_i[:, :], table).then_inc(table_ready, 1)
            split_weights(slice(NE, NPASS))
            dve.wait_ge(lo_ready, 8)
            with dve.Fori(0, NE // QUAD) as q:
                for i in range(QUAD):
                    expert_pass(q, i)
            with dve.If(dve.value_load(table_i[0:1, OVER:OVER + 1], min_val=0, max_val=OVER) > 0):
                for i in range(QUAD):
                    expert_pass(NE // QUAD, i, final=True)
            gated_add("ye", 10, 1, out_ready)

        @block.gpsimd
        def _(pool):
            for n in range(8):
                pool.sem_inc(drained[n], 1)
            pool.sem_inc(block_used[1], 1)
            pool.wait_ge(half_ready, 1)
            pool.wait_ge(const_in, 16)

            def root(S, dst, src, n, scale, eps, ready):
                v = ms[:, dst:dst + n]
                settle(pool, passed)
                if scale is None:
                    S.then(pool.tensor_scalar(v, src, eps, None, ALU.add))
                else:
                    S.then(pool.tensor_scalar(v, src, scale, eps, ALU.mult, ALU.add))
                pool.tensor_tensor(rstd[:, dst:dst + n], v, half[:, 0:n], ALU.pow).then_inc(ready, 1)

            def row_roots(S, count, o=0):
                for t in range(NT):
                    pool.wait_ge(ss_ready, count + t + 1)
                    root(S, o + t, ss[:, o + t:o + t + 1], 1, 1.0 / D, EPS, rstd_ready)

            with pool.Fori(0, DEPTH) as l:
                res = layer_results(l)
                S = Steps(pool, pool_step, l * POOL_STEPS)

                def rest_of(hi, count, dst, src, high, subs, done):
                    for i, n in enumerate(subs):
                        at = slice(n * 1024, (n + 1) * 1024)
                        pool.wait_ge(hi, count + i + 1)
                        settle(pool, passed)
                        pool.tensor_tensor(dst[:, at], src[:, at], f32(high[:, at]), ALU.subtract).then_inc(done, 1)

                row_roots(S, 4 * l)
                rest_of(w1_hi, 12 * l, w_l[:, 2, :], m[:, 2, :], dadg_h, range(2), w1_pool)
                rest_of(w1_hi, 12 * l + 4, w_l[:, 0, :], m[:, 0, :], vqi_h, range(2), w1_pool)
                pool.wait_ge(rows_ws_in, 32 * l + 32)
                settle(pool, passed)
                pool.affine_select(out=wsT, in_=wsT, pattern=[[0, H], [1, P]], compare_op=ALU.is_ge, fill=0.0, base=0,
                                   channel_multiplier=-1).then_inc(ws_ready, 1)
                rest_of(w1_hi, 12 * l + 8, w_l[:, 1, :], m[:, 1, :], dadg_h, range(2), w1_pool)
                rest_of(in_hi, IN_SUBS * l, fw_l[:, 0, :], blocks_w[:, 0, :], fw_l[:, 1, :], range(4, 6), ab_lo)
                rest_of(in_hi, IN_SUBS * l + 2, fw_l[:, 0, :], blocks_w[:, 0, :], fw_l[:, 1, :], range(4), ab_lo)
                for t in range(NT):
                    res.arrived(pool, f"qk{t}")
                    z8 = zq[:, t, :].rearrange("p (h d) -> p h d", h=8)
                    hd = HD // 2
                    S.did(pool.tensor_tensor(ga, z8, cos2[:, t, :].unsqueeze(1).to_broadcast([P, 8, HD]), ALU.mult))
                    S.did(pool.tensor_tensor(gc[:, :, 0:hd], z8[:, :, hd:HD],
                                             sin2[:, t, 0:hd].unsqueeze(1).to_broadcast([P, 8, hd]), ALU.mult))
                    S.then(pool.tensor_tensor(gc[:, :, hd:HD], z8[:, :, 0:hd],
                                              sin2[:, t, hd:HD].unsqueeze(1).to_broadcast([P, 8, hd]), ALU.mult))
                    pool.tensor_tensor(rq[:, t], ga, gc, ALU.add).then_inc(rq_ready, 1)
                    pool.wait_ge(rq_ready, 2 * l + t + 1)
                for t in range(NT):
                    pool.wait_ge(score_ready, 2 * l + t + 1)
                    settle(pool, passed)
                    part = score[t][:, t * P:(t + 1) * P]
                    pool.affine_select(out=part, in_=part, pattern=[[-1, P]], compare_op=ALU.is_ge, fill=NEG, base=0,
                                       channel_multiplier=1).then_inc(score_masked, 1)
                rest_of(in_hi, IN_SUBS * l + 10, w_l[:, 0, :], m[:, 0, :], w_l[:, 2, :], range(2), out_lo)
                pool.wait_ge(var_ready, 2 * l + 1)
                root(S, 2, bnag[:, 0:2, 1], 2, None, LN_EPS, norm_rstd)

                rest_of(in_hi, IN_SUBS * l + 14, w_l[:, 1, :], m[:, 1, :], w_l[:, 3, :], (0,), out_lo)
                for t in range(NT):
                    pool.wait_ge(v_norm, 2 * l + t + 1)
                    v = zg[:, t, G:2 * G]
                    S.then(pool.tensor_tensor(v, v, lnrow[:, 0, :], ALU.mult))
                    pool.tensor_tensor(v, v, lnrow[:, 1, :], ALU.add).then_inc(v_ready, 1)
                for t in range(NT):
                    pool.wait_ge(sel_ready, 2 * l + t + 1)
                    settle(pool, passed)
                    part = sel[t][:, t * P:(t + 1) * P]
                    pool.affine_select(out=part, in_=part, pattern=[[-1, P]], compare_op=ALU.is_ge, fill=-1.0, base=0,
                                       channel_multiplier=1).then_inc(sel_masked, 1)
                pool.wait_ge(var_ready, 2 * l + 2)
                root(S, 4, bnag[:, 2:4, 1], 2, None, LN_EPS, norm_rstd)
                rest_of(in_hi, IN_SUBS * l + 15, w_l[:, 1, :], m[:, 1, :], w_l[:, 3, :], (1, 2, 3), out_lo)
                row_roots(S, 4 * l + 2)
                assert S.n == POOL_STEPS, S.n

            S = Steps(pool, pool_step, DEPTH * POOL_STEPS)
            N = 4 * DEPTH

            def rest_of_chunk(i, s):
                pool.wait_ge(ada_hi, 4 * (ADA * i + s) + 1)
                settle(pool, passed)
                pool.tensor_tensor(ada_l[s][:, 0:1024], ada_w[s][:, 0:1024], f32(ada_h[s % 2][:, 0:1024]), ALU.subtract)\
                    .then_inc(ada_first, 1)

            rest_of_chunk(0, 0)
            row_roots(S, N)
            for n in range(1, 2 * ADA):
                rest_of_chunk(n // ADA, n % ADA)
            row_roots(S, N + 2, 2)
            row_roots(S, N + 4)
            for j in range(2):
                at = slice(j * 1024, (j + 1) * 1024)
                pool.wait_ge(w2_hi, j + 1)
                pool.tensor_tensor(w_l[:, 0, at], m[:, 0, at], f32(xm_h[:, at]), ALU.subtract).then_inc(w2_first, 1)
            sec.ready(pool, "modT")
            S.then(pool.memset(xmp[:, :, :, 0:1], 0.0))
            pool.memset(xmp[:, :, :, CTX + 1:CTX + 2], 0.0).then_inc(zeros_ready, 1)
            sec.ready(pool, "xm3")
            S.then(pool.memset(cum[0:ROWS, :], 0.0))
            S.then(pool.memset(rmax[0:ROWS, :], 0.0))
            pool.memset(vtok[:, :, :, DH:DH + 1], 1.0).then_inc(zeros_ready, 1)
            S.then(pool.memset(nq, 0.0))
            pool.memset(rq2, 0.0).then_inc(zeros_ready, 1)
            sec.ready(pool, "u1")
            S.then(pool.memset(E[:, :, 0, 3, 0:P], 0.0))
            pool.memset(E[:, :, 1, 2, P:T], 0.0).then_inc(zeros_ready, 1)
            def rest_of_out(n):
                s, j = 1 - n // 4, n % 4
                high = w_l[:, 3, j * D:(j + 1) * D] if s else (wo_a, wo_b)[j // 2][:, j % 2, :]
                pool.wait_ge(wo_hi, n + 2)
                at = slice(j * D, (j + 1) * D)
                pool.tensor_tensor(w_l[:, s, at], m[:, s, at], f32(high), ALU.subtract).then_inc(wo_lo, 1)

            for h in range(MH):
                sec.arrived(pool, f"rb{h}")
                for d in range(2):
                    for c in (2, 3):
                        part = E[:, h % 2, d, c, (c - 2) * P:(c - 1) * P]
                        s = 1 if d == 0 else -1
                        pool.affine_select(out=part, in_=part, pattern=[[s, P]], compare_op=ALU.is_ge, fill=0.0, base=0,
                                           channel_multiplier=-s).then_inc(e_masked, 1)
                if h == 1:
                    pool.wait_ge(wo_hi, 1)
                    pool.tensor_tensor(y_l[:, 4:8, :], yT[:, 4:8, :], f32(fy_h[:, :, :]), ALU.subtract).then_inc(wo_lo, 1)
                for n in ((), (0, 1), (2,), (3, 4, 5, 6, 7))[h]:
                    rest_of_out(n)
            pool.wait_ge(h_var, 1)
            root(S, 0, bag[:, :, 1], 8, None, EPS, h_rstd)

            def result_root(count):
                for t in range(NT):
                    pool.wait_ge(ss_ready, N + count + 2 * t + 2)
                    S.then(pool.tensor_tensor(ms[:, 6 + t:7 + t], ss[:, 2 * t:2 * t + 1], ss[:, 2 * t + 1:2 * t + 2], ALU.add))
                    root(S, t, ms[:, 6 + t:7 + t], 1, 1.0 / D, EPS, rstd_ready)

            result_root(6)
            row_roots(S, N + 10)
            sec.ready(pool, "wo3")
            pool.tensor_scalar(y2[:, 0, :], half[:, 0:1].to_broadcast([P, D]), 0.0, None, ALU.mult).then_inc(y_zero, 1)
            pool.tensor_scalar(y2[:, 1, :], half[:, 0:1].to_broadcast([P, D]), 0.0, None, ALU.mult).then_inc(y_zero, 1)
            pool.tensor_scalar(choice_t[:, QUAD - 1, :], half[:, 0:1].to_broadcast([P, T]), 0.0, None, ALU.mult)\
                .then_inc(y_zero, 1)
            for j in range(4):
                at = slice(j * 1024, (j + 1) * 1024)
                pool.wait_ge(hi_ready, 4 + j + 1)
                pool.tensor_tensor(w_l[:, 1, at], m[:, 1, at], f32(w_h[:, 1, at]), ALU.subtract).then_inc(lo_ready, 1)
            result_root(12)


def constants():
    c = np.zeros((P, N_CONST), np.float64)
    c[:, K_ID:K_ID + P] = np.eye(P)
    angle = np.arange(T, dtype=np.float32)[:, None] * (np.float32(ROPE_THETA) ** (-np.arange(0, HD, 2, dtype=np.float32) / HD))
    angle = angle.astype(np.float32).astype(np.float64).reshape(NT, P, HD // 2).transpose(1, 0, 2)
    cos, sin = np.cos(angle), np.sin(angle)
    c[:, K_COS:K_COS + 2 * HD] = np.concatenate([cos, cos], -1).reshape(P, -1)
    c[:, K_SIN:K_SIN + 2 * HD] = np.concatenate([-sin, sin], -1).reshape(P, -1)
    w = 2 * np.pi * (np.outer(np.arange(P), np.arange(P)) % P) / P
    c[:, K_CC:K_CC + P] = np.cos(w) / P ** 0.5
    c[:, K_SC:K_SC + P] = -np.sin(w) / P ** 0.5
    w = 2 * np.pi * (np.outer(np.arange(T), np.arange(T)) % T) / T
    w = np.concatenate([np.cos(w), np.sin(w)], 1) / T ** 0.5
    c[:, K_DFT:K_RANK] = w.reshape(NT, P, 2 * T).transpose(1, 0, 2).reshape(P, -1)
    c[:, K_RANK:K_SLOT] = np.arange(NE, 0, -1)
    c[:, K_SLOT:K_BEFORE] = np.arange(1, P + 1)
    c[:, K_BEFORE:K_ONES] = np.triu(np.ones((P, P)), 1)
    c[:, K_ONES:] = 1
    quarter = D // 4
    freq = (1.0 / (np.float32(POS_BASE) ** (np.arange(quarter, dtype=np.float32) / np.float32(quarter)))).astype(np.float32)

    def table(n):
        v = (np.arange(n, dtype=np.float32)[:, None] * freq).astype(np.float64)
        return np.concatenate([np.sin(v), np.cos(v)], -1)

    rows = T // GRID_W
    pos = np.concatenate([np.repeat(table(rows), GRID_W, 0), np.tile(table(GRID_W), (rows, 1))], -1)
    return c.astype(np.float32), by_partition(pos.astype(np.float32))


def by_partition(w):
    *lead, k, n = w.shape
    w = w.reshape(*lead, k // P, P, n)
    return np.ascontiguousarray(np.moveaxis(w, -3, -2)).reshape(*lead, P, k // P * n)


def columns(*vectors):
    return np.concatenate([np.swapaxes(v.reshape(-1, P), 0, 1) for v in vectors], 1)


def layouts(i):
    cuts = np.cumsum([256] * 9 + [64, 4, 256, 256])[:-1]
    ab, ac, ah, gu, gv, q, k, v, qi, ki, wi, da, dg = np.split(i["w_in"], cuts, axis=2)
    groups = {"vqi": (v, qi), "kwi": (ki, wi), "dadg": (da, dg), "qk": (q, k), "guv": (gu, gv), "abac": (ab, ac), "ah": (ah,)}
    a = {}
    a["x"] = i["x"][0]
    a["w_in"] = np.concatenate([by_partition(np.concatenate(groups[n], 2)) for n in IN_COLS], 2)
    a["prm"] = np.stack([np.concatenate([
        columns(i["g_mix"][l], i["g_ffn"][l], i["w_conv_a"][l], i["w_conf"][l], i["b_conf"][l], i["conf_ln_g"][l],
                i["conf_ln_b"][l]), i["b_s"][l].T], 1) for l in range(DEPTH)])
    a["gmlp_ln"] = np.concatenate([i["gmlp_ln_g"], i["gmlp_ln_b"]], 1)
    a["w_s"] = i["w_s"].transpose(0, 3, 1, 2).reshape(DEPTH, P, H * P)
    a["w_out"] = by_partition(i["w_out"])

    def in_blocks(w, n):
        *lead, k, c = w.shape
        return by_partition(np.moveaxis(w.reshape(*lead, k, c // n, n), -2, -3))

    a["ffn"] = np.concatenate([in_blocks(i["w_gate"], FB), in_blocks(i["w_up"], FB),
                               by_partition(i["w_down"].reshape(DEPTH, NFB, FB, D))], 3)
    a["g_final"] = i["g_final"]
    pad = np.zeros((P, 2), np.float32)
    for d, name in enumerate(("b_if_fwd_2", "b_if_bwd_2")):
        for q in range(2):
            pad[32 * d:32 * d + MH, q] = i[name][0, q * MH:(q + 1) * MH]
    a["prm2"] = np.concatenate([columns(i["g_pre_mix_2"], i["g_pre_ffn_2"], i["conv_w_2"], i["conv_b_2"], i["mlstm_norm_w_2"],
                                        i["mlstm_skip_2"], i["c_2"], i["c_ctx_2"]), pad], 1)
    a["w_ada"] = in_blocks(i["w_ada_2"][0], 512).reshape(-1, ADA, P, 4096)
    a["b_ada"] = i["b_ada_2"][0]
    a["g_post"] = np.concatenate([i["g_post_mix_2"][0], i["g_post_ffn_2"][0]])
    a["ctx"] = i["ctx_2"][0]
    a["w_in_2"] = in_blocks(i["w_in_2"][0], 512)
    n = P // 4
    bd = np.zeros((3, MH, n, 4, n, 4), np.float32)
    for q, name in enumerate(("w_q_2", "w_k_2", "w_v_2")):
        for b in range(n):
            bd[q, :, b, :, b, :] = i[name][0].reshape(MH, n, 4, 4)[:, b]
    w_if = np.zeros((12, P, P), np.float32)
    for d, name in enumerate(("w_if_fwd_2", "w_if_bwd_2")):
        for q in range(2):
            w_if[:, :, 64 * q + 32 * d:64 * q + 32 * d + MH] = i[name][0].reshape(12, P, 2, MH)[:, :, q]
    a["heads_2"] = np.concatenate([bd.reshape(12, P, P), w_if, i["w_fourier_2"][0]]).transpose(1, 0, 2).reshape(P, -1)
    a["w_out_2"] = by_partition(i["w_out_2"][0])
    a["w_router"] = by_partition(np.concatenate([i["w_router_group_2"][0], i["w_router_expert_2"][0]], 1))
    a["b_router"] = np.concatenate([i["b_router_group_2"][0], i["b_router_expert_2"][0]])
    a["experts"] = np.concatenate([by_partition(i["w_gate_2"][0]), by_partition(i["w_up_2"][0]), by_partition(i["w_down_2"][0])], 2)
    a["const"], a["pos"] = constants()
    return {f"in_{k}": np.ascontiguousarray(v) for k, v in a.items()}


def kernel(**inputs):
    import concourse.bacc as bacc
    from concourse.bass_utils import run_bass_kernel_spmd

    arrays = layouts({k: np.asarray(v) for k, v in inputs.items()})
    nc = bacc.Bacc("TRN2", target_bir_lowering=False, num_devices=1)
    args = {n[3:]: nc.dram_tensor(n, v.shape, F32, kind="ExternalInput").ap() for n, v in arrays.items()}
    out = nc.dram_tensor("out", (T, D), F32, kind="ExternalOutput").ap()
    build(nc, args, out)
    return run_bass_kernel_spmd(nc, [arrays], core_ids=[0]).results[0]["out"].reshape(1, T, D)
```
